# Optimizing a Trainium2 kernel written in Bass

```python
import math
import jax, jax.numpy as jnp
from jax import lax
import numpy as np

D_MODEL = 1024
BATCH = 1
SEQ = 512
DEPTH = 2

MLA_HEADS = 8
MLA_NOPE_DIM = 128
MLA_ROPE_DIM = 64
MLA_V_DIM = 128
MLA_Q_RANK = 384
MLA_KV_RANK = 256
ROPE_THETA = 10000.0
SWA_Q_HEADS = 16
SWA_KV_HEADS = 4
SWA_HEAD_DIM = 64
WINDOW = 128
REL_BUCKETS = 32
REL_MAX_DIST = 128
D_FF = 4 * D_MODEL
BLOCK = 128
LN_EPS = 1e-5
RMS_EPS = 1e-6


def _layernorm(x, g, b):
    xf = x.astype(jnp.float32)
    mu = xf.mean(-1, keepdims=True)
    var = jnp.square(xf - mu).mean(-1, keepdims=True)
    return ((xf - mu) * lax.rsqrt(var + LN_EPS) * g + b).astype(x.dtype)

def _rmsnorm(x, g):
    xf = x.astype(jnp.float32)
    return (xf * lax.rsqrt(jnp.mean(xf * xf, -1, keepdims=True) + RMS_EPS) * g).astype(x.dtype)

def _rope(x, pos):
    half = x.shape[-1] // 2
    inv = ROPE_THETA ** (-jnp.arange(half, dtype=jnp.float32) / half)
    ang = pos.astype(jnp.float32)[:, None] * inv[None, :]
    ang = ang.reshape(ang.shape[:1] + (1,) * (x.ndim - 3) + ang.shape[1:])
    cos, sin = jnp.cos(ang), jnp.sin(ang)
    xf = x.astype(jnp.float32)
    x1, x2 = xf[..., :half], xf[..., half:]
    return jnp.concatenate([x1 * cos - x2 * sin, x1 * sin + x2 * cos], -1).astype(x.dtype)

def _t5_bucket(dist):
    n = jnp.maximum(dist, 0)
    max_exact = REL_BUCKETS // 2
    nf = jnp.maximum(n, 1).astype(jnp.float32)
    large = max_exact + (jnp.log(nf / max_exact) / math.log(REL_MAX_DIST / max_exact)
                         * (REL_BUCKETS - max_exact)).astype(jnp.int32)
    large = jnp.minimum(large, REL_BUCKETS - 1)
    return jnp.where(n < max_exact, n, large)

def _to_blocks(t, nb):
    return t.reshape((t.shape[0], nb, BLOCK) + t.shape[2:]).swapaxes(0, 1)

def _mla(x, w_in, g_q, g_kv, w_uq, w_uk, w_uv, w_o, pos):
    B, S, _ = x.shape
    nb = S // BLOCK
    h = x @ w_in
    c_q = _rmsnorm(h[..., :MLA_Q_RANK], g_q)
    c_kv = _rmsnorm(h[..., MLA_Q_RANK:MLA_Q_RANK + MLA_KV_RANK], g_kv)
    k_r = _rope(h[..., MLA_Q_RANK + MLA_KV_RANK:], pos)
    q = jnp.einsum('bsr,rhd->bshd', c_q, w_uq)
    q_n = q[..., :MLA_NOPE_DIM]
    q_r = _rope(q[..., MLA_NOPE_DIM:], pos)
    q_lat = jnp.einsum('bshn,chn->bshc', q_n, w_uk)
    scale = (MLA_NOPE_DIM + MLA_ROPE_DIM) ** -0.5
    kpos = jnp.arange(S)

    def block(args):
        ql, qr, i = args
        s = (jnp.einsum('bqhc,bkc->bhqk', ql, c_kv)
             + jnp.einsum('bqhr,bkr->bhqk', qr, k_r)).astype(jnp.float32) * scale
        qpos = i * BLOCK + jnp.arange(BLOCK)
        s = jnp.where(kpos[None, :] <= qpos[:, None], s, -jnp.inf)
        p = jax.nn.softmax(s, axis=-1).astype(x.dtype)
        return jnp.einsum('bhqk,bkc->bqhc', p, c_kv)

    o_lat = lax.map(block, (_to_blocks(q_lat, nb), _to_blocks(q_r, nb), jnp.arange(nb)))
    o_lat = o_lat.swapaxes(0, 1).reshape(B, S, MLA_HEADS, MLA_KV_RANK)
    o = jnp.einsum('bshc,chv->bshv', o_lat, w_uv).reshape(B, S, MLA_HEADS * MLA_V_DIM)
    return o @ w_o

def _shared_kv(x, w_kv):
    B, S, _ = x.shape
    nb = S // BLOCK
    kv = (x @ w_kv).reshape(B, nb, BLOCK, 2, SWA_KV_HEADS, SWA_HEAD_DIM)
    k, v = kv[:, :, :, 0], kv[:, :, :, 1]

    def band(t):
        prev = jnp.pad(t, ((0, 0), (1, 0), (0, 0), (0, 0), (0, 0)))[:, :-1]
        return jnp.concatenate([prev, t], axis=2)

    return band(k), band(v)

def _swa(x, w_q, sinks, w_o, k_band, v_band, rel_bias):
    B, S, _ = x.shape
    nb = S // BLOCK
    G = SWA_Q_HEADS // SWA_KV_HEADS
    q = (x @ w_q).reshape(B, nb, BLOCK, SWA_KV_HEADS, G, SWA_HEAD_DIM)
    s = jnp.einsum('bnqkgd,bnjkd->bnkgqj', q, k_band).astype(jnp.float32) * SWA_HEAD_DIM ** -0.5
    i = jnp.arange(BLOCK)
    j = jnp.arange(2 * BLOCK)
    dist = i[:, None] + BLOCK - j[None, :]
    bias = rel_bias[_t5_bucket(dist)].astype(jnp.float32)
    bias = bias.transpose(2, 0, 1).reshape(SWA_KV_HEADS, G, BLOCK, 2 * BLOCK)
    kpos = jnp.arange(nb)[:, None] * BLOCK - BLOCK + j[None, :]
    valid = (dist >= 0) & (dist < WINDOW)
    mask = valid[None] & (kpos >= 0)[:, None, :]
    s = jnp.where(mask[None, :, None, None], s + bias, -jnp.inf)
    sink = sinks.astype(jnp.float32).reshape(SWA_KV_HEADS, G)[..., None]
    m = jnp.maximum(s.max(-1), sink)
    p = jnp.exp(s - m[..., None])
    denom = p.sum(-1) + jnp.exp(sink - m)
    p = (p / denom[..., None]).astype(x.dtype)
    o = jnp.einsum('bnkgqj,bnjkd->bnqkgd', p, v_band).reshape(B, S, SWA_Q_HEADS * SWA_HEAD_DIM)
    return o @ w_o

def _mlp(x, w_up, w_down):
    h = jax.nn.relu(x @ w_up)
    return (h * h) @ w_down

def first_inputs(seed: int = 0) -> dict:
    key = jax.random.key(seed)
    ks = jax.random.split(key, 20)
    n_a = DEPTH // 2
    n_b = DEPTH - n_a
    beta = (8 * DEPTH) ** -0.25
    f32 = jnp.float32

    def nrm(k, shape, fan_in, gain=1.0):
        return jax.random.normal(k, shape, f32) * (gain * fan_in ** -0.5)

    in_w = MLA_Q_RANK + MLA_KV_RANK + MLA_ROPE_DIM
    kv_k = nrm(ks[8], (D_MODEL, 1, SWA_KV_HEADS * SWA_HEAD_DIM), D_MODEL)
    kv_v = nrm(ks[9], (D_MODEL, 1, SWA_KV_HEADS * SWA_HEAD_DIM), D_MODEL, beta)
    return {
        'x': jax.random.normal(ks[0], (BATCH, SEQ, D_MODEL), f32),
        'mla_w_in': nrm(ks[1], (n_a, D_MODEL, in_w), D_MODEL),
        'mla_g_q': 1.0 + 0.05 * jax.random.normal(ks[2], (n_a, MLA_Q_RANK), f32),
        'mla_g_kv': 1.0 + 0.05 * jax.random.normal(ks[3], (n_a, MLA_KV_RANK), f32),
        'mla_w_uq': nrm(ks[4], (n_a, MLA_Q_RANK, MLA_HEADS, MLA_NOPE_DIM + MLA_ROPE_DIM), MLA_Q_RANK),
        'mla_w_uk': nrm(ks[5], (n_a, MLA_KV_RANK, MLA_HEADS, MLA_NOPE_DIM), MLA_KV_RANK),
        'mla_w_uv': nrm(ks[6], (n_a, MLA_KV_RANK, MLA_HEADS, MLA_V_DIM), MLA_KV_RANK, beta),
        'mla_w_o': nrm(ks[7], (n_a, MLA_HEADS * MLA_V_DIM, D_MODEL), MLA_HEADS * MLA_V_DIM, beta),
        'kv_w_shared': jnp.concatenate([kv_k, kv_v], axis=1).reshape(D_MODEL, 2 * SWA_KV_HEADS * SWA_HEAD_DIM),
        'swa_w_q': nrm(ks[10], (n_b, D_MODEL, SWA_Q_HEADS * SWA_HEAD_DIM), D_MODEL),
        'swa_sinks': 0.5 * jax.random.normal(ks[11], (n_b, SWA_Q_HEADS), f32),
        'swa_w_o': nrm(ks[12], (n_b, SWA_Q_HEADS * SWA_HEAD_DIM, D_MODEL), SWA_Q_HEADS * SWA_HEAD_DIM, beta),
        'rel_bias': 0.5 * jax.random.normal(ks[13], (REL_BUCKETS, SWA_Q_HEADS), f32),
        'mlp_w_up': nrm(ks[14], (DEPTH, D_MODEL, D_FF), D_MODEL),
        'mlp_w_down': nrm(ks[15], (DEPTH, D_FF, D_MODEL), D_FF, beta),
        'ln_mix_g': 1.0 + 0.05 * jax.random.normal(ks[16], (DEPTH, D_MODEL), f32),
        'ln_mix_b': 0.02 * jax.random.normal(ks[17], (DEPTH, D_MODEL), f32),
        'ln_mlp_g': 1.0 + 0.05 * jax.random.normal(ks[18], (DEPTH, D_MODEL), f32),
        'ln_mlp_b': 0.02 * jax.random.normal(ks[19], (DEPTH, D_MODEL), f32),
    }

def first_block(x, mla_w_in, mla_g_q, mla_g_kv, mla_w_uq, mla_w_uk, mla_w_uv, mla_w_o,
              kv_w_shared, swa_w_q, swa_sinks, swa_w_o, rel_bias,
              mlp_w_up, mlp_w_down, ln_mix_g, ln_mix_b, ln_mlp_g, ln_mlp_b):
    alpha = (2 * DEPTH) ** 0.25
    n_a = DEPTH // 2
    pos = jnp.arange(x.shape[1])
    k_band = v_band = None
    for l in range(DEPTH):
        if l < n_a:
            y = _mla(x, mla_w_in[l], mla_g_q[l], mla_g_kv[l], mla_w_uq[l], mla_w_uk[l],
                     mla_w_uv[l], mla_w_o[l], pos)
        else:
            if l == n_a:
                k_band, v_band = _shared_kv(x, kv_w_shared)
            b = l - n_a
            y = _swa(x, swa_w_q[b], swa_sinks[b], swa_w_o[b], k_band, v_band, rel_bias)
        x = _layernorm(alpha * x + y, ln_mix_g[l], ln_mix_b[l])
        x = _layernorm(alpha * x + _mlp(x, mlp_w_up[l], mlp_w_down[l]), ln_mlp_g[l], ln_mlp_b[l])
    return x


DEPTH_2 = 1

CONV_W = D_MODEL // 2
N_HEADS = 8
HEAD_DIM = (D_MODEL - CONV_W) // N_HEADS
ATTN_W = N_HEADS * HEAD_DIM
IN_COLS = 3 * CONV_W + 3 * ATTN_W
CONV_K = 3
D_FF_2 = 2816
PLE_DIM = 256
DILATED_PAIRS = ((128, 1), (512, 4), (2048, 16))
EPS = 1e-6


def rmsnorm(a, g):
    af = a.astype(jnp.float32)
    af = af * lax.rsqrt(jnp.mean(af * af, axis=-1, keepdims=True) + EPS)
    return (af * g.astype(jnp.float32)).astype(a.dtype)

def causal_dwconv3(u, w, b):
    up = jnp.pad(u, ((0, 0), (CONV_K - 1, 0), (0, 0)))
    t = u.shape[1]
    return up[:, 0:t] * w[0] + up[:, 1:t + 1] * w[1] + up[:, 2:t + 2] * w[2] + b

def alibi_slopes(n):
    return jnp.exp2(-8.0 * jnp.arange(1, n + 1, dtype=jnp.float32) / n)

def dilated_branch(q, k, v, slopes, window, dilation):
    b, t, h, hd = q.shape
    steps = window // dilation
    L = t // dilation
    nb = -(-L // BLOCK)
    lp = nb * BLOCK

    def to_blocks(a):
        a = a.reshape(b, L, dilation, h, hd).transpose(0, 2, 3, 1, 4)
        a = jnp.pad(a, ((0, 0), (0, 0), (0, 0), (0, lp - L), (0, 0)))
        return a.reshape(b, dilation, h, nb, BLOCK, hd)

    def with_prev(a):
        prev = jnp.pad(a[:, :, :, :-1], ((0, 0), (0, 0), (0, 0), (1, 0), (0, 0), (0, 0)))
        return jnp.concatenate([prev, a], axis=4)

    qb = to_blocks(q)
    kk = with_prev(to_blocks(k))
    vv = with_prev(to_blocks(v))

    s = jnp.einsum('brhnqd,brhnkd->brhnqk', qb, kk) * (hd ** -0.5)
    qi = jnp.arange(BLOCK)[:, None] + BLOCK
    kj = jnp.arange(2 * BLOCK)[None, :]
    step = qi - kj
    band = (step >= 0) & (step <= steps)
    first = (jnp.arange(nb)[:, None, None] == 0) & (kj < BLOCK)[None]
    mask = band[None] & ~first
    dist = (step * dilation).astype(jnp.float32)
    bias = -slopes[:, None, None] * dist[None]
    s = jnp.where(mask, s + bias[:, None], -jnp.inf)
    m = jnp.max(s, axis=-1, keepdims=True)
    e = jnp.exp(s - m)
    den = jnp.sum(e, axis=-1, keepdims=True)
    o = jnp.einsum('brhnqk,brhnkd->brhnqd', e, vv) / den
    lse = (m + jnp.log(den))[..., 0]

    o = o.reshape(b, dilation, h, lp, hd)[:, :, :, :L]
    o = o.transpose(0, 3, 1, 2, 4).reshape(b, t, h, hd)
    lse = lse.reshape(b, dilation, h, lp)[:, :, :, :L]
    lse = lse.transpose(0, 3, 1, 2).reshape(b, t, h)
    return o, lse

def dilated_attention(q, k, v):
    slopes = alibi_slopes(q.shape[2])
    outs, lses = [], []
    for window, dilation in DILATED_PAIRS:
        o, lse = dilated_branch(q, k, v, slopes, window, dilation)
        outs.append(o)
        lses.append(lse)
    wts = jax.nn.softmax(jnp.stack(lses, axis=0), axis=0)
    o = jnp.sum(wts[..., None] * jnp.stack(outs, axis=0), axis=0)
    return o

def second_inputs(seed: int = 0) -> dict:
    key = jax.random.key(seed)
    ks = jax.random.split(key, 24)
    f32 = jnp.float32

    def nrm(k, shape, fan):
        return jax.random.normal(k, shape, f32) * (fan ** -0.5)

    def gain(k, shape):
        return 1.0 + 0.05 * jax.random.normal(k, shape, f32)

    def bias(k, shape):
        return 0.01 * jax.random.normal(k, shape, f32)

    return {
        'x': jax.random.normal(ks[0], (BATCH, SEQ, D_MODEL), f32),
        'p': jax.random.normal(ks[1], (DEPTH_2, BATCH, SEQ, PLE_DIM), f32),
        'g_mix': gain(ks[2], (DEPTH_2, D_MODEL)),
        'w_in': nrm(ks[3], (DEPTH_2, D_MODEL, IN_COLS), D_MODEL),
        'conv_w': nrm(ks[4], (DEPTH_2, CONV_K, CONV_W), CONV_K),
        'conv_b': bias(ks[5], (DEPTH_2, CONV_W)),
        'q_norm_g': gain(ks[6], (DEPTH_2, HEAD_DIM)),
        'k_norm_g': gain(ks[7], (DEPTH_2, HEAD_DIM)),
        'g_out_conv': gain(ks[8], (DEPTH_2, CONV_W)),
        'g_out_attn': gain(ks[9], (DEPTH_2, ATTN_W)),
        'w_out': nrm(ks[10], (DEPTH_2, CONV_W + ATTN_W, D_MODEL), CONV_W + ATTN_W),
        'g_ffn': gain(ks[11], (DEPTH_2, D_MODEL)),
        'w_gate': nrm(ks[12], (DEPTH_2, D_MODEL, D_FF_2), D_MODEL),
        'w_up': nrm(ks[13], (DEPTH_2, D_MODEL, D_FF_2), D_MODEL),
        'ffn_conv_w': nrm(ks[14], (DEPTH_2, CONV_K, D_FF_2), CONV_K),
        'ffn_conv_b': bias(ks[15], (DEPTH_2, D_FF_2)),
        'w_down': nrm(ks[16], (DEPTH_2, D_FF_2, D_MODEL), D_FF_2),
        'g_ple': gain(ks[17], (DEPTH_2, D_MODEL)),
        'w_ple_gate': nrm(ks[18], (DEPTH_2, D_MODEL, D_MODEL), D_MODEL),
        'w_ple_proj': nrm(ks[19], (DEPTH_2, PLE_DIM, D_MODEL), PLE_DIM),
    }

def second_block(x, p, g_mix, w_in, conv_w, conv_b, q_norm_g, k_norm_g, g_out_conv,
              g_out_attn, w_out, g_ffn, w_gate, w_up, ffn_conv_w, ffn_conv_b, w_down,
              g_ple, w_ple_gate, w_ple_proj):
    b, t, _ = x.shape
    for i in range(DEPTH_2):
        h = rmsnorm(x, g_mix[i])
        z = h @ w_in[i]
        zb, zc, zx, zq, zk, zv = jnp.split(
            z, np.cumsum([CONV_W, CONV_W, CONV_W, ATTN_W, ATTN_W]), axis=-1)
        y_c = zb * causal_dwconv3(zc * zx, conv_w[i], conv_b[i])
        q = rmsnorm(zq.reshape(b, t, N_HEADS, HEAD_DIM), q_norm_g[i]).astype(jnp.float32)
        k = rmsnorm(zk.reshape(b, t, N_HEADS, HEAD_DIM), k_norm_g[i]).astype(jnp.float32)
        v = zv.reshape(b, t, N_HEADS, HEAD_DIM).astype(jnp.float32)
        y_a = dilated_attention(q, k, v).reshape(b, t, ATTN_W).astype(x.dtype)
        y = jnp.concatenate([rmsnorm(y_c, g_out_conv[i]), rmsnorm(y_a, g_out_attn[i])], axis=-1)
        x = x + y @ w_out[i]
        h = rmsnorm(x, g_ffn[i])
        gate = causal_dwconv3(h @ w_gate[i], ffn_conv_w[i], ffn_conv_b[i])
        x = x + (jax.nn.silu(gate) * (h @ w_up[i])) @ w_down[i]
        ple_gate = jax.nn.sigmoid(rmsnorm(x, g_ple[i]) @ w_ple_gate[i])
        x = x + ple_gate * (p[i].astype(x.dtype) @ w_ple_proj[i])
    return x


def setup_inputs(seed=0):
    out = dict(first_inputs(seed))
    for name, value in second_inputs(seed + 1).items():
        if name != "x":
            out[name + "_2"] = value
    return out


def reference(
    x, mla_w_in, mla_g_q, mla_g_kv, mla_w_uq, mla_w_uk, mla_w_uv, mla_w_o, kv_w_shared, swa_w_q,
    swa_sinks, swa_w_o, rel_bias, mlp_w_up, mlp_w_down, ln_mix_g, ln_mix_b, ln_mlp_g, ln_mlp_b,
    p_2, g_mix_2, w_in_2, conv_w_2, conv_b_2, q_norm_g_2, k_norm_g_2, g_out_conv_2,
    g_out_attn_2, w_out_2, g_ffn_2, w_gate_2, w_up_2, ffn_conv_w_2, ffn_conv_b_2, w_down_2,
    g_ple_2, w_ple_gate_2, w_ple_proj_2,
):
    x = first_block(
        x, mla_w_in, mla_g_q, mla_g_kv, mla_w_uq, mla_w_uk, mla_w_uv, mla_w_o, kv_w_shared,
        swa_w_q, swa_sinks, swa_w_o, rel_bias, mlp_w_up, mlp_w_down, ln_mix_g, ln_mix_b,
        ln_mlp_g, ln_mlp_b,
    )
    return second_block(
        x, p_2, g_mix_2, w_in_2, conv_w_2, conv_b_2, q_norm_g_2, k_norm_g_2, g_out_conv_2,
        g_out_attn_2, w_out_2, g_ffn_2, w_gate_2, w_up_2, ffn_conv_w_2, ffn_conv_b_2, w_down_2,
        g_ple_2, w_ple_gate_2, w_ple_proj_2,
    )


_drawn_inputs = setup_inputs


def setup_inputs(seed=0):
    import zlib

    import numpy as np

    out = dict(_drawn_inputs(seed))
    spreads = {}
    factors = {'mla_g_q': 8.0,
     'mla_g_kv': 8.0,
     'swa_sinks': 8.0,
     'rel_bias': 3.158,
     'conv_b_2': 8.0,
     'q_norm_g_2': 4.221,
     'k_norm_g_2': 4.064,
     'ffn_conv_b_2': 8.0,
     'g_ple_2': 21.594}
    for name, (base, spread) in spreads.items():
        noise = np.random.default_rng([zlib.crc32(name.encode()), seed]).standard_normal(out[name].shape)
        drawn = base * np.exp(spread * noise) if base else spread * noise
        out[name] = __import__('jax').numpy.asarray(drawn.astype(out[name].dtype))
    for name, factor in factors.items():
        out[name] = (out[name] * factor).astype(out[name].dtype)
    return out
```

```python
from contextlib import ExitStack

import numpy as np

import concourse.bass as bass
from concourse import mybir

ALU = mybir.AluOpType
ACT = mybir.ActivationFunctionType
F32 = mybir.dt.float32
F32R = mybir.dt.float32r

P = 128
T = 512
D = 1024
KT = D // P
BANK = 512
SLAB = 2048
ALPHA = float((2 * 2) ** 0.25)
LN_EPS, RMS_EPS = 1e-5, 1e-6
Q_RANK, KV_RANK = 384, 256
MLA_SCALE = float((128 + 64) ** -0.5)
HEAD_SCALE = 64.0 ** -0.5
MASKED = -1e30
HUGE = 3e38

MLA_IN = 0
MLA_HALF = 3
MLA_OUT = 11
MLP0 = 15
SWA_HALF = 47
SWA_OUT = 55
MLP1 = 59
CONV = 91
DIL_HALF = 97
MIX_OUT = 105
FFN_A, FFN_A_DOWN = 109, 121
FFN_B, FFN_B_DOWN = 129, 139
PLE_PROJ = 147
PLE_GATE = 148
SLABS = 152
FF_A, FF_B = 12, 10

X_IN, MLA_O, LN_0, LN_1, SWA_O, LN_2, LN_3, MIX_Y, FFN_X, PLE_X = range(0, 80, 8)


def slab_width(g):
    if MLA_HALF <= g < MLA_OUT:
        return (3 * 384, 3 * 384, 2 * 512, 2 * 512)[(g - MLA_HALF) % 4]
    if SWA_HALF <= g < SWA_OUT:
        return (KT * P, KT * P, SLAB, SLAB)[(g - SWA_HALF) % 4]
    if DIL_HALF <= g < MIX_OUT:
        return (SLAB, SLAB, KT * P, KT * P)[(g - DIL_HALF) % 4]
    if FFN_A_DOWN <= g < FFN_B:
        return FF_A * P
    if FFN_B_DOWN <= g < PLE_PROJ:
        return FF_B * P
    return SLAB


VEC = {}
NVEC = 0
for _name, _n in (("g_q", 3), ("g_kv", 2), ("mix_g0", 8), ("mix_b0", 8), ("mlp_g0", 8), ("mlp_b0", 8),
                  ("mix_g1", 8), ("mix_b1", 8), ("mlp_g1", 8), ("mlp_b1", 8), ("g_mix", 8),
                  ("conv_w", 12), ("conv_b", 4), ("qn_g", 1), ("kn_g", 1), ("g_oc", 4), ("g_oa", 4),
                  ("g_ffn", 8), ("fconv_w", 66), ("fconv_b", 22), ("g_ple", 8), ("sink", 16),
                  ):
    VEC[_name] = NVEC
    NVEC += _n
LINE = 384


class Heads:

    def __init__(self, band):
        first = [max(0, i - 1) if band else 0 for i in range(4)]
        self.key0 = [f * P for f in first]
        self.tiles = [list(range(first[i], i + 1)) for i in range(4)]
        self.width = [len(t) * P for t in self.tiles]
        self.off = [sum(self.width[:i]) for i in range(4)]
        self.total = sum(self.width)
        if band:
            self.place = [(0, 0), (0, 128), (1, 0), (1, 256)]
            keys = [(0, 0), (0, 256), (1, 0), (1, 256)]
            self.segments = [512, 384]
        else:
            self.place = [(0, 0), (1, 0), (0, 128), (2, 0)]
            keys = [(0, 0), (1, 0), (2, 0), (1, 384)]
            self.segments = [512, 512, 256]
        reach = 2 if band else 4
        self.keys = [(min(4 - j, reach), *keys[j]) for j in range(4)]
        self.groups = [[0, 1], [2, 3]] if band else [[0, 2], [1], [3]]
        self.order = [i for group in self.groups for i in group]

    def blocks(self, n):
        return [(j + k, j, c + k * P) for j, (reach, bank, c) in enumerate(self.keys) if bank == n
                for k in range(reach)]


CAUSAL, BAND = Heads(False), Heads(True)


def program(nc, slabs, x_t, ple_t, vecs, rel_bias, onehot, line_mask, rope, mats, causal, dilated, out):
    ctx = ExitStack()
    with ctx:
        def sem(name):
            return ctx.enter_context(nc.semaphore(name))

        def keep(name, shape, dt=F32):
            return ctx.enter_context(nc.sbuf_tensor(name, shape, dt))

        stage = [keep(f"stage{s}", [P, SLAB]) for s in range(2)]
        w_hi = [keep(f"w_hi{s}", [P, SLAB], F32R) for s in range(2)]
        w_lo = [keep(f"w_lo{s}", [P, SLAB], F32R) for s in range(2)]
        act_hi = keep("act_hi", [P, KT, T], F32R)
        act_lo = keep("act_lo", [P, KT, T], F32R)
        y = keep("y", [P, KT, T])
        tmp = keep("tmp", [P, 2, 2, T])
        vec = keep("vec", [P, NVEC])
        mat = keep("mat", [P, 4, P])
        ident, ones, ones64, swap = (mat[:, i, :] for i in range(4))
        eps = keep("eps", [P, 2])
        sum1 = keep("sum1", [P, T])
        sum2 = keep("sum2", [P, T])
        rstd = keep("rstd", [P, T])
        stat = keep("stat", [P, T])
        rstd_tok = keep("rstd_tok", [P, 4])
        negmax = keep("negmax", [P, 4 * 16])
        rowsum = keep("rowsum", [P, 4 * 16])
        sinkexp = keep("sinkexp", [P, 4 * 16])
        rden = keep("rden", [P, 4 * 16])
        negsink = keep("negsink", [P, 16])
        ps = ctx.enter_context(nc.psum_tensor("ps", [P, 8, BANK], F32))

        floors = [0]

        def part(floor, *specs):
            made = []
            with ExitStack() as shared:
                if floor:
                    floors[0] += 1
                    shared.enter_context(nc.sbuf_tensor(f"floor{floors[0]}", [P, floor], F32))
                for name, shape, dt in specs:
                    made.append(shared.enter_context(nc.sbuf_tensor(name, shape, dt)))
                    floor += int(np.prod(shape[1:]))
            return (*made, floor)

        (qr_hi, qr_lo, kn_hi, kn_lo, kr_hi, kr_lo, mv_hi, mv_lo, c_hi, c_lo, cossin, strip, top) = part(
            0, ("qr_hi", [P, 2, T], F32R), ("qr_lo", [P, 2, T], F32R), ("kn_hi", [P, 4, T], F32R),
            ("kn_lo", [P, 4, T], F32R), ("kr_hi", [P, T], F32R), ("kr_lo", [P, T], F32R),
            ("mv_hi", [P, 4, T], F32R), ("mv_lo", [P, 4, T], F32R), ("c_hi", [P, 5, T], F32R),
            ("c_lo", [P, 5, T], F32R), ("cossin", [P, 2, T], F32), ("strip", [P, T], F32))
        c_raw, rope_raw, rope_cos, rope_sin, _ = part(
            top, ("c_raw", [P, 5, T], F32), ("rope_raw", [P, T], F32), ("rope_cos", [P, T], F32),
            ("rope_sin", [P, T], F32))
        m_prob, m_pt_hi, m_pt_lo, _ = part(
            top, ("m_prob", [P, 2, CAUSAL.total], F32), ("m_pt_hi", [P, CAUSAL.total], F32R),
            ("m_pt_lo", [P, CAUSAL.total], F32R))
        hid_hi, hid_lo, relu, top = part(
            0, ("hid_hi", [P, KT, T], F32R), ("hid_lo", [P, KT, T], F32R), ("relu", [P, 2, 2, T], F32))
        strips, top_strips = part(top, ("strips", [P, SLAB], F32))
        o_hi, o_lo, gap = part(0, ("o_hi", [P, KT, T], F32R), ("o_lo", [P, KT, T], F32R))
        swa_k_hi, swa_k_lo, _ = part(gap, ("swa_k_hi", [P, T], F32R), ("swa_k_lo", [P, T], F32R))
        dv_hi, dv_lo, top = part(gap, ("dv_hi", [P, 2, T], F32R), ("dv_lo", [P, 2, T], F32R))
        assert top <= top_strips - SLAB
        (sq_hi, sq_lo, va_hi, va_lo, vb_hi, vb_lo, s_prob, s_pt_hi, s_pt_lo, _) = part(
            top_strips, ("sq_hi", [P, 4, T], F32R), ("sq_lo", [P, 4, T], F32R), ("va_hi", [P, 4, P], F32R),
            ("va_lo", [P, 4, P], F32R), ("vb_hi", [P, 4, P], F32R), ("vb_lo", [P, 4, P], F32R),
            ("s_prob", [P, 2, BAND.total], F32), ("s_pt_hi", [P, BAND.total], F32R),
            ("s_pt_lo", [P, BAND.total], F32R))
        dq_hi, dq_lo, dk_hi, dk_lo, top = part(
            top_strips, ("dq_hi", [P, 2, T], F32R), ("dq_lo", [P, 2, T], F32R), ("dk_hi", [P, 2, T], F32R),
            ("dk_lo", [P, 2, T], F32R))
        zc, u_pad, conv, yc, _ = part(
            top, ("zc", [P, 2, T], F32), ("u_pad", [P, 2, T + 2], F32), ("conv", [P, 2, T], F32),
            ("yc", [P, 4, T], F32))
        d_prob, d_pt_hi, d_pt_lo, _ = part(
            top, ("d_prob", [P, 2, CAUSAL.total], F32), ("d_pt_hi", [P, CAUSAL.total], F32R),
            ("d_pt_lo", [P, CAUSAL.total], F32R))
        h_hi, h_lo, top = part(0, ("h_hi", [P, FF_A, T], F32R), ("h_lo", [P, FF_A, T], F32R))
        gate, gconv, silu, ffh, top = part(
            top, ("gate", [P, 2, T + 2], F32), ("gconv", [P, 2, T], F32), ("silu", [P, 2, T], F32),
            ("ffh", [P, 2, T], F32))
        p_raw, p_hi, p_lo, _ = part(top, ("p_raw", [P, 2, T], F32), ("p_hi", [P, 2, T], F32R),
                                    ("p_lo", [P, 2, T], F32R))
        proj, gate_in, _ = part(0, ("proj", [P, KT, T], F32), ("gate_in", [P, 2, 2, T], F32))
        bias_line = nc.dram_tensor("bias_line", (16, LINE), F32, kind="Internal").ap()
        bias_rows = nc.dram_tensor("bias_rows", (16, P, LINE), F32, kind="Internal").ap()

        landed = [sem(f"landed{s}") for s in range(2)]
        cast_hi, cast_lo = sem("cast_hi"), sem("cast_lo")
        slab_done = sem("slab_done")
        slab_read = sem("slab_read")
        act_ready = sem("act_ready")
        x_landed = [sem(f"x_landed{i}") for i in range(4)]
        x_hi, x_scaled = sem("x_hi"), sem("x_scaled")
        const_landed, p_landed = sem("const_landed"), sem("p_landed")
        eps_set = sem("eps_set")
        act_link, dve_link = sem("act_link"), sem("dve_link")
        sq_done = sem("sq_done")
        sum_ready, stat_done = sem("sum_ready"), sem("stat_done")
        rstd_ready, stat_act = sem("rstd_ready"), sem("stat_act")
        norm_z, norm_hi = sem("norm_z"), sem("norm_hi")
        c_read, c_full, c_split, c_ready = sem("c_read"), sem("c_full"), sem("c_split"), sem("c_ready")
        rope_in, rope_swapped, rope_out, rope_hi, rope_lo = (
            sem("rope_in"), sem("rope_swapped"), sem("rope_out"), sem("rope_hi"), sem("rope_lo"))
        proj_hi = sem("proj_hi")
        relu_done, sqr_done, hid_split = sem("relu_done"), sem("sqr_done"), sem("hid_split")
        line_done, line_ready, line_stored, rows_stored = (sem("line_done"), sem("line_ready"),
                                                           sem("line_stored"), sem("rows_stored"))
        strips_landed = sem("strips_landed")
        v_zeroed, u_zeroed = sem("v_zeroed"), sem("u_zeroed")
        qk_raw, qk_sq, qk_stat, qk_rstd, qk_full = (sem("qk_raw"), sem("qk_sq"), sem("qk_stat"), sem("qk_rstd"),
                                                    sem("qk_full"))
        mix_sq, mix_hi, dv_raw = sem("mix_sq"), sem("mix_hi"), sem("dv_raw")
        conv_done, silu_done, ffh_done, ffh_hi = sem("conv_done"), sem("silu_done"), sem("ffh_done"), sem("ffh_hi")
        ff_step, h_ready = sem("ff_step"), sem("h_ready")
        p_split, proj_act, sig_done, out_ready, stored = (sem("p_split"), sem("proj_act"), sem("sig_done"),
                                                          sem("out_ready"), sem("stored"))

        class Attention:

            def __init__(self, name, heads, score_banks, trans_bank, ahead):
                self.h, self.score_banks, self.trans_bank, self.ahead = heads, score_banks, trans_bank, ahead
                self.scored = sem(name + "_scored")
                self.biased = sem(name + "_biased")
                self.exped = sem(name + "_exped")
                self.summed = sem(name + "_summed")
                self.normed = sem(name + "_normed")
                self.turned = sem(name + "_turned")
                self.turn_hi = sem(name + "_turn_hi")
                self.turn_lo = sem(name + "_turn_lo")
                self.mixed = sem(name + "_mixed")
                self.out_hi = sem(name + "_out_hi")
                self.out_read = sem(name + "_out_read")
                self.nseg = len(heads.segments)

        mla = Attention("mla", CAUSAL, [0, 0], 3, 1)
        swa = Attention("swa", BAND, [0, 2], 4, 2)
        dil = Attention("dil", CAUSAL, [0, 0], 3, 1)

        def col(name, i=0):
            at = VEC[name] + i
            return vec[:, at:at + 1]

        def f32(ap):
            return ap.bitcast(F32)

        def pair(ap2d):
            return ap2d.unsqueeze(1).broadcast_to([P, 2, T])

        def banks(g):
            return 2 * (g % 2)

        block = ctx.enter_context(nc.Block())

        @block.sync
        def _(sp):
            for s in range(2):
                sp.dma_start(stage[s][:, :], slabs[s]).then_inc(landed[s], 16)
            with sp.Fori(1, SLABS // 2) as n:
                for s in range(2):
                    sp.wait_ge(cast_lo, n * 2 + (s - 1))
                    sp.dma_start(stage[s][:, :], slabs[bass.ds(n * 2 + s, 1)].rearrange("a p w -> p (a w)"))\
                      .then_inc(landed[s], 16)

        @block.gpsimd
        def _(pool):
            nc.gpsimd.memset(eps[:, 0:1], LN_EPS).then_inc(eps_set, 1)
            nc.gpsimd.memset(eps[:, 1:2], RMS_EPS).then_inc(eps_set, 1)
            for p in range(4):
                pool.wait_ge(act_ready, X_IN + 2 * p + 2)
                nc.gpsimd.tensor_scalar(y[:, 2 * p:2 * p + 2, :], y[:, 2 * p:2 * p + 2, :], ALPHA, None,
                                        ALU.mult).then_inc(x_scaled, 1)

            def divide(a, prob, u):
                h = a.h
                for k, i in enumerate(h.order):
                    pool.wait_ge(a.summed, 4 * u + k + 1)
                    n = 4 * (u % 16) + i
                    part = prob[:, u % 2, h.off[i]:h.off[i] + h.width[i]]
                    nc.gpsimd.tensor_scalar(part, part, rden[:, n:n + 1], None, ALU.mult).then_inc(a.normed, 1)

            def residual(gen, beta):
                for t in range(KT):
                    pool.wait_ge(act_ready, gen + t + 1)
                    nc.gpsimd.tensor_scalar(y[:, t, :], y[:, t, :], col(beta, t), ALPHA, ALU.add, ALU.mult)\
                        .then_inc(x_scaled, 1)

            for u in range(8):
                divide(mla, m_prob, u)
            residual(LN_0, "mix_b0")
            residual(LN_1, "mlp_b0")
            pool.wait_ge(act_ready, LN_1 + 1)
            for v in (va_hi, va_lo, vb_hi, vb_lo):
                nc.gpsimd.memset(v[:, :, :].bitcast(F32), 0.0).then_inc(v_zeroed, 1)
            for u in range(16):
                divide(swa, s_prob, u)
            residual(LN_2, "mix_b1")
            pool.wait_ge(act_ready, LN_3 + 1)
            nc.gpsimd.memset(u_pad[:, :, 0:2], 0.0).then_inc(u_zeroed, 1)
            for u in range(8):
                divide(dil, d_prob, u)
            pool.wait_ge(act_ready, FFN_X + 1)
            nc.gpsimd.memset(gate[:, :, 0:2], 0.0).then_inc(u_zeroed, 1)

        @block.scalar
        def _(act):
            links = [0]

            def link(ins):
                links[0] += 1
                ins.then_inc(act_link, 1)
                act.wait_ge(act_link, links[0])

            def cast(g, more=0, width=None):
                if g >= SLABS:
                    return
                s, w = g % 2, width or slab_width(g)
                act.wait_ge(landed[s], 16 * (g // 2 + 1) + more * 8)
                if g >= 2:
                    act.wait_ge(slab_done, g - 1 + more)
                nc.scalar.activation(w_hi[s][:, 0:w], stage[s][:, 0:w], ACT.Copy).then_inc(cast_hi, 1)

            def root(dst, src, scale, which):
                link(nc.scalar.activation(dst, src, ACT.Ln, scale=scale, bias=eps[:, which:which + 1]))
                return nc.scalar.activation(dst, dst, ACT.Exp, scale=-0.5)

            def exps(a, prob, u, sink=None):
                h = a.h
                for k, i in enumerate(h.order):
                    n = 4 * (u % 16) + i
                    act.wait_ge(a.biased, 4 * u + k + 1)
                    part = prob[:, u % 2, h.off[i]:h.off[i] + h.width[i]]
                    nc.scalar.activation(part, part, ACT.Exp, scale=-1.0, bias=negmax[:, n:n + 1],
                                         accum_out=rowsum[:, n:n + 1]).then_inc(a.exped, 1)
                if sink is not None:
                    n = 4 * (u % 16)
                    nc.scalar.activation(sinkexp[:, n:n + 4], negmax[:, n:n + 4], ACT.Exp, bias=sink)\
                        .then_inc(a.exped, 1)

            def turn_hi(a, pt_hi, u):
                for n, w in enumerate(a.h.segments):
                    act.wait_ge(a.turned, a.nseg * u + n + 1)
                    nc.scalar.activation(pt_hi[:, BANK * n:BANK * n + w], ps[:, a.trans_bank + n, 0:w],
                                         ACT.Copy).then_inc(a.turn_hi, 1)

            def squares(g, tiles, count):
                act.wait_ge(slab_read, g + 1)
                nc.scalar.activation(tmp[:, count % 2, 0:len(tiles), :], y[:, tiles[0]:tiles[-1] + 1, :],
                                     ACT.Square).then_inc(sq_done, 1)

            for p in range(4):
                act.dma_start(y[:, 2 * p:2 * p + 2, :], x_t[:, 2 * p:2 * p + 2, :]).then_inc(x_landed[p], 16)
            act.dma_start(vec[:, :], vecs).then_inc(const_landed, 16)
            act.dma_start(mat[:, :, :], mats).then_inc(const_landed, 16)
            act.dma_start(cossin[:, :, :], rope).then_inc(const_landed, 16)
            act.dma_start(strip[:, :], causal).then_inc(const_landed, 16)
            act.dma_start(stat[0:32, 0:16], rel_bias).then_inc(const_landed, 16)
            act.dma_start(sum2[0:32, 0:LINE], onehot).then_inc(const_landed, 16)
            act.dma_start(sum1[0:16, 0:LINE], line_mask).then_inc(const_landed, 16)
            for p in range(4):
                act.wait_ge(x_landed[p], 16)
                nc.scalar.activation(act_hi[:, 2 * p:2 * p + 2, :], y[:, 2 * p:2 * p + 2, :], ACT.Copy)\
                    .then_inc(x_hi, 1)
                if p < 2:
                    cast(p)
            act.wait_ge(line_ready, 1)
            act.dma_start(bias_line, rstd[0:16, 0:LINE]).then_inc(line_stored, 16)
            act.wait_ge(line_stored, 16)
            act.dma_start(bias_rows, bias_line.unsqueeze(1).broadcast_to([16, P, LINE])).then_inc(rows_stored, 16)

            act.wait_ge(const_landed, 16 * 7)
            act.wait_ge(eps_set, 2)
            for j in range(3):
                g = MLA_IN + j
                b = banks(g)
                act.wait_ge(slab_done, g + 1)
                if j < 2:
                    nc.scalar.activation(c_raw[:, 2 * j:2 * j + 2, :], ps[:, b:b + 2, :], ACT.Copy)
                    nc.scalar.activation(tmp[:, j, :, :], ps[:, b:b + 2, :], ACT.Square).then_inc(c_read, 1)
                else:
                    act.wait_ge(c_split, 1)
                    nc.scalar.activation(rope_raw[:, :], ps[:, b + 1, :], ACT.Copy).then_inc(rope_in, 1)
                    nc.scalar.activation(c_raw[:, 4, :], ps[:, b, :], ACT.Copy)
                    nc.scalar.activation(tmp[:, 0, 0, :], ps[:, b, :], ACT.Square).then_inc(c_read, 1)
                cast(g + 2)
            for n, (dst, scale, src) in enumerate(((rstd, D / Q_RANK, 4), (stat, D / KV_RANK, 5))):
                act.wait_ge(stat_done, n + 1)
                root(dst[:, :], ps[:, src, :], float(scale), 1).then_inc(rstd_ready, 1)
            for t in range(5):
                act.wait_ge(c_full, t + 1)
                nc.scalar.activation(c_hi[:, t, :], c_raw[:, t, :], ACT.Copy).then_inc(c_split, 1)
            act.wait_ge(rope_out, 1)
            nc.scalar.activation(kr_hi[:, :], rope_cos[:, :], ACT.Copy).then_inc(rope_hi, 1)

            for half in range(2):
                g = MLA_HALF + 4 * half
                for p in range(2):
                    b = 4 * p
                    act.wait_ge(slab_done, g + p + 1)
                    n = 1 + 2 * half + p
                    act.wait_ge(rope_out, n)
                    nc.scalar.activation(rope_raw[:, :], ps[:, b + 2, :], ACT.Copy, scale=MLA_SCALE)\
                        .then_inc(rope_in, 1)
                    nc.scalar.activation(act_hi[:, 4 + 2 * p:6 + 2 * p, :], ps[:, b:b + 2, :], ACT.Copy,
                                         scale=MLA_SCALE).then_inc(proj_hi, 1)
                    cast(g + p + 2)
                    act.wait_ge(rope_out, n + 1)
                    nc.scalar.activation(qr_hi[:, p, :], rope_cos[:, :], ACT.Copy).then_inc(rope_hi, 1)
                for p, dst in ((2, kn_hi), (3, mv_hi)):
                    b = 4 * (p - 2)
                    act.wait_ge(slab_done, g + p + 1)
                    for q in range(2):
                        nc.scalar.activation(dst[:, 2 * q:2 * q + 2, :], ps[:, b + 2 * q:b + 2 * q + 2, :],
                                             ACT.Copy).then_inc(proj_hi, 1)
                    cast(g + p + 2)
                exps(mla, m_prob, 4 * half)
                for u in range(4 * half, 4 * half + 4):
                    turn_hi(mla, m_pt_hi, u)
                    if u < 4 * half + 3:
                        exps(mla, m_prob, u + 1)
                    act.wait_ge(mla.mixed, u + 1)
                    nc.scalar.activation(act_hi[:, u, :], ps[:, 6 + u % 2, :], ACT.Copy).then_inc(mla.out_hi, 1)

            def load_bias(half):
                act.dma_start(strips[:, :].rearrange("p (h j) -> p h j", h=8),
                              bass.AP(bias_rows.tensor, 8 * half * P * LINE + P - 1,
                                      [[LINE - 1, P], [P * LINE, 8], [1, 2 * P]])).then_inc(strips_landed, 16)

            def plain_out(first, start):
                for j in range(4):
                    squares(first + j, [2 * j, 2 * j + 1], start + j)
                    cast(first + j + 2)

            def mean_square(n):
                act.wait_ge(stat_done, 2 + 2 * n + 1)
                nc.scalar.activation(sum1[:, :], ps[:, 4, :], ACT.Copy).then_inc(stat_act, 1)
                act.wait_ge(stat_act, 2 * n + 1)
                nc.scalar.activation(stat[:, :], sum1[:, :], ACT.Square).then_inc(stat_act, 1)

            def layer_norm(n, gen, beta):
                mean_square(n)
                act.wait_ge(sum_ready, 2 + 3 * n + 3)
                root(rstd[:, :], stat[:, :], 1.0, 0).then_inc(rstd_ready, 1)
                for t in range(KT):
                    act.wait_ge(norm_z, 8 * n + t + 1)
                    nc.scalar.activation(act_hi[:, t, :], y[:, t, :], ACT.Identity, bias=col(beta, t))\
                        .then_inc(norm_hi, 1)

            def mlp(first, layer, sq):
                def up(j, more, done):
                    g = first + j
                    b = banks(g)
                    act.wait_ge(slab_done, g + 1 + more)
                    act.wait_ge(slab_read, g - 1 + more)
                    nc.scalar.activation(relu[:, j % 2, :, :], ps[:, b:b + 2, :], ACT.Relu).then_inc(relu_done, 1)
                    act.wait_ge(sqr_done, done + j + 1)
                    nc.scalar.activation(hid_hi[:, 2 * j:2 * j + 2, :], relu[:, j % 2, :, :], ACT.Copy)\
                        .then_inc(hid_split, 1)
                    cast(g + 2, more)

                with act.Fori(0, 3) as r:
                    for j in range(4):
                        up(j, r * 8, r * 4 + 16 * layer)
                    for j in range(4, 8):
                        cast(first + j + 2, r * 8)
                for j in range(4):
                    up(j, 24, 12 + 16 * layer)
                for j in range(4):
                    squares(first + 28 + j, [2 * j, 2 * j + 1], sq + j)
                    cast(first + 28 + j + 2)

            plain_out(MLA_OUT, 0)
            layer_norm(0, LN_0, "mix_b0")
            act.wait_ge(rows_stored, 16)
            load_bias(0)
            mlp(MLP0, 0, 4)
            layer_norm(1, LN_1, "mlp_b0")

            for half in range(2):
                g = SWA_HALF + 4 * half
                if half:
                    act.wait_ge(swa.biased, 32)
                    load_bias(1)
                act.wait_ge(slab_done, g + 1)
                nc.scalar.activation(swa_k_hi[:, :], ps[:, banks(g), :], ACT.Copy).then_inc(proj_hi, 1)
                cast(g + 2)
                act.wait_ge(slab_done, g + 2)
                act.wait_ge(v_zeroed, 4)
                for v_hi, c in ((va_hi, 0), (vb_hi, 64)):
                    nc.scalar.activation(v_hi[:, :, c:c + 64],
                                         ps[:, banks(g + 1), :].rearrange("p (i c) -> p i c", i=4)[:, :, c:c + 64],
                                         ACT.Copy).then_inc(proj_hi, 1)
                cast(g + 3)
                for p in range(2):
                    b = banks(g + 2 + p)
                    act.wait_ge(slab_done, g + 3 + p)
                    nc.scalar.activation(sq_hi[:, 2 * p:2 * p + 2, :], ps[:, b:b + 2, :], ACT.Copy,
                                         scale=HEAD_SCALE).then_inc(proj_hi, 1)
                    cast(g + 4 + p)
                u0 = 8 * half
                for u in (u0, u0 + 1):
                    exps(swa, s_prob, u, col("sink", u))
                for u in range(u0, u0 + 8):
                    turn_hi(swa, s_pt_hi, u)
                    if u + 2 < u0 + 8:
                        exps(swa, s_prob, u + 2, col("sink", u + 2))
                    if u % 2:
                        act.wait_ge(swa.mixed, u // 2 + 1)
                        nc.scalar.activation(o_hi[:, u // 2, :], ps[:, 6 + (u // 2) % 2, :], ACT.Copy)\
                            .then_inc(swa.out_hi, 1)

            act.wait_ge(swa.biased, 64)
            act.dma_start(strips[:, :], dilated[0]).then_inc(strips_landed, 16)
            plain_out(SWA_OUT, 8)
            layer_norm(2, LN_2, "mix_b1")
            mlp(MLP1, 1, 12)

            mean_square(3)
            act.wait_ge(sum_ready, 2 + 3 * 3 + 3)
            root(rstd[:, :], stat[:, :], 1.0, 0).then_inc(rstd_ready, 1)
            for t in range(KT):
                act.wait_ge(norm_z, 24 + t + 1)
                link(nc.scalar.activation(y[:, t, :], y[:, t, :], ACT.Identity, bias=col("mlp_b1", t)))
                nc.scalar.activation(act_hi[:, t, :], y[:, t, :], ACT.Copy, scale=col("g_mix", t))\
                    .then_inc(norm_hi, 1)
                if t >= 2:
                    act.wait_ge(mix_sq, t - 1)
                nc.scalar.activation(tmp[:, t % 2, 0, :], y[:, t, :], ACT.Square).then_inc(sq_done, 1)

            act.wait_ge(stat_done, 11)
            root(rstd[:, :], ps[:, 4, :], 1.0, 1).then_inc(rstd_ready, 1)
            act.wait_ge(stat_done, 12)
            root(rstd_tok[:, :], ps[:, 5, 0:4], 1.0, 1).then_inc(rstd_ready, 1)
            for i in range(2):
                for j in range(3):
                    cast(CONV + 3 * i + j + 2)
                act.wait_ge(conv_done, i + 1)
                nc.scalar.activation(tmp[:, 1, :, :], yc[:, 2 * i:2 * i + 2, :], ACT.Square).then_inc(sq_done, 1)
            act.wait_ge(stat_done, 13)
            root(stat[:, :], ps[:, 6, :], 2.0, 1).then_inc(rstd_ready, 1)
            for t in range(4):
                act.wait_ge(conv_done, 2 + t + 1)
                nc.scalar.activation(o_hi[:, t, :], yc[:, t, :], ACT.Copy).then_inc(mix_hi, 1)

            for half in range(2):
                g = DIL_HALF + 4 * half
                if half:
                    act.wait_ge(dil.biased, 16)
                    act.dma_start(strips[:, :], dilated[1]).then_inc(strips_landed, 16)
                for p, (dst, scale, b) in enumerate(((dq_hi, HEAD_SCALE, 4), (dk_hi, 1.0, 6))):
                    n = 2 * half + p
                    act.wait_ge(qk_raw, n + 1)
                    nc.scalar.activation(tmp[:, 1, :, :], tmp[:, 0, :, :], ACT.Square).then_inc(qk_sq, 1)
                    cast(g + p + 2)
                    act.wait_ge(qk_stat, n + 1)
                    root(tmp[:, 1, :, :], ps[:, b:b + 2, :], 1.0, 1).then_inc(qk_rstd, 1)
                    act.wait_ge(qk_full, n + 1)
                    nc.scalar.activation(dst[:, :, :], tmp[:, 0, :, :], ACT.Copy, scale=scale)\
                        .then_inc(proj_hi, 1)
                for p in range(2):
                    act.wait_ge(dv_raw, 2 * half + p + 1)
                    nc.scalar.activation(dv_hi[:, p, :], tmp[:, 0, p, :], ACT.Copy).then_inc(proj_hi, 1)
                    cast(g + p + 4)
                u0 = 4 * half
                exps(dil, d_prob, u0)
                for u in range(u0, u0 + 4):
                    turn_hi(dil, d_pt_hi, u)
                    if u + 1 < u0 + 4:
                        exps(dil, d_prob, u + 1)
                    r, t = 64 * (u % 2), u // 2
                    act.wait_ge(dil.mixed, u + 1)
                    nc.scalar.activation(o_hi[r:r + 64, 4 + t, :], ps[r:r + 64, 6 + u % 2, :], ACT.Copy,
                                         scale=vec[r:r + 64, VEC["g_oa"] + t:VEC["g_oa"] + t + 1])\
                        .then_inc(dil.out_hi, 1)
                    if t >= 1:
                        act.wait_ge(mix_sq, 8 + t)
                    nc.scalar.activation(stat[r:r + 64, :], ps[r:r + 64, 6 + u % 2, :], ACT.Square)\
                        .then_inc(sq_done, 1)

            def rms_out(g, tiles, n, gain):
                act.wait_ge(slab_read, g + 1)
                for t in tiles:
                    nc.scalar.activation(act_hi[:, t, :], y[:, t, :], ACT.Copy, scale=col(gain, t))\
                        .then_inc(mix_hi, 1)
                nc.scalar.activation(tmp[:, n % 2, 0:len(tiles), :], y[:, tiles[0]:tiles[-1] + 1, :],
                                     ACT.Square).then_inc(sq_done, 1)

            act.wait_ge(stat_done, 14)
            root(stat[:, :], ps[:, 0, :], 2.0, 1).then_inc(rstd_ready, 1)
            for j in range(4):
                rms_out(MIX_OUT + j, [2 * j, 2 * j + 1], j, "g_ffn")
                cast(MIX_OUT + j + 2)

            act.wait_ge(stat_done, 15)
            root(rstd[:, :], ps[:, 7, :], 1.0, 1).then_inc(rstd_ready, 1)
            for rnd, (first, down, before, count) in enumerate(((FFN_A, FFN_A_DOWN, 0, FF_A),
                                                                (FFN_B, FFN_B_DOWN, FF_A, FF_B))):
                with act.Fori(0, count // 2) as i:
                    for b in range(2):
                        act.wait_ge(conv_done, 6 + before + b + 1 + i * 2)
                        nc.scalar.activation(silu[:, b, :], gconv[:, b, :], ACT.Silu).then_inc(silu_done, 1)
                        cast(first + b + 2, i * 2, SLAB)
                        act.wait_ge(ffh_done, before + b + 1 + i * 2)
                        nc.scalar.activation(h_hi[:, bass.ds(i * 2 + b, 1), :], ffh[:, b:b + 1, :], ACT.Copy)\
                            .then_inc(ffh_hi, 1)
                if rnd == 0:
                    for j in range(8):
                        cast(down + j + 2)
            for j in range(8):
                rms_out(FFN_B_DOWN + j, [j], j, "g_ple")
                cast(FFN_B_DOWN + j + 2)

            act.dma_start(p_raw[:, :, :], ple_t).then_inc(p_landed, 16)
            act.wait_ge(p_landed, 16)
            nc.scalar.activation(p_hi[:, :, :], p_raw[:, :, :], ACT.Copy).then_inc(p_split, 1)
            act.wait_ge(slab_done, PLE_PROJ + 1)
            for q in range(2):
                last = nc.scalar.activation(proj[:, 2 * q:2 * q + 2, :], ps[:, 2 * q:2 * q + 2, :], ACT.Copy)
            last.then_inc(proj_act, 1)
            cast(PLE_PROJ + 2)
            act.wait_ge(stat_done, 16)
            root(rstd[:, :], ps[:, 7, :], 1.0, 1).then_inc(rstd_ready, 1)
            for j in range(4):
                act.wait_ge(slab_read, PLE_GATE + j + 1)
                nc.scalar.activation(gate_in[:, j % 2, :, :], gate_in[:, j % 2, :, :], ACT.Sigmoid)\
                    .then_inc(sig_done, 1)
                cast(PLE_GATE + j + 2)
                act.wait_ge(out_ready, j + 1)
                act.dma_start(out[:, 2 * j:2 * j + 2, :], y[:, 2 * j:2 * j + 2, :]).then_inc(stored, 16)
            act.wait_ge(stored, 16 * 4)
            act.wait_ge(rows_stored, 16)


        @block.vector
        def _(dve):
            links = [0]

            def link(ins):
                links[0] += 1
                ins.then_inc(dve_link, 1)
                dve.wait_ge(dve_link, links[0])

            def split(dst, src, hi):
                return nc.vector.tensor_tensor(dst, src, f32(hi), ALU.subtract)

            def split_scaled(dst, src, scale, hi, op=ALU.mult):
                return nc.vector.scalar_tensor_tensor(dst, src, scale, f32(hi), op, ALU.subtract)

            def cast(g, more=0, width=None):
                if g >= SLABS:
                    return
                s, w = g % 2, width or slab_width(g)
                dve.wait_ge(cast_hi, g + 1 + more)
                split(w_lo[s][:, 0:w], stage[s][:, 0:w], w_hi[s][:, 0:w]).then_inc(cast_lo, 1)

            def bias(a, prob, u, table, floor=None, banks_per=None):
                h, at = a.h, a.score_banks[u % 2]
                if u >= 2:
                    dve.wait_ge(a.turned, a.nseg * (u - 1))
                k = 0
                for m, group in enumerate(h.groups):
                    dve.wait_ge(a.scored, len(h.groups) * u + m + 1)
                    for i in group:
                        bank, c = h.place[i]
                        w, n = h.width[i], 4 * (u % 16) + i
                        nc.vector.tensor_tensor_reduce(
                            prob[:, u % 2, h.off[i]:h.off[i] + w], ps[:, at + bank, c:c + w], table(w),
                            -1.0, HUGE if floor is None else floor, ALU.add, ALU.min,
                            negmax[:, n:n + 1]).then_inc(a.biased, 1)
                        k += 1

            def invert(a, u, sink=False):
                n = 4 * (u % 16)
                if sink:
                    dve.wait_ge(a.exped, 5 * u + 5)
                    link(nc.vector.tensor_tensor(rowsum[:, n:n + 4], rowsum[:, n:n + 4], sinkexp[:, n:n + 4],
                                                 ALU.add))
                    nc.vector.reciprocal(rden[:, n:n + 4], rowsum[:, n:n + 4]).then_inc(a.summed, 4)
                    return
                for k, i in enumerate(a.h.order):
                    dve.wait_ge(a.exped, 4 * u + k + 1)
                    nc.vector.reciprocal(rden[:, n + i:n + i + 1], rowsum[:, n + i:n + i + 1])\
                        .then_inc(a.summed, 1)

            def turn_lo(a, pt_hi, pt_lo, u):
                for n, w in enumerate(a.h.segments):
                    dve.wait_ge(a.turn_hi, a.nseg * u + n + 1)
                    split(pt_lo[:, BANK * n:BANK * n + w], ps[:, a.trans_bank + n, 0:w],
                          pt_hi[:, BANK * n:BANK * n + w]).then_inc(a.turn_lo, 1)

            def sums(tiles, n, first, last, with_mean):
                for dst, parts, wait in ((sum1, [y[:, t, :] for t in tiles], False),
                                         (sum2, [tmp[:, n % 2, k, :] for k in range(len(tiles))], True)):
                    if dst is sum1 and not with_mean:
                        continue
                    if wait:
                        dve.wait_ge(sq_done, n + 1)
                    if first and len(parts) == 2:
                        ins = nc.vector.tensor_tensor(dst[:, :], parts[0], parts[1], ALU.add)
                        parts = []
                    elif first:
                        ins = nc.vector.tensor_copy(dst[:, :], parts[0])
                        parts = []
                    for k, part in enumerate(parts):
                        ins = nc.vector.tensor_tensor(dst[:, :], dst[:, :], part, ALU.add)
                        if k < len(parts) - 1:
                            link(ins)
                    if last:
                        ins.then_inc(sum_ready, 1)
                    else:
                        link(ins)

            def add_out(g, t, more=0):
                b = banks(g)
                dve.wait_ge(slab_done, g + 1 + more)
                nc.vector.tensor_tensor(y[:, t:t + 2, :], y[:, t:t + 2, :], ps[:, b:b + 2, :], ALU.add)\
                    .then_inc(slab_read, 1)

            def last_out(first, sq):
                for j in range(4):
                    add_out(first + j, 2 * j)
                    cast(first + j + 2)
                    dve.wait_ge(slab_read, first + j + 1)
                    sums([2 * j, 2 * j + 1], sq + j, j == 0, j == 3, True)

            def layer_norm(n, gen, gain, beta, last=False):
                def centre(p):
                    return nc.vector.tensor_tensor(y[:, 2 * p:2 * p + 2, :], y[:, 2 * p:2 * p + 2, :],
                                                   pair(sum1[:, :]), ALU.subtract)

                def lo(t):
                    dve.wait_ge(norm_hi, 8 * n + t + 1)
                    if last:
                        split_scaled(act_lo[:, t, :], y[:, t, :], col("g_mix", t), act_hi[:, t, :])\
                            .then_inc(act_ready, 1)
                        dve.wait_ge(sq_done, 16 + t + 1)
                        if t == 0:
                            ins = nc.vector.tensor_copy(sum2[:, :], tmp[:, 0, 0, :])
                        else:
                            ins = nc.vector.tensor_tensor(sum2[:, :], sum2[:, :], tmp[:, t % 2, 0, :], ALU.add)
                        ins.then_inc(mix_sq, 1)
                        if t == KT - 1:
                            dve.wait_ge(mix_sq, KT)
                            nc.vector.tensor_copy(sum1[:, 0:1], sum2[:, 0:1]).then_inc(sum_ready, 1)
                        else:
                            dve.wait_ge(mix_sq, t + 1)
                    else:
                        split_scaled(act_lo[:, t, :], y[:, t, :], col(beta, t), act_hi[:, t, :], ALU.add)\
                            .then_inc(act_ready, 1)

                dve.wait_ge(stat_act, 2 * n + 1)
                link(centre(0))
                dve.wait_ge(stat_done, 2 + 2 * n + 2)
                dve.wait_ge(stat_act, 2 * n + 2)
                link(nc.vector.tensor_tensor(stat[:, :], ps[:, 5, :], stat[:, :], ALU.subtract))
                nc.vector.tensor_scalar(stat[:, :], stat[:, :], 0.0, None, ALU.max).then_inc(sum_ready, 1)
                for p in range(1, 4):
                    link(centre(p))
                dve.wait_ge(rstd_ready, RSTD_LN + n + 1 if n < 4 else 0)
                for t in range(KT):
                    nc.vector.scalar_tensor_tensor(y[:, t, :], y[:, t, :], col(gain, t), rstd[:, :],
                                                   ALU.mult, ALU.mult).then_inc(norm_z, 1)
                    if t:
                        lo(t - 1)
                lo(KT - 1)

            def mlp(first, layer, scaled, sq):
                def up(j, more, done):
                    dve.wait_ge(relu_done, done + j + 1)
                    nc.vector.tensor_tensor(relu[:, j % 2, :, :], relu[:, j % 2, :, :], relu[:, j % 2, :, :],
                                            ALU.mult).then_inc(sqr_done, 1)
                    dve.wait_ge(hid_split, done + j + 1)
                    split(hid_lo[:, 2 * j:2 * j + 2, :], relu[:, j % 2, :, :], hid_hi[:, 2 * j:2 * j + 2, :])\
                        .then_inc(slab_read, 1)
                    cast(first + j + 2, more)

                dve.wait_ge(x_scaled, scaled)
                with dve.Fori(0, 3) as r:
                    for j in range(4):
                        up(j, r * 8, r * 4 + 16 * layer)
                    for j in range(4):
                        add_out(first + 4 + j, 2 * j, r * 8)
                        cast(first + 4 + j + 2, r * 8)
                for j in range(4):
                    up(j, 24, 12 + 16 * layer)
                last_out(first + 28, sq)

            RSTD_LN = 2

            for p in range(4):
                dve.wait_ge(x_hi, p + 1)
                split(act_lo[:, 2 * p:2 * p + 2, :], y[:, 2 * p:2 * p + 2, :], act_hi[:, 2 * p:2 * p + 2, :])\
                    .then_inc(act_ready, 2)
                if p < 2:
                    cast(p)
            dve.wait_ge(const_landed, 16 * 7)
            dve.wait_ge(line_done, 1)
            nc.vector.tensor_tensor(rstd[0:16, 0:LINE], ps[0:16, 7, 0:LINE], sum1[0:16, 0:LINE], ALU.add)\
                .then_inc(line_ready, 1)
            nc.vector.tensor_scalar(negsink[:, :], vec[:, VEC["sink"]:VEC["sink"] + 16], -1.0, None, ALU.mult)

            def rope_rotate(n):
                dve.wait_ge(rope_in, n + 1)
                if n:
                    dve.wait_ge(rope_lo, n)
                nc.vector.tensor_tensor(rope_cos[:, :], rope_raw[:, :], cossin[:, 0, :], ALU.mult)
                dve.wait_ge(rope_swapped, n + 1)
                bank = (6, 3, 7, 3, 7)[n]
                link(nc.vector.tensor_tensor(rope_sin[:, :], ps[:, bank, :], cossin[:, 1, :], ALU.mult))
                nc.vector.tensor_tensor(rope_cos[:, :], rope_cos[:, :], rope_sin[:, :], ALU.add)\
                    .then_inc(rope_out, 1)

            dve.wait_ge(line_done, 1)
            dve.wait_ge(c_read, 1)
            link(nc.vector.tensor_tensor(sum1[:, :], tmp[:, 0, 0, :], tmp[:, 0, 1, :], ALU.add))
            nc.vector.tensor_copy(negmax[:, 0:1], sum1[:, 0:1]).then_inc(c_split, 1)
            nc.vector.tensor_copy(negmax[:, 1:2], sum1[:, 0:1]).then_inc(slab_read, 1)
            cast(2)
            dve.wait_ge(slab_read, 1)
            dve.wait_ge(c_read, 2)
            nc.vector.tensor_tensor(sum1[:, :], sum1[:, :], tmp[:, 1, 0, :], ALU.add).then_inc(sum_ready, 1)
            nc.vector.tensor_copy(sum2[:, :], tmp[:, 1, 1, :]).then_inc(slab_read, 1)
            cast(3)
            dve.wait_ge(slab_read, 2)
            dve.wait_ge(c_read, 3)
            nc.vector.tensor_tensor(sum2[:, :], sum2[:, :], tmp[:, 0, 0, :], ALU.add).then_inc(sum_ready, 1)
            nc.vector.tensor_copy(negmax[:, 0:1], tmp[:, 0, 0, 0:1]).then_inc(slab_read, 1)
            for t in range(5):
                src, gain = (rstd, col("g_q", t)) if t < 3 else (stat, col("g_kv", t - 3))
                dve.wait_ge(rstd_ready, 1 if t < 3 else 2)
                nc.vector.scalar_tensor_tensor(c_raw[:, t, :], c_raw[:, t, :], gain, src[:, :],
                                               ALU.mult, ALU.mult).then_inc(c_full, 1)
                if t:
                    dve.wait_ge(c_split, 1 + t)
                    split(c_lo[:, t - 1, :], c_raw[:, t - 1, :], c_hi[:, t - 1, :]).then_inc(c_ready, 1)
            dve.wait_ge(c_split, 6)
            split(c_lo[:, 4, :], c_raw[:, 4, :], c_hi[:, 4, :]).then_inc(c_ready, 1)
            cast(4)
            rope_rotate(0)
            dve.wait_ge(rope_hi, 1)
            split(kr_lo[:, :], rope_cos[:, :], kr_hi[:, :]).then_inc(rope_lo, 1)

            for half in range(2):
                g = MLA_HALF + 4 * half
                for p in range(2):
                    n = 6 * half + p
                    dve.wait_ge(proj_hi, n + 1)
                    split_scaled(act_lo[:, 4 + 2 * p:6 + 2 * p, :], ps[:, 4 * p:4 * p + 2, :], MLA_SCALE,
                                 act_hi[:, 4 + 2 * p:6 + 2 * p, :]).then_inc(slab_read, 1)
                    cast(g + p + 2)
                    rope_rotate(1 + 2 * half + p)
                    dve.wait_ge(rope_hi, 2 + 2 * half + p)
                    split(qr_lo[:, p, :], rope_cos[:, :], qr_hi[:, p, :]).then_inc(rope_lo, 1)
                for p, hi, lo in ((2, kn_hi, kn_lo), (3, mv_hi, mv_lo)):
                    for q in range(2):
                        n = 6 * half + 2 * p - 2 + q
                        dve.wait_ge(proj_hi, n + 1)
                        b = 4 * (p - 2) + 2 * q
                        ins = split(lo[:, 2 * q:2 * q + 2, :], ps[:, b:b + 2, :], hi[:, 2 * q:2 * q + 2, :])
                    ins.then_inc(slab_read, 1)
                    cast(g + p + 2)

                def mla_bias(u):
                    bias(mla, m_prob, u, lambda w: strip[:, T - w:T])
                    invert(mla, u)

                mla_bias(4 * half)
                for u in range(4 * half, 4 * half + 4):
                    turn_lo(mla, m_pt_hi, m_pt_lo, u)
                    if u < 4 * half + 3:
                        mla_bias(u + 1)
                    dve.wait_ge(mla.out_hi, u + 1)
                    split(act_lo[:, u, :], ps[:, 6 + u % 2, :], act_hi[:, u, :]).then_inc(act_ready, 1)

            dve.wait_ge(x_scaled, 4)
            last_out(MLA_OUT, 0)
            layer_norm(0, LN_0, "mix_g0", "mix_b0")
            mlp(MLP0, 0, 12, 4)
            layer_norm(1, LN_1, "mlp_g0", "mlp_b0")

            for half in range(2):
                g = SWA_HALF + 4 * half
                n = 12 + 5 * half
                dve.wait_ge(proj_hi, n + 1)
                split(swa_k_lo[:, :], ps[:, banks(g), :], swa_k_hi[:, :]).then_inc(slab_read, 1)
                cast(g + 2)
                dve.wait_ge(proj_hi, n + 3)
                for v_hi, v_lo, c in ((va_hi, va_lo, 0), (vb_hi, vb_lo, 64)):
                    ins = split(v_lo[:, :, c:c + 64],
                                ps[:, banks(g + 1), :].rearrange("p (i c) -> p i c", i=4)[:, :, c:c + 64],
                                v_hi[:, :, c:c + 64])
                ins.then_inc(slab_read, 1)
                cast(g + 3)
                for p in range(2):
                    b = banks(g + 2 + p)
                    dve.wait_ge(proj_hi, n + 4 + p)
                    split_scaled(sq_lo[:, 2 * p:2 * p + 2, :], ps[:, b:b + 2, :], HEAD_SCALE,
                                 sq_hi[:, 2 * p:2 * p + 2, :]).then_inc(slab_read, 1)
                    cast(g + 4 + p)
                dve.wait_ge(strips_landed, 16 * (half + 1))
                u0 = 8 * half

                def swa_bias(u):
                    c = 2 * P * (u % 8)
                    bias(swa, s_prob, u, lambda w: strips[:, c + 2 * P - w:c + 2 * P], negsink[:, u:u + 1])
                    invert(swa, u, True)

                swa_bias(u0)
                swa_bias(u0 + 1)
                for u in range(u0, u0 + 8):
                    turn_lo(swa, s_pt_hi, s_pt_lo, u)
                    if u + 2 < u0 + 8:
                        swa_bias(u + 2)
                    if u % 2:
                        t = u // 2
                        dve.wait_ge(swa.out_hi, t + 1)
                        split(o_lo[:, t, :], ps[:, 6 + t % 2, :], o_hi[:, t, :]).then_inc(act_ready, 1)

            dve.wait_ge(x_scaled, 20)
            last_out(SWA_OUT, 8)
            layer_norm(2, LN_2, "mix_g1", "mix_b1")
            mlp(MLP1, 1, 28, 12)
            layer_norm(3, LN_3, "mlp_g1", "mlp_b1", True)

            dve.wait_ge(rstd_ready, 7)
            dve.wait_ge(u_zeroed, 1)
            for i in range(2):
                g = CONV + 3 * i
                for j, dst in ((0, zc[:, :, :]), (1, tmp[:, 0, :, :]), (2, yc[:, 2 * i:2 * i + 2, :])):
                    b = banks(g + j)
                    dve.wait_ge(slab_done, g + j + 1)
                    nc.vector.tensor_tensor(dst, ps[:, b:b + 2, :], pair(rstd[:, :]), ALU.mult)\
                        .then_inc(slab_read, 1)
                    cast(g + j + 2)
                    dve.wait_ge(slab_read, g + j + 1)
                    if j == 1:
                        link(nc.vector.tensor_tensor(u_pad[:, :, 2:T + 2], tmp[:, 0, :, :], zc[:, :, :], ALU.mult))
                        for k in range(2):
                            c, t = conv[:, k, :], 2 * i + k
                            link(nc.vector.tensor_scalar(c, u_pad[:, k, 2:T + 2], col("conv_w", 8 + t),
                                                         col("conv_b", t), ALU.mult, ALU.add))
                            link(nc.vector.scalar_tensor_tensor(c, u_pad[:, k, 1:T + 1], col("conv_w", 4 + t), c,
                                                                ALU.mult, ALU.add))
                            link(nc.vector.scalar_tensor_tensor(c, u_pad[:, k, 0:T], col("conv_w", t), c,
                                                                ALU.mult, ALU.add))
                nc.vector.tensor_tensor(yc[:, 2 * i:2 * i + 2, :], yc[:, 2 * i:2 * i + 2, :], conv[:, :, :],
                                        ALU.mult).then_inc(conv_done, 1)
                dve.wait_ge(sq_done, 24 + i + 1)
                if i:
                    link(nc.vector.tensor_tensor(sum1[:, :], sum1[:, :], tmp[:, 1, 0, :], ALU.add))
                    nc.vector.tensor_tensor(sum1[:, :], sum1[:, :], tmp[:, 1, 1, :], ALU.add).then_inc(sum_ready, 1)
                else:
                    link(nc.vector.tensor_tensor(sum1[:, :], tmp[:, 1, 0, :], tmp[:, 1, 1, :], ALU.add))
            dve.wait_ge(rstd_ready, 9)
            for t in range(4):
                nc.vector.scalar_tensor_tensor(yc[:, t, :], yc[:, t, :], col("g_oc", t), stat[:, :],
                                               ALU.mult, ALU.mult).then_inc(conv_done, 1)
                dve.wait_ge(mix_hi, t + 1)
                split(o_lo[:, t, :], yc[:, t, :], o_hi[:, t, :]).then_inc(act_ready, 1)

            for half in range(2):
                g = DIL_HALF + 4 * half
                n = 22 + 4 * half
                for p, (hi, lo, scale, gain) in enumerate(((dq_hi, dq_lo, HEAD_SCALE, "qn_g"),
                                                           (dk_hi, dk_lo, 1.0, "kn_g"))):
                    b, k = banks(g + p), 2 * half + p
                    dve.wait_ge(slab_done, g + p + 1)
                    dve.wait_ge(slab_read, g + p)
                    nc.vector.tensor_tensor(tmp[:, 0, :, :], ps[:, b:b + 2, :], pair(rstd[:, :]), ALU.mult)\
                        .then_inc(qk_raw, 1)
                    cast(g + p + 2)
                    dve.wait_ge(qk_rstd, k + 1)
                    nc.vector.scalar_tensor_tensor(tmp[:, 0, :, :], tmp[:, 0, :, :], col(gain), tmp[:, 1, :, :],
                                                   ALU.mult, ALU.mult).then_inc(qk_full, 1)
                    dve.wait_ge(proj_hi, n + p + 1)
                    split_scaled(lo[:, :, :], tmp[:, 0, :, :], scale, hi[:, :, :]).then_inc(slab_read, 1)
                for p in range(2):
                    dve.wait_ge(slab_done, g + p + 3)
                    dve.wait_ge(slab_read, g + 2)
                    nc.vector.tensor_tensor(tmp[:, 0, p, :].rearrange("p (i c) -> p i c", i=4),
                                            ps[:, banks(g + 2 + p), :].rearrange("p (i c) -> p i c", i=4),
                                            rstd_tok[:, :].unsqueeze(2).broadcast_to([P, 4, P]), ALU.mult)\
                        .then_inc(dv_raw, 1)
                    cast(g + p + 4)
                    dve.wait_ge(proj_hi, n + p + 3)
                    split(dv_lo[:, p, :], tmp[:, 0, p, :], dv_hi[:, p, :]).then_inc(slab_read, 1)
                dve.wait_ge(strips_landed, 16 * (half + 3))
                u0 = 4 * half

                def dil_bias(u):
                    c = T * (u % 4)
                    bias(dil, d_prob, u, lambda w: strips[:, c + T - w:c + T])
                    invert(dil, u)

                dil_bias(u0)
                for u in range(u0, u0 + 4):
                    turn_lo(dil, d_pt_hi, d_pt_lo, u)
                    if u + 1 < u0 + 4:
                        dil_bias(u + 1)
                    r, t = 64 * (u % 2), u // 2
                    dve.wait_ge(sq_done, 26 + u + 1)
                    ins = split_scaled(o_lo[r:r + 64, 4 + t, :], ps[r:r + 64, 6 + u % 2, :],
                                       vec[r:r + 64, VEC["g_oa"] + t:VEC["g_oa"] + t + 1],
                                       o_hi[r:r + 64, 4 + t, :]).then_inc(dil.out_read, 1)
                    if u % 2:
                        if t:
                            ins = nc.vector.tensor_tensor(sum2[:, :], sum2[:, :], stat[:, :], ALU.add)
                        else:
                            dve.wait_ge(stat_done, 12)
                            ins = nc.vector.tensor_copy(sum2[:, :], stat[:, :])
                        ins.then_inc(mix_sq, 1)
                        dve.wait_ge(mix_sq, 8 + t + 1)
                        dve.wait_ge(dil.out_read, u + 1)
                        ins = nc.vector.tensor_copy(negmax[:, 0:1], sum2[:, 0:1])
                        ins.then_inc(act_ready, 1)

            def rms_out(tiles, n, gain, last):
                for k, t in enumerate(tiles):
                    dve.wait_ge(mix_hi, n_hi[0] + 1)
                    n_hi[0] += 1
                    split_scaled(act_lo[:, t, :], y[:, t, :], col(gain, t), act_hi[:, t, :])\
                        .then_inc(act_ready, 1)
                sums(tiles, n, n in (34, 38), last, False)

            n_hi = [4]
            dve.wait_ge(rstd_ready, 10)
            for j in range(4):
                g = MIX_OUT + j
                b = banks(g)
                dve.wait_ge(slab_done, g + 1)
                link(nc.vector.tensor_tensor(conv[:, :, :], ps[:, 4 + b:6 + b, :], pair(stat[:, :]), ALU.mult))
                link(nc.vector.tensor_tensor(y[:, 2 * j:2 * j + 2, :], y[:, 2 * j:2 * j + 2, :], conv[:, :, :],
                                             ALU.add))
                nc.vector.tensor_tensor(y[:, 2 * j:2 * j + 2, :], y[:, 2 * j:2 * j + 2, :], ps[:, b:b + 2, :],
                                        ALU.add).then_inc(slab_read, 1)
                cast(g + 2)
                rms_out([2 * j, 2 * j + 1], 34 + j, "g_ffn", j == 3)

            dve.wait_ge(rstd_ready, 11)
            dve.wait_ge(u_zeroed, 2)
            for rnd, (first, down, before, count) in enumerate(((FFN_A, FFN_A_DOWN, 0, FF_A),
                                                                (FFN_B, FFN_B_DOWN, FF_A, FF_B))):
                with dve.Fori(0, count // 2) as i:
                    for b in range(2):
                        more, at = i * 2, before + b
                        bank = banks(first + b)
                        dve.wait_ge(slab_done, first + b + 1 + more)
                        nc.vector.tensor_tensor(gate[:, b, 2:T + 2], ps[:, bank, :], rstd[:, :], ALU.mult)\
                            .then_inc(ff_step, 1)
                        nc.vector.tensor_tensor(ffh[:, b, :], ps[:, bank + 1, :], rstd[:, :], ALU.mult)\
                            .then_inc(slab_read, 1)

                        def taps(name, k):
                            c = VEC[name] + k * 22 + at
                            return vec[:, bass.ds(i * 2 + c, 1)]

                        dve.wait_ge(ff_step, 3 * at + 1 + i * 6)
                        nc.vector.tensor_scalar(gconv[:, b, :], gate[:, b, 2:T + 2], taps("fconv_w", 2),
                                                taps("fconv_b", 0), ALU.mult, ALU.add).then_inc(ff_step, 1)
                        dve.wait_ge(ff_step, 3 * at + 2 + i * 6)
                        nc.vector.scalar_tensor_tensor(gconv[:, b, :], gate[:, b, 1:T + 1], taps("fconv_w", 1),
                                                       gconv[:, b, :], ALU.mult, ALU.add).then_inc(ff_step, 1)
                        dve.wait_ge(ff_step, 3 * at + 3 + i * 6)
                        nc.vector.scalar_tensor_tensor(gconv[:, b, :], gate[:, b, 0:T], taps("fconv_w", 0),
                                                       gconv[:, b, :], ALU.mult, ALU.add).then_inc(conv_done, 1)
                        cast(first + b + 2, more, SLAB)
                        dve.wait_ge(silu_done, at + 1 + more)
                        nc.vector.tensor_tensor(ffh[:, b, :], ffh[:, b, :], silu[:, b, :], ALU.mult)\
                            .then_inc(ffh_done, 1)
                        dve.wait_ge(ffh_hi, at + 1 + more)
                        split(h_lo[:, bass.ds(i * 2 + b, 1), :], ffh[:, b:b + 1, :],
                              h_hi[:, bass.ds(i * 2 + b, 1), :]).then_inc(h_ready, 1)
                for j in range(8):
                    g = down + j
                    dve.wait_ge(slab_done, g + 1)
                    nc.vector.tensor_tensor(y[:, j, :], y[:, j, :], ps[:, banks(g), :], ALU.add)\
                        .then_inc(slab_read, 1)
                    cast(g + 2)
                    if rnd:
                        rms_out([j], 38 + j, "g_ple", j == 7)

            dve.wait_ge(p_split, 1)
            split(p_lo[:, :, :], p_raw[:, :, :], p_hi[:, :, :]).then_inc(p_split, 1)
            dve.wait_ge(slab_done, PLE_PROJ + 1)
            link(nc.vector.tensor_copy(proj[:, 4:6, :], ps[:, 4:6, :]))
            dve.wait_ge(proj_act, 1)
            nc.vector.tensor_copy(proj[:, 6:8, :], ps[:, 6:8, :]).then_inc(slab_read, 1)
            cast(PLE_PROJ + 2)
            dve.wait_ge(rstd_ready, 12)
            for j in range(4):
                b = banks(PLE_GATE + j)
                dve.wait_ge(slab_done, PLE_GATE + j + 1)
                nc.vector.tensor_tensor(gate_in[:, j % 2, :, :], ps[:, b:b + 2, :], pair(rstd[:, :]), ALU.mult)\
                    .then_inc(slab_read, 1)
                cast(PLE_GATE + j + 2)
                dve.wait_ge(slab_read, PLE_GATE + j + 1)
                dve.wait_ge(sig_done, j + 1)
                link(nc.vector.tensor_tensor(gate_in[:, j % 2, :, :], gate_in[:, j % 2, :, :],
                                             proj[:, 2 * j:2 * j + 2, :], ALU.mult))
                nc.vector.tensor_tensor(y[:, 2 * j:2 * j + 2, :], y[:, 2 * j:2 * j + 2, :],
                                        gate_in[:, j % 2, :, :], ALU.add).then_inc(out_ready, 1)

        @block.tensor
        def _(pe):
            def product(out, l_hi, l_lo, r_hi, r_lo, start, stop, shared=False):
                mm = nc.tensor.matmul
                mm(out, l_lo, r_hi, start=start, stop=False, skip_group_check=shared)
                mm(out, l_hi, r_hi, start=False, stop=False, skip_group_check=shared)
                return mm(out, l_hi, r_lo, start=False, stop=stop, skip_group_check=shared)

            def gemm(g, outs, kt, hi, lo, ready=None, more=0, free=None, at=0):
                s = g % 2
                if free is None:
                    free = g - 1
                if free > 0:
                    pe.wait_ge(slab_read, free + more)
                pe.wait_ge(cast_lo, g + 1 + more)
                for k in range(kt):
                    if ready:
                        ready(k)
                    for m, o in enumerate(outs):
                        c = (k * len(outs) + m) * P
                        last = product(o, w_hi[s][:, c:c + P], w_lo[s][:, c:c + P], hi[:, at + k, :],
                                       lo[:, at + k, :], k == 0, k == kt - 1)
                last.then_inc(slab_done, 1)

            def plain(g, kt=KT, hi=act_hi, lo=act_lo, ready=None, more=0, n=2, free=None):
                b = banks(g)
                gemm(g, [ps[:, b + m, :] for m in range(n)], kt, hi, lo, ready, more, free)

            def act_tiles(gen):
                return lambda k: pe.wait_ge(act_ready, gen + k + 1)

            def values(g, bank, free):
                s = g % 2
                pe.wait_ge(slab_read, free)
                pe.wait_ge(cast_lo, g + 1)
                for i in range(4):
                    for k in range(KT):
                        q = slice(i * P, (i + 1) * P)
                        last = product(ps[:, bank, q], act_hi[:, k, q], act_lo[:, k, q],
                                       w_hi[s][:, k * P:(k + 1) * P], w_lo[s][:, k * P:(k + 1) * P],
                                       k == 0, k == KT - 1)
                last.then_inc(slab_done, 1)

            def column_sums(src, bank, rhs=None):
                last = nc.tensor.matmul(ps[:, bank, :], ones, src, start=True, stop=True)
                last.then_inc(stat_done, 1)

            def score(a, u, operands, first):
                h, at = a.h, a.score_banks[u % 2]
                for m, group in enumerate(h.groups):
                    v = u - a.ahead
                    if v >= first:
                        read = 4 * v + sum(len(x) for x in h.groups[:m + 1])
                        pe.wait_ge(a.biased, read)
                    for i in group:
                        bank, c = h.place[i]
                        dst = ps[:, at + bank, c:c + h.width[i]]
                        parts = operands(u, i, slice(h.key0[i], h.key0[i] + h.width[i]))
                        for x, part in enumerate(parts):
                            last = product(dst, *part, x == 0, x == len(parts) - 1)
                    last.then_inc(a.scored, 1)

            def turn(a, u, prob):
                h = a.h
                waited = 0
                for n in range(a.nseg):
                    if u:
                        pe.wait_ge(a.turn_lo, a.nseg * (u - 1) + n + 1)
                    for i, j, c in h.blocks(n):
                        need = h.order.index(i) + 1
                        if need > waited:
                            pe.wait_ge(a.normed, 4 * u + need)
                            waited = need
                        k = h.off[i] + j * P - h.key0[i]
                        last = nc.tensor.transpose(ps[:, a.trans_bank + n, c:c + P], prob[:, u % 2, k:k + P], ident)
                    last.then_inc(a.turned, 1)

            def mix(a, u, bank, pt_hi, pt_lo, v_of, start=True, stop=True):
                for j, (reach, seg, c) in enumerate(a.h.keys):
                    pe.wait_ge(a.turn_lo, a.nseg * u + seg + 1)
                    c += BANK * seg
                    w = reach * P
                    last = product(ps[:, bank, j * P:j * P + w], *v_of(u, j), pt_hi[:, c:c + w], pt_lo[:, c:c + w],
                                   start and j == 0, stop and j == 3, True)
                if stop:
                    last.then_inc(a.mixed, 1)

            for j in range(3):
                g = MLA_IN + j
                plain(g, ready=act_tiles(X_IN) if j == 0 else None)
                if j == 0:
                    pe.wait_ge(const_landed, 16 * 7)
                    nc.tensor.matmul(ps[0:16, 7, 0:LINE], stat[0:32, 0:16], sum2[0:32, 0:LINE], start=True,
                                     stop=True).then_inc(line_done, 1)
            pe.wait_ge(sum_ready, 1)
            column_sums(sum1[:, :], 4)
            pe.wait_ge(sum_ready, 2)
            column_sums(sum2[:, :], 5)
            pe.wait_ge(rope_in, 1)
            nc.tensor.matmul(ps[:, 6, :], swap, rope_raw[:, :], start=True, stop=True).then_inc(rope_swapped, 1)

            def mla_operands(u, i, keys):
                x, q, r = u % 4, slice(i * P, (i + 1) * P), 64 * (u % 2)
                return [(act_hi[:, 4 + x, q], act_lo[:, 4 + x, q], kn_hi[:, x, keys], kn_lo[:, x, keys]),
                        (qr_hi[r:r + 64, x // 2, q], qr_lo[r:r + 64, x // 2, q],
                         kr_hi[r:r + 64, keys], kr_lo[r:r + 64, keys])]

            def mla_values(u, j):
                c = slice(P * (u % 4), P * (u % 4) + P)
                return mv_hi[:, j, c], mv_lo[:, j, c]

            def c_tiles(at):
                return lambda k: pe.wait_ge(c_ready, at + k + 1)

            for half in range(2):
                g = MLA_HALF + 4 * half
                if half:
                    pe.wait_ge(mla.biased, 16)
                else:
                    pe.wait_ge(slab_read, 3)
                gemm(g, [ps[:, b, :] for b in range(3)], 3, c_hi, c_lo, c_tiles(0), free=g)
                if half:
                    pe.wait_ge(mla.turn_lo, 3 * 4)
                    pe.wait_ge(act_ready, MLA_O + 4)
                else:
                    pe.wait_ge(rope_out, 1)
                gemm(g + 1, [ps[:, b, :] for b in range(4, 7)], 3, c_hi, c_lo, c_tiles(0), free=g)
                pe.wait_ge(rope_in, 2 + 2 * half)
                nc.tensor.matmul(ps[:, 3, :], swap, rope_raw[:, :], start=True, stop=True).then_inc(rope_swapped, 1)
                pe.wait_ge(rope_out, 2 + 2 * half)
                gemm(g + 2, [ps[:, b, :] for b in range(4)], 2, c_hi, c_lo, c_tiles(3), free=g + 1, at=3)
                pe.wait_ge(rope_in, 3 + 2 * half)
                nc.tensor.matmul(ps[:, 7, :], swap, rope_raw[:, :], start=True, stop=True).then_inc(rope_swapped, 1)
                pe.wait_ge(rope_out, 3 + 2 * half)
                s = (g + 3) % 2
                pe.wait_ge(slab_read, g + 2)
                pe.wait_ge(cast_lo, g + 4)
                for i in range(4):
                    for k in range(2):
                        q = slice(i * P, (i + 1) * P)
                        last = product(ps[:, 4 + i, :], c_hi[:, 3 + k, q], c_lo[:, 3 + k, q],
                                       w_hi[s][:, k * T:(k + 1) * T], w_lo[s][:, k * T:(k + 1) * T],
                                       k == 0, k == 1)
                last.then_inc(slab_done, 1)
                pe.wait_ge(slab_read, g + 3)
                pe.wait_ge(rope_lo, 3 + 2 * half)
                u0 = 4 * half
                score(mla, u0, mla_operands, u0)
                pe.wait_ge(slab_read, g + 4)
                for u in range(u0, u0 + 4):
                    turn(mla, u, m_prob)
                    if u < u0 + 3:
                        score(mla, u + 1, mla_operands, u0)
                    mix(mla, u, 6 + u % 2, m_pt_hi, m_pt_lo, mla_values)

            def layer_stats(n):
                for k in range(2):
                    pe.wait_ge(sum_ready, 2 + 3 * n + k + 1)
                    column_sums((sum1, sum2)[k][:, :], 4 + k)

            def mlp(first, gen):
                def hidden(g, more):
                    return lambda k: pe.wait_ge(slab_read, first + k // 2 + 1 + more)

                def rnd(more):
                    for j in range(4):
                        plain(first + j, more=more, ready=act_tiles(gen))
                    for j in range(4):
                        plain(first + 4 + j, hi=hid_hi, lo=hid_lo, more=more, ready=hidden(j, more) if j == 0 else None)

                with pe.Fori(0, 3) as r:
                    rnd(r * 8)
                rnd(24)

            pe.wait_ge(mla.turn_lo, 3 * 8)
            for j in range(4):
                plain(MLA_OUT + j, ready=act_tiles(MLA_O))
            layer_stats(0)
            mlp(MLP0, LN_0)
            layer_stats(1)

            def swa_operands(u, i, keys):
                t, q, r = (u // 2) % 4, slice(i * P, (i + 1) * P), 64 * (u % 2)
                return [(sq_hi[r:r + 64, t, q], sq_lo[r:r + 64, t, q], swa_k_hi[r:r + 64, keys],
                         swa_k_lo[r:r + 64, keys])]

            def swa_values(u, j):
                hi, lo = ((va_hi, va_lo), (vb_hi, vb_lo))[u % 2]
                return hi[:, j, :], lo[:, j, :]

            for half in range(2):
                g = SWA_HALF + 4 * half
                if half:
                    pe.wait_ge(swa.biased, 32)
                plain(g, n=1, ready=act_tiles(LN_1))
                values(g + 1, banks(g + 1), g)
                for p in range(2):
                    plain(g + 2 + p)
                pe.wait_ge(slab_read, g + 4)
                u0 = 8 * half
                score(swa, u0, swa_operands, u0)
                score(swa, u0 + 1, swa_operands, u0)
                for u in range(u0, u0 + 8):
                    turn(swa, u, s_prob)
                    if u + 2 < u0 + 8:
                        score(swa, u + 2, swa_operands, u0)
                    t = u // 2
                    if u % 2 == 0 and t >= 2:
                        pe.wait_ge(act_ready, SWA_O + t - 1)
                    mix(swa, u, 6 + t % 2, s_pt_hi, s_pt_lo, swa_values, u % 2 == 0, u % 2 == 1)

            for j in range(4):
                plain(SWA_OUT + j, hi=o_hi, lo=o_lo, ready=act_tiles(SWA_O))
            layer_stats(2)
            mlp(MLP1, LN_2)
            layer_stats(3)

            for j in range(6):
                plain(CONV + j, ready=act_tiles(LN_3) if j == 0 else None)
                if j == 0:
                    pe.wait_ge(sum_ready, 15)
                    column_sums(sum2[:, :], 4)
                    for i in range(4):
                        last = nc.tensor.matmul(ps[:, 5, i:i + 1], sum2[:, i * P:(i + 1) * P], ones[:, 0:1],
                                                start=True, stop=True)
                    last.then_inc(stat_done, 1)

            def dil_operands(u, i, keys):
                p, q, r = (u // 2) % 2, slice(i * P, (i + 1) * P), 64 * (u % 2)
                return [(dq_hi[r:r + 64, p, q], dq_lo[r:r + 64, p, q], dk_hi[r:r + 64, p, keys],
                         dk_lo[r:r + 64, p, keys])]

            def dil_values(u, j):
                p, c = (u // 2) % 2, slice(j * P, (j + 1) * P)
                return dv_hi[:, p, c], dv_lo[:, p, c]

            def head_norm(n, bank):
                pe.wait_ge(qk_sq, n + 1)
                for k in range(2):
                    last = nc.tensor.matmul(ps[:, bank + k, :], ones64, tmp[:, 1, k, :], start=True, stop=True)
                last.then_inc(qk_stat, 1)

            for half in range(2):
                g = DIL_HALF + 4 * half
                if half:
                    pe.wait_ge(dil.turn_lo, 3 * 4)
                plain(g)
                if half == 0:
                    pe.wait_ge(sum_ready, 16)
                    column_sums(sum1[:, :], 6)
                plain(g + 1, free=g - 1 if half == 0 else g - 1)
                head_norm(2 * half, 4)
                values(g + 2, banks(g + 2), g + 1)
                if half == 0:
                    pe.wait_ge(rstd_ready, 9)
                else:
                    pe.wait_ge(dil.out_read, 4)
                head_norm(2 * half + 1, 6)
                values(g + 3, banks(g + 3), g + 2)
                pe.wait_ge(slab_read, g + 4)
                u0 = 4 * half
                score(dil, u0, dil_operands, u0)
                for u in range(u0, u0 + 4):
                    turn(dil, u, d_prob)
                    if u < u0 + 3:
                        score(dil, u + 1, dil_operands, u0)
                    if u - 2 >= u0:
                        pe.wait_ge(dil.out_read, u - 1)
                    mix(dil, u, 6 + u % 2, d_pt_hi, d_pt_lo, dil_values)

            pe.wait_ge(dil.turn_lo, 3 * 8)
            for j in range(4):
                g = MIX_OUT + j
                s, b = g % 2, banks(g)
                if j < 2:
                    pe.wait_ge(dil.turn_lo, 3 * 8)
                    if j == 0:
                        pe.wait_ge(dil.out_read, 8)
                else:
                    pe.wait_ge(slab_read, g - 1)
                if j == 1:
                    pe.wait_ge(rstd_ready, 10)
                pe.wait_ge(cast_lo, g + 1)
                for k in range(KT):
                    if j == 0:
                        pe.wait_ge(act_ready, MIX_Y + k + 1)
                    if j == 0 and k == 4:
                        pe.wait_ge(mix_sq, 12)
                        column_sums(sum2[:, :], 0)
                    for m in range(2):
                        c = (k * 2 + m) * P
                        last = product(ps[:, b + m + (4 if k >= 4 else 0), :], w_hi[s][:, c:c + P],
                                       w_lo[s][:, c:c + P], o_hi[:, k, :], o_lo[:, k, :], k % 4 == 0, k % 4 == 3)
                last.then_inc(slab_done, 1)

            for rnd, (first, down, before, count) in enumerate(((FFN_A, FFN_A_DOWN, 0, FF_A),
                                                                (FFN_B, FFN_B_DOWN, FF_A, FF_B))):
                if rnd == 0:
                    plain(first, ready=act_tiles(FFN_X))
                    pe.wait_ge(sum_ready, 17)
                    column_sums(sum2[:, :], 7)
                    plain(first + 1)
                with pe.Fori(1 if rnd == 0 else 0, count // 2) as i:
                    for b in range(2):
                        plain(first + b, more=i * 2)
                for j in range(8):
                    def hidden(k):
                        pe.wait_ge(h_ready, before + k + 1)
                    plain(down + j, kt=count, hi=h_hi, lo=h_lo, ready=hidden if j == 0 else None, n=1)

            s = PLE_PROJ % 2
            pe.wait_ge(p_split, 2)
            pe.wait_ge(slab_read, PLE_PROJ)
            pe.wait_ge(cast_lo, PLE_PROJ + 1)
            for m in range(KT):
                for k in range(2):
                    c = (k * KT + m) * P
                    last = product(ps[:, m, :], w_hi[s][:, c:c + P], w_lo[s][:, c:c + P], p_hi[:, k, :],
                                   p_lo[:, k, :], k == 0, k == 1)
            last.then_inc(slab_done, 1)
            for j in range(4):
                plain(PLE_GATE + j, ready=act_tiles(PLE_X) if j == 0 else None,
                      free=PLE_GATE if j < 2 else None)
                if j == 0:
                    pe.wait_ge(sum_ready, 18)
                    column_sums(sum2[:, :], 7)


def rope_table():
    half = 32
    inv = np.float32(10000.0) ** (-np.arange(half, dtype=np.float32) / np.float32(half))
    ang = (np.arange(T, dtype=np.float32)[:, None] * inv[None, :].astype(np.float32)).T.astype(np.float32)
    cos, sin = np.cos(ang), np.sin(ang)
    return np.stack([np.concatenate([cos] * 4), np.concatenate([-sin, sin] * 2)], 1).astype(np.float32)


def matrices():
    eye = np.eye(P)
    ones = np.full((P, P), 1.0 / D)
    heads = np.kron(np.eye(2), np.full((64, 64), 1.0 / 64))
    swap = eye[np.arange(P) ^ 32]
    return np.stack([eye, ones, heads, swap], 1).astype(np.float32)


def strip_distance():
    return np.arange(P)[:, None] + (T - P) - np.arange(T)[None, :]


def causal_table():
    return np.where(strip_distance() >= 0, 0.0, MASKED).astype(np.float32)


def dilated_table():
    d = strip_distance()
    count = (d <= 128).astype(int) + (d % 4 == 0) + (d % 16 == 0)
    slopes = np.exp2(-np.arange(1, 9, dtype=np.float32))
    table = np.where((d >= 0) & (count > 0), np.log(np.maximum(count, 1)) - slopes[:, None, None] * d, MASKED)
    return np.ascontiguousarray(table.reshape(2, 4, P, T).transpose(0, 2, 1, 3).reshape(2, P, 4 * T), np.float32)


def t5_tables():
    d = 2 * P - 1 - np.arange(LINE)
    n = np.maximum(d, 0)
    nf = np.maximum(n, 1).astype(np.float32)
    large = 16 + (np.log(nf / np.float32(16)) / np.float32(np.log(128 / 16)) * np.float32(16)).astype(np.int32)
    bucket = np.where(n < 16, n, np.minimum(large, 31))
    valid = (d >= 0) & (d < P)
    onehot = ((np.arange(32)[:, None] == bucket[None, :]) & valid[None, :]).astype(np.float32)
    return onehot, np.broadcast_to(np.where(valid, 0.0, MASKED), (16, LINE)).astype(np.float32)


def blocks(w):
    k, n = w.shape
    return w.reshape(k // P, P, n).transpose(1, 0, 2).reshape(P, -1)


def columns(w, n):
    return [blocks(w[:, c:c + n]) for c in range(0, w.shape[1], n)]


def head_order():
    return [(2 * (u // 8) + u % 2) * 4 + (u // 2) % 4 for u in range(16)]


def pack_slabs(a):
    out = []
    w = a["mla_w_in"][0]
    w = np.concatenate([w, w[:, Q_RANK + KV_RANK:]], 1)
    out += columns(w, 256)
    uq, uk, uv = a["mla_w_uq"][0], a["mla_w_uk"][0], a["mla_w_uv"][0]
    for half in range(2):
        for p in range(2):
            h = 4 * half + 2 * p
            out.append(blocks(np.concatenate([uq[:, h, :128], uq[:, h + 1, :128], uq[:, h, 128:],
                                              uq[:, h + 1, 128:]], 1)))
        for m in (uk, uv):
            out.append(blocks(m[:, 4 * half:4 * half + 4].reshape(KV_RANK, 512)))
    out += columns(a["mla_w_o"][0], 256)

    def mlp(layer):
        for r in range(4):
            s = slice(D * r, D * (r + 1))
            out.extend(columns(a["mlp_w_up"][layer][:, s], 256))
            out.extend(columns(a["mlp_w_down"][layer][s], 256))

    mlp(0)
    order = head_order()
    kv = a["kv_w_shared"]
    q = a["swa_w_q"][0].reshape(D, 16, 64)[:, order].reshape(D, D)
    for half in range(2):
        for at in (0, 256):
            out.append(blocks(kv[:, at + 128 * half:at + 128 * half + 128]))
        out += columns(q[:, 512 * half:512 * (half + 1)], 256)
    out += columns(a["swa_w_o"][0].reshape(16, 64, D)[order].reshape(D, D), 256)
    mlp(1)
    zb, zc, zx, zq, zk, zv = np.split(a["w_in_2"][0], 6, 1)
    for i in range(2):
        s = slice(256 * i, 256 * (i + 1))
        out += [blocks(zc[:, s]), blocks(zx[:, s]), blocks(zb[:, s])]
    for half in range(2):
        s = slice(256 * half, 256 * (half + 1))
        out += [blocks(zq[:, s]), blocks(zk[:, s]), *columns(zv[:, s], 128)]
    out += columns(a["w_out_2"][0], 256)
    gate, up, down = a["w_gate_2"][0], a["w_up_2"][0], a["w_down_2"][0]
    for before, count in ((0, FF_A), (FF_A, FF_B)):
        for t in range(before, before + count):
            s = slice(P * t, P * (t + 1))
            out.append(blocks(np.concatenate([gate[:, s], up[:, s]], 1)))
        out += columns(down[P * before:P * (before + count)], P)
    out.append(blocks(a["w_ple_proj_2"][0]))
    out += columns(a["w_ple_gate_2"][0], 256)
    slabs = np.zeros((SLABS, P, SLAB), np.float32)
    assert len(out) == SLABS
    for g, w in enumerate(out):
        assert w.shape[1] == slab_width(g) or w.shape[1] == SLAB, (g, w.shape)
        slabs[g, :, :w.shape[1]] = w
    return slabs


def pack_vectors(a):
    def tiles(v):
        return v.reshape(-1, P).T

    parts = {"g_q": tiles(a["mla_g_q"][0]), "g_kv": tiles(a["mla_g_kv"][0]), "g_mix": tiles(a["g_mix_2"][0]),
             "conv_w": tiles(a["conv_w_2"][0]), "conv_b": tiles(a["conv_b_2"][0]),
             "qn_g": tiles(np.tile(a["q_norm_g_2"][0], 2)), "kn_g": tiles(np.tile(a["k_norm_g_2"][0], 2)),
             "g_oc": tiles(a["g_out_conv_2"][0]), "g_oa": tiles(a["g_out_attn_2"][0]),
             "g_ffn": tiles(a["g_ffn_2"][0]), "fconv_w": tiles(a["ffn_conv_w_2"][0]),
             "fconv_b": tiles(a["ffn_conv_b_2"][0]), "g_ple": tiles(a["g_ple_2"][0]),
             "sink": np.broadcast_to(a["swa_sinks"][0][head_order()], (P, 16))}
    for layer in range(2):
        for kind in ("mix", "mlp"):
            parts[f"{kind}_g{layer}"] = tiles(a[f"ln_{kind}_g"][layer])
            parts[f"{kind}_b{layer}"] = tiles(a[f"ln_{kind}_b"][layer])
    vecs = np.zeros((P, NVEC), np.float32)
    for name, part in parts.items():
        vecs[:, VEC[name]:VEC[name] + part.shape[1]] = part
    return vecs


def kernel(**inputs):
    import concourse.bacc as bacc
    from concourse.bass_utils import run_bass_kernel_spmd as run

    a = {name: np.asarray(value) for name, value in inputs.items()}
    onehot, line_mask = t5_tables()
    arrays = {
        "slabs": pack_slabs(a),
        "x_t": a["x"][0].T.reshape(KT, P, T).transpose(1, 0, 2),
        "ple_t": a["p_2"][0, 0].T.reshape(2, P, T).transpose(1, 0, 2),
        "vecs": pack_vectors(a),
        "rel_bias": a["rel_bias"][:, head_order()],
        "onehot": onehot,
        "line_mask": line_mask,
        "rope": rope_table(),
        "mats": matrices(),
        "causal": causal_table(),
        "dilated": dilated_table(),
    }
    arrays = {name: np.ascontiguousarray(value) for name, value in arrays.items()}
    nc = bacc.Bacc("TRN2", target_bir_lowering=False, num_devices=1)
    args = {name: nc.dram_tensor(name, value.shape, F32, kind="ExternalInput").ap()
            for name, value in arrays.items()}
    out = nc.dram_tensor("out", (P, KT, T), F32, kind="ExternalOutput").ap()
    program(nc, **args, out=out)
    result = run(nc, [arrays], core_ids=[0]).results[0]["out"]
    return np.ascontiguousarray(result.transpose(1, 0, 2).reshape(D, T).T).reshape(1, T, D)
```

```python
from contextlib import ExitStack

import numpy as np

import concourse.bass as bass
from concourse import mybir

ALU = mybir.AluOpType
ACT = mybir.ActivationFunctionType
F32 = mybir.dt.float32
F32R = mybir.dt.float32r

P = 128
T = 512
D = 1024
KT = D // P
BANK = 512
SLAB = 2048
ALPHA = float((2 * 2) ** 0.25)
LN_EPS, RMS_EPS = 1e-5, 1e-6
Q_RANK, KV_RANK = 384, 256
MLA_SCALE = float((128 + 64) ** -0.5)
HEAD_SCALE = 64.0 ** -0.5
MASKED = -1e30
HUGE = 3e38

MLA_IN = 0
MLA_HALF = 3
MLA_OUT = 11
MLP0 = 15
SWA_HALF = 47
SWA_OUT = 55
MLP1 = 59
CONV = 91
DIL_HALF = 97
MIX_OUT = 105
FFN_A, FFN_A_DOWN = 109, 121
FFN_B, FFN_B_DOWN = 129, 139
PLE_PROJ = 147
PLE_GATE = 148
SLABS = 152
FF_A, FF_B = 12, 10

NORM = {name: n + 1 for n, name in enumerate(
    ("mla", "ln0", "ln1", "ln2", "ln3", "mix", "conv", "q0", "k0", "q1", "k1", "attn", "ffn", "ple"))}
SUM_READY = {"mla_q": 1, "mla_kv": 2, "ln": 2, "conv": 11, "ffn": 12, "ple": 13}
SQUARED = {"mix": 20, "conv": 28, "dil": 30, "ffn": 38, "ple": 42}
RSTD = {"mix": 1, "attn": 2, "ffn": 3, "ple": 4}

X_IN, MLA_O, LN_0, LN_1, SWA_O, LN_2, LN_3, MIX_Y, FFN_X, PLE_X = range(0, 80, 8)


def slab_width(g):
    if MLA_HALF <= g < MLA_OUT:
        return (3 * 384, 3 * 384, 2 * 512, 2 * 512)[(g - MLA_HALF) % 4]
    if SWA_HALF <= g < SWA_OUT:
        return (KT * P, KT * P, SLAB, SLAB)[(g - SWA_HALF) % 4]
    if DIL_HALF <= g < MIX_OUT:
        return (SLAB, SLAB, KT * P, KT * P)[(g - DIL_HALF) % 4]
    if FFN_A_DOWN <= g < FFN_B:
        return FF_A * P
    if FFN_B_DOWN <= g < PLE_PROJ:
        return FF_B * P
    return SLAB


VEC = {}
NVEC = 0
for _name, _n in (("g_q", 3), ("g_kv", 2), ("mix_g0", 8), ("mix_b0", 8), ("mlp_g0", 8), ("mlp_b0", 8),
                  ("mix_g1", 8), ("mix_b1", 8), ("mlp_g1", 8), ("mlp_b1", 8), ("g_mix", 8),
                  ("conv_w", 12), ("conv_b", 4), ("qn_g", 1), ("kn_g", 1), ("g_oc", 4), ("g_oa", 4),
                  ("g_ffn", 8), ("fconv_w", 66), ("fconv_b", 22), ("g_ple", 8), ("sink", 16),
                  ):
    VEC[_name] = NVEC
    NVEC += _n
LINE = 384


class Heads:

    def __init__(self, band):
        first = [max(0, i - 1) if band else 0 for i in range(4)]
        self.key0 = [f * P for f in first]
        self.tiles = [list(range(first[i], i + 1)) for i in range(4)]
        self.width = [len(t) * P for t in self.tiles]
        self.off = [sum(self.width[:i]) for i in range(4)]
        self.total = sum(self.width)
        if band:
            self.place = [(0, 0), (0, 128), (1, 0), (1, 256)]
            keys = [(0, 0), (0, 256), (1, 0), (1, 256)]
            self.segments = [512, 384]
        else:
            self.place = [(0, 0), (1, 0), (0, 128), (2, 0)]
            keys = [(0, 0), (1, 0), (2, 0), (1, 384)]
            self.segments = [512, 512, 256]
        reach = 2 if band else 4
        self.keys = [(min(4 - j, reach), *keys[j]) for j in range(4)]
        self.groups = [[0, 1], [2, 3]] if band else [[0, 2], [1], [3]]
        self.order = [i for group in self.groups for i in group]

    def blocks(self, n):
        return [(j + k, j, c + k * P) for j, (reach, bank, c) in enumerate(self.keys) if bank == n
                for k in range(reach)]


CAUSAL, BAND = Heads(False), Heads(True)


def program(nc, slabs, x_t, ple_t, vecs, rel_bias, onehot, line_mask, rope, mats, causal, dilated, out):
    ctx = ExitStack()
    with ctx:
        def sem(name):
            return ctx.enter_context(nc.semaphore(name))

        def keep(name, shape, dt=F32):
            return ctx.enter_context(nc.sbuf_tensor(name, shape, dt))

        stage = [keep(f"stage{s}", [P, SLAB]) for s in range(2)]
        w_hi = [keep(f"w_hi{s}", [P, SLAB], F32R) for s in range(2)]
        w_lo = [keep(f"w_lo{s}", [P, SLAB], F32R) for s in range(2)]
        act_hi = keep("act_hi", [P, KT, T], F32R)
        act_lo = keep("act_lo", [P, KT, T], F32R)
        y = keep("y", [P, KT, T])
        tmp = keep("tmp", [P, 2, 2, T])
        vec = keep("vec", [P, NVEC])
        mat = keep("mat", [P, 4, P])
        ident, ones, ones64, swap = (mat[:, i, :] for i in range(4))
        eps = keep("eps", [P, 2])
        sum1 = keep("sum1", [P, T])
        sum2 = keep("sum2", [P, T])
        rstd = keep("rstd", [P, T])
        stat = keep("stat", [P, T])
        tok_v, tok_s, tok_r, tok_q = (keep(f"tok_{x}", [P, 16]) for x in "vsrq")
        rstd_tok = keep("rstd_tok", [P, 4])
        table_mark = keep("table_mark", [P, 1])
        mark = keep("mark", [P, 1])
        negmax = keep("negmax", [P, 4 * 16])
        rowsum = keep("rowsum", [P, 4 * 16])
        sinkexp = keep("sinkexp", [P, 4 * 16])
        rden = keep("rden", [P, 4 * 16])
        negsink = keep("negsink", [P, 16])
        ps = ctx.enter_context(nc.psum_tensor("ps", [P, 8, BANK], F32))

        floors = [0]

        def part(floor, *specs):
            made = []
            with ExitStack() as shared:
                if floor:
                    floors[0] += 1
                    shared.enter_context(nc.sbuf_tensor(f"floor{floors[0]}", [P, floor], F32))
                for name, shape, dt in specs:
                    made.append(shared.enter_context(nc.sbuf_tensor(name, shape, dt)))
                    floor += int(np.prod(shape[1:]))
            return (*made, floor)

        (qr_hi, qr_lo, kn_hi, kn_lo, kr_hi, kr_lo, mv_hi, mv_lo, c_hi, c_lo, cossin, strip, top) = part(
            0, ("qr_hi", [P, 2, T], F32R), ("qr_lo", [P, 2, T], F32R), ("kn_hi", [P, 4, T], F32R),
            ("kn_lo", [P, 4, T], F32R), ("kr_hi", [P, T], F32R), ("kr_lo", [P, T], F32R),
            ("mv_hi", [P, 4, T], F32R), ("mv_lo", [P, 4, T], F32R), ("c_hi", [P, 5, T], F32R),
            ("c_lo", [P, 5, T], F32R), ("cossin", [P, 2, T], F32), ("strip", [P, T], F32))
        c_raw, rope_raw, rope_cos, rope_sin, _ = part(
            top, ("c_raw", [P, 5, T], F32), ("rope_raw", [P, T], F32), ("rope_cos", [P, T], F32),
            ("rope_sin", [P, T], F32))
        m_prob, m_pt_hi, m_pt_lo, _ = part(
            top, ("m_prob", [P, 2, CAUSAL.total], F32), ("m_pt_hi", [P, CAUSAL.total], F32R),
            ("m_pt_lo", [P, CAUSAL.total], F32R))
        hid_hi, hid_lo, relu, top = part(
            0, ("hid_hi", [P, KT, T], F32R), ("hid_lo", [P, KT, T], F32R), ("relu", [P, 2, 2, T], F32))
        strips, top_strips = part(top, ("strips", [P, SLAB], F32))
        o_hi, o_lo, gap = part(0, ("o_hi", [P, KT, T], F32R), ("o_lo", [P, KT, T], F32R))
        swa_k_hi, swa_k_lo, _ = part(gap, ("swa_k_hi", [P, T], F32R), ("swa_k_lo", [P, T], F32R))
        dv_hi, dv_lo, top = part(gap, ("dv_hi", [P, 2, T], F32R), ("dv_lo", [P, 2, T], F32R))
        assert top <= top_strips - SLAB
        (sq_hi, sq_lo, va_hi, va_lo, vb_hi, vb_lo, s_prob, s_pt_hi, s_pt_lo, _) = part(
            top_strips, ("sq_hi", [P, 4, T], F32R), ("sq_lo", [P, 4, T], F32R), ("va_hi", [P, 4, P], F32R),
            ("va_lo", [P, 4, P], F32R), ("vb_hi", [P, 4, P], F32R), ("vb_lo", [P, 4, P], F32R),
            ("s_prob", [P, 2, BAND.total], F32), ("s_pt_hi", [P, BAND.total], F32R),
            ("s_pt_lo", [P, BAND.total], F32R))
        dq_hi, dq_lo, dk_hi, dk_lo, top = part(
            top_strips, ("dq_hi", [P, 2, T], F32R), ("dq_lo", [P, 2, T], F32R), ("dk_hi", [P, 2, T], F32R),
            ("dk_lo", [P, 2, T], F32R))
        zc, u_pad, conv, yc, _ = part(
            top, ("zc", [P, 2, T], F32), ("u_pad", [P, 2, T + 2], F32), ("conv", [P, 2, T], F32),
            ("yc", [P, 4, T], F32))
        d_prob, d_pt_hi, d_pt_lo, k_raw, _ = part(
            top, ("d_prob", [P, 2, CAUSAL.total], F32), ("d_pt_hi", [P, CAUSAL.total], F32R),
            ("d_pt_lo", [P, CAUSAL.total], F32R), ("k_raw", [P, 2, T], F32))
        h_hi, h_lo, top = part(0, ("h_hi", [P, FF_A, T], F32R), ("h_lo", [P, FF_A, T], F32R))
        gate, gconv, silu, ffh, top = part(
            top, ("gate", [P, 2, T + 2], F32), ("gconv", [P, 2, T], F32), ("silu", [P, 2, T], F32),
            ("ffh", [P, 2, T], F32))
        p_raw, p_hi, p_lo, _ = part(top, ("p_raw", [P, 2, T], F32), ("p_hi", [P, 2, T], F32R),
                                    ("p_lo", [P, 2, T], F32R))
        proj, gate_in, _ = part(0, ("proj", [P, KT, T], F32), ("gate_in", [P, 2, 2, T], F32))
        bias_line = nc.dram_tensor("bias_line", (16, LINE), F32, kind="Internal").ap()
        bias_rows = nc.dram_tensor("bias_rows", (16, P, LINE), F32, kind="Internal").ap()

        landed = [sem(f"landed{s}") for s in range(2)]
        cast_hi, cast_lo = sem("cast_hi"), sem("cast_lo")
        slab_done = sem("slab_done")
        slab_read = sem("slab_read")
        act_ready = sem("act_ready")
        x_landed = [sem(f"x_landed{i}") for i in range(4)]
        x_hi, x_scaled = sem("x_hi"), sem("x_scaled")
        const_landed, p_landed = sem("const_landed"), sem("p_landed")
        eps_set = sem("eps_set")
        act_link, dve_link = sem("act_link"), sem("dve_link")
        sq_done = sem("sq_done")
        sum_ready, mean_done, mean_ready = sem("sum_ready"), sem("mean_done"), sem("mean_ready")
        half_done, tile_added, centred = sem("half_done"), sem("tile_added"), sem("centred")
        pool_cast = sem("pool_cast")
        tok_sums, var_ready, std_ready = sem("tok_sums"), sem("var_ready"), sem("std_ready")
        tok_ready, spread_done, rstd_ready = sem("tok_ready"), sem("spread_done"), sem("rstd_ready")
        norm_z, norm_hi = sem("norm_z"), sem("norm_hi")
        c_read, c_full, c_split, c_ready = sem("c_read"), sem("c_full"), sem("c_split"), sem("c_ready")
        rope_in, rope_swapped, rope_out, rope_hi, rope_lo = (
            sem("rope_in"), sem("rope_swapped"), sem("rope_out"), sem("rope_hi"), sem("rope_lo"))
        proj_hi = sem("proj_hi")
        relu_done, sqr_done, hid_split = sem("relu_done"), sem("sqr_done"), sem("hid_split")
        line_done, line_ready, line_stored, rows_stored = (sem("line_done"), sem("line_ready"),
                                                           sem("line_stored"), sem("rows_stored"))
        strips_landed = sem("strips_landed")
        v_zeroed, u_zeroed = sem("v_zeroed"), sem("u_zeroed")
        qk_sq, qk_full = sem("qk_sq"), sem("qk_full")
        dil_ready = sem("dil_ready")
        mix_sq, mix_hi = sem("mix_sq"), sem("mix_hi")
        conv_done, silu_done, ffh_done, ffh_hi = sem("conv_done"), sem("silu_done"), sem("ffh_done"), sem("ffh_hi")
        ff_step, h_ready = sem("ff_step"), sem("h_ready")
        p_split, proj_act, sig_done, out_ready, stored = (sem("p_split"), sem("proj_act"), sem("sig_done"),
                                                          sem("out_ready"), sem("stored"))

        class Attention:

            def __init__(self, name, heads, score_banks, trans_bank, ahead):
                self.h, self.score_banks, self.trans_bank, self.ahead = heads, score_banks, trans_bank, ahead
                self.scored = sem(name + "_scored")
                self.biased = sem(name + "_biased")
                self.exped = sem(name + "_exped")
                self.summed = sem(name + "_summed")
                self.normed = sem(name + "_normed")
                self.turned = sem(name + "_turned")
                self.turn_hi = sem(name + "_turn_hi")
                self.turn_lo = sem(name + "_turn_lo")
                self.mixed = sem(name + "_mixed")
                self.out_hi = sem(name + "_out_hi")
                self.out_read = sem(name + "_out_read")
                self.nseg = len(heads.segments)

        mla = Attention("mla", CAUSAL, [0, 0], 3, 1)
        swa = Attention("swa", BAND, [0, 2], 4, 2)
        dil = Attention("dil", CAUSAL, [0, 0], 3, 1)

        def col(name, i=0):
            at = VEC[name] + i
            return vec[:, at:at + 1]

        def f32(ap):
            return ap.bitcast(F32)

        def pair(ap2d):
            return ap2d.unsqueeze(1).broadcast_to([P, 2, T])

        def banks(g):
            return 2 * (g % 2)

        block = ctx.enter_context(nc.Block())

        @block.sync
        def _(sp):
            for s in range(2):
                sp.dma_start(stage[s][:, :], slabs[s]).then_inc(landed[s], 16)
            with sp.Fori(1, SLABS // 2) as n:
                for s in range(2):
                    sp.wait_ge(cast_lo, n * 2 + (s - 1))
                    sp.dma_start(stage[s][:, :], slabs[bass.ds(n * 2 + s, 1)].rearrange("a p w -> p (a w)"))\
                      .then_inc(landed[s], 16)

        @block.gpsimd
        def _(pool):
            nc.gpsimd.memset(eps[:, 0:1], LN_EPS).then_inc(eps_set, 1)
            nc.gpsimd.memset(eps[:, 1:2], RMS_EPS).then_inc(eps_set, 1)
            for p in range(4):
                pool.wait_ge(act_ready, X_IN + 2 * p + 2)
                nc.gpsimd.tensor_scalar(y[:, 2 * p:2 * p + 2, :], y[:, 2 * p:2 * p + 2, :], ALPHA, None,
                                        ALU.mult).then_inc(x_scaled, 1)

            def divide(a, prob, u):
                h = a.h
                for k, i in enumerate(h.order):
                    pool.wait_ge(a.summed, 4 * u + k + 1)
                    n = 4 * (u % 16) + i
                    part = prob[:, u % 2, h.off[i]:h.off[i] + h.width[i]]
                    nc.gpsimd.tensor_scalar(part, part, rden[:, n:n + 1], None, ALU.mult).then_inc(a.normed, 1)

            def residual(gen, beta):
                for t in range(KT):
                    pool.wait_ge(act_ready, gen + t + 1)
                    nc.gpsimd.tensor_scalar(y[:, t, :], y[:, t, :], col(beta, t), ALPHA, ALU.add, ALU.mult)\
                        .then_inc(x_scaled, 1)

            def norm_share(n, g):
                pool.wait_ge(mean_ready, n + 1)
                pool.wait_ge(slab_read, g - 1)
                nc.gpsimd.tensor_tensor(y[:, 6:8, :], y[:, 6:8, :], pair(stat[:, :]), ALU.subtract)\
                    .then_inc(centred, 1)
                if n == 3:
                    for t in range(4):
                        mix_square(t)
                s = g % 2
                pool.wait_ge(cast_hi, g + 1)
                nc.gpsimd.tensor_tensor(w_lo[s][:, :], stage[s][:, :], f32(w_hi[s][:, :]), ALU.subtract)\
                    .then_inc(pool_cast, 1)

            def mix_square(t):
                pool.wait_ge(sq_done, SQUARED["mix"] + t + 1)
                if t == 0:
                    pool.wait_ge(tok_ready, NORM["ln3"])
                    nc.gpsimd.tensor_copy(sum2[:, :], tmp[:, 0, 0, :]).then_inc(mix_sq, 1)
                else:
                    pool.wait_ge(mix_sq, t)
                    nc.gpsimd.tensor_tensor(sum2[:, :], sum2[:, :], tmp[:, t // 2 % 2, t % 2, :], ALU.add)\
                        .then_inc(mix_sq, 1)

            for u in range(8):
                divide(mla, m_prob, u)
            norm_share(0, MLP0 + 1)
            residual(LN_0, "mix_b0")
            norm_share(1, SWA_HALF + 1)
            residual(LN_1, "mlp_b0")
            pool.wait_ge(act_ready, LN_1 + 1)
            for v in (va_hi, va_lo, vb_hi, vb_lo):
                nc.gpsimd.memset(v[:, :, :].bitcast(F32), 0.0).then_inc(v_zeroed, 1)
            for u in range(16):
                divide(swa, s_prob, u)
            norm_share(2, MLP1 + 1)
            residual(LN_2, "mix_b1")
            norm_share(3, CONV + 1)
            for t in range(4, KT):
                mix_square(t)
            pool.wait_ge(act_ready, LN_3 + 1)
            nc.gpsimd.memset(u_pad[:, :, 0:2], 0.0).then_inc(u_zeroed, 1)
            for u in range(8):
                divide(dil, d_prob, u)
            pool.wait_ge(act_ready, FFN_X + 1)
            nc.gpsimd.memset(gate[:, :, 0:2], 0.0).then_inc(u_zeroed, 1)

        @block.scalar
        def _(act):
            links = [0]

            def link(ins):
                links[0] += 1
                ins.then_inc(act_link, 1)
                act.wait_ge(act_link, links[0])

            def cast(g, more=0, width=None):
                if g >= SLABS:
                    return
                s, w = g % 2, width or slab_width(g)
                act.wait_ge(landed[s], 16 * (g // 2 + 1) + more * 8)
                if g >= 2:
                    act.wait_ge(slab_done, g - 1 + more)
                nc.scalar.activation(w_hi[s][:, 0:w], stage[s][:, 0:w], ACT.Copy).then_inc(cast_hi, 1)

            def root(name, width=4):
                act.wait_ge(var_ready, NORM[name])
                nc.scalar.activation(tok_s[:, 0:width], tok_v[:, 0:width], ACT.Sqrt).then_inc(std_ready, 1)

            def rstd_copy(name, dst, bank):
                act.wait_ge(spread_done, NORM[name])
                nc.scalar.activation(dst[:, :], ps[:, bank, :], ACT.Copy).then_inc(rstd_ready, 1)

            def load_table(func):
                link(nc.scalar.activation(table_mark[:, :], eps[:, 0:1], func))

            def exps(a, prob, u, sink=None):
                h = a.h
                for k, i in enumerate(h.order):
                    n = 4 * (u % 16) + i
                    act.wait_ge(a.biased, 4 * u + k + 1)
                    part = prob[:, u % 2, h.off[i]:h.off[i] + h.width[i]]
                    nc.scalar.activation(part, part, ACT.Exp, scale=-1.0, bias=negmax[:, n:n + 1],
                                         accum_out=rowsum[:, n:n + 1]).then_inc(a.exped, 1)
                if sink is not None:
                    n = 4 * (u % 16)
                    nc.scalar.activation(sinkexp[:, n:n + 4], negmax[:, n:n + 4], ACT.Exp, bias=sink)\
                        .then_inc(a.exped, 1)

            def turn_hi(a, pt_hi, u):
                for n, w in enumerate(a.h.segments):
                    act.wait_ge(a.turned, a.nseg * u + n + 1)
                    if n == 0 and a is not swa and u:
                        act.wait_ge(a.mixed, u)
                    nc.scalar.activation(pt_hi[:, BANK * n:BANK * n + w], ps[:, a.trans_bank + n, 0:w],
                                         ACT.Copy).then_inc(a.turn_hi, 1)



            for p in range(4):
                act.dma_start(y[:, 2 * p:2 * p + 2, :], x_t[:, 2 * p:2 * p + 2, :]).then_inc(x_landed[p], 16)
            act.dma_start(vec[:, :], vecs).then_inc(const_landed, 16)
            act.dma_start(mat[:, :, :], mats).then_inc(const_landed, 16)
            act.dma_start(cossin[:, :, :], rope).then_inc(const_landed, 16)
            act.dma_start(strip[:, :], causal).then_inc(const_landed, 16)
            act.dma_start(stat[0:32, 0:16], rel_bias).then_inc(const_landed, 16)
            act.dma_start(sum2[0:32, 0:LINE], onehot).then_inc(const_landed, 16)
            act.dma_start(sum1[0:16, 0:LINE], line_mask).then_inc(const_landed, 16)
            for p in range(4):
                act.wait_ge(x_landed[p], 16)
                nc.scalar.activation(act_hi[:, 2 * p:2 * p + 2, :], y[:, 2 * p:2 * p + 2, :], ACT.Copy)\
                    .then_inc(x_hi, 1)
                if p < 2:
                    cast(p)
            act.wait_ge(line_ready, 1)
            act.dma_start(bias_line, rstd[0:16, 0:LINE]).then_inc(line_stored, 16)
            act.wait_ge(line_stored, 16)
            act.dma_start(bias_rows, bias_line.unsqueeze(1).broadcast_to([16, P, LINE])).then_inc(rows_stored, 16)

            act.wait_ge(const_landed, 16 * 7)
            act.wait_ge(eps_set, 2)
            for j in range(3):
                g = MLA_IN + j
                b = banks(g)
                act.wait_ge(slab_done, g + 1)
                if j < 2:
                    nc.scalar.activation(c_raw[:, 2 * j:2 * j + 2, :], ps[:, b:b + 2, :], ACT.Copy)
                    nc.scalar.activation(tmp[:, j, :, :], ps[:, b:b + 2, :], ACT.Square).then_inc(c_read, 1)
                else:
                    act.wait_ge(c_split, 1)
                    nc.scalar.activation(rope_raw[:, :], ps[:, b + 1, :], ACT.Copy).then_inc(rope_in, 1)
                    nc.scalar.activation(c_raw[:, 4, :], ps[:, b, :], ACT.Copy)
                    nc.scalar.activation(tmp[:, 0, 0, :], ps[:, b, :], ACT.Square).then_inc(c_read, 1)
                cast(g + 2)
            root("mla", 8)
            for t in range(5):
                act.wait_ge(c_full, t + 1)
                nc.scalar.activation(c_hi[:, t, :], c_raw[:, t, :], ACT.Copy).then_inc(c_split, 1)
            act.wait_ge(rope_out, 1)
            nc.scalar.activation(kr_hi[:, :], rope_cos[:, :], ACT.Copy).then_inc(rope_hi, 1)

            for half in range(2):
                g = MLA_HALF + 4 * half
                for p in range(2):
                    b = 4 * p
                    act.wait_ge(slab_done, g + p + 1)
                    n = 1 + 2 * half + p
                    act.wait_ge(rope_out, n)
                    nc.scalar.activation(rope_raw[:, :], ps[:, b + 2, :], ACT.Copy, scale=MLA_SCALE)\
                        .then_inc(rope_in, 1)
                    nc.scalar.activation(act_hi[:, 4 + 2 * p:6 + 2 * p, :], ps[:, b:b + 2, :], ACT.Copy,
                                         scale=MLA_SCALE).then_inc(proj_hi, 1)
                    cast(g + p + 2)
                    act.wait_ge(rope_out, n + 1)
                    nc.scalar.activation(qr_hi[:, p, :], rope_cos[:, :], ACT.Copy).then_inc(rope_hi, 1)
                for p, dst in ((2, kn_hi), (3, mv_hi)):
                    b = 4 * (p - 2)
                    act.wait_ge(slab_done, g + p + 1)
                    for q in range(2):
                        nc.scalar.activation(dst[:, 2 * q:2 * q + 2, :], ps[:, b + 2 * q:b + 2 * q + 2, :],
                                             ACT.Copy).then_inc(proj_hi, 1)
                    cast(g + p + 2)
                def mla_out(u):
                    act.wait_ge(mla.mixed, u + 1)
                    nc.scalar.activation(act_hi[:, u, :], ps[:, 6 + u % 2, :], ACT.Copy).then_inc(mla.out_hi, 1)

                u0 = 4 * half
                exps(mla, m_prob, u0)
                for u in range(u0, u0 + 4):
                    if u < u0 + 3:
                        exps(mla, m_prob, u + 1)
                    turn_hi(mla, m_pt_hi, u)
                    if u > u0:
                        mla_out(u - 1)
                mla_out(u0 + 3)

            def load_bias(half):
                act.dma_start(strips[:, :].rearrange("p (h j) -> p h j", h=8),
                              bass.AP(bias_rows.tensor, 8 * half * P * LINE + P - 1,
                                      [[LINE - 1, P], [P * LINE, 8], [1, 2 * P]])).then_inc(strips_landed, 16)

            def last_squares(first, n):
                for j in range(3):
                    act.wait_ge(slab_read, first + j + 1)
                    nc.scalar.activation(tmp[:, j % 2, :, :], y[:, 2 * j:2 * j + 2, :], ACT.Square)\
                        .then_inc(sq_done, 1)
                    cast(first + j + 2)
                load_table(ACT.Sqrt)
                act.wait_ge(tile_added, n + 1)
                nc.scalar.activation(tmp[:, 1, 0, :], y[:, 6, :], ACT.Square).then_inc(sq_done, 1)
                act.wait_ge(slab_read, first + 4)
                nc.scalar.activation(tmp[:, 1, 1, :], y[:, 7, :], ACT.Square).then_inc(sq_done, 1)
                act.wait_ge(mean_done, n + 1)
                nc.scalar.activation(stat[:, :], ps[:, 4, :], ACT.Copy).then_inc(mean_ready, 1)
                root(f"ln{n}")
                cast(first + 5)

            def layer_norm(n, beta):
                for t in range(KT):
                    act.wait_ge(norm_z, 8 * n + t + 1)
                    nc.scalar.activation(act_hi[:, t, :], y[:, t, :], ACT.Identity, bias=col(beta, t))\
                        .then_inc(norm_hi, 1)

            def mlp(first, layer):
                def up(j, more, done):
                    g = first + j
                    b = banks(g)
                    act.wait_ge(slab_done, g + 1 + more)
                    act.wait_ge(slab_read, g - 1 + more)
                    nc.scalar.activation(relu[:, j % 2, :, :], ps[:, b:b + 2, :], ACT.Relu).then_inc(relu_done, 1)
                    act.wait_ge(sqr_done, done + j + 1)
                    nc.scalar.activation(hid_hi[:, 2 * j:2 * j + 2, :], relu[:, j % 2, :, :], ACT.Copy)\
                        .then_inc(hid_split, 1)
                    cast(g + 2, more)

                with act.Fori(0, 3) as r:
                    for j in range(4):
                        up(j, r * 8, r * 4 + 16 * layer)
                    for j in range(4, 8):
                        cast(first + j + 2, r * 8)
                for j in range(4):
                    up(j, 24, 12 + 16 * layer)
                last_squares(first + 28, 2 * layer + 1)

            last_squares(MLA_OUT, 0)
            layer_norm(0, "mix_b0")
            act.wait_ge(rows_stored, 16)
            load_bias(0)
            mlp(MLP0, 0)
            layer_norm(1, "mlp_b0")

            for half in range(2):
                g = SWA_HALF + 4 * half
                if half:
                    act.wait_ge(swa.biased, 32)
                    load_bias(1)
                act.wait_ge(slab_done, g + 1)
                nc.scalar.activation(swa_k_hi[:, :], ps[:, banks(g), :], ACT.Copy).then_inc(proj_hi, 1)
                cast(g + 2)
                act.wait_ge(slab_done, g + 2)
                act.wait_ge(v_zeroed, 4)
                for v_hi, c in ((va_hi, 0), (vb_hi, 64)):
                    nc.scalar.activation(v_hi[:, :, c:c + 64],
                                         ps[:, banks(g + 1), :].rearrange("p (i c) -> p i c", i=4)[:, :, c:c + 64],
                                         ACT.Copy).then_inc(proj_hi, 1)
                cast(g + 3)
                for p in range(2):
                    b = banks(g + 2 + p)
                    act.wait_ge(slab_done, g + 3 + p)
                    nc.scalar.activation(sq_hi[:, 2 * p:2 * p + 2, :], ps[:, b:b + 2, :], ACT.Copy,
                                         scale=HEAD_SCALE).then_inc(proj_hi, 1)
                    cast(g + 4 + p)
                u0 = 8 * half
                for u in (u0, u0 + 1):
                    exps(swa, s_prob, u, col("sink", u))
                for u in range(u0, u0 + 8):
                    turn_hi(swa, s_pt_hi, u)
                    if u + 2 < u0 + 8:
                        exps(swa, s_prob, u + 2, col("sink", u + 2))
                    if u % 2:
                        act.wait_ge(swa.mixed, u // 2 + 1)
                        nc.scalar.activation(o_hi[:, u // 2, :], ps[:, 6 + (u // 2) % 2, :], ACT.Copy)\
                            .then_inc(swa.out_hi, 1)

            act.wait_ge(swa.biased, 64)
            act.dma_start(strips[:, :], dilated[0]).then_inc(strips_landed, 16)
            last_squares(SWA_OUT, 2)
            layer_norm(2, "mix_b1")
            mlp(MLP1, 1)

            for t in range(KT):
                act.wait_ge(norm_z, 24 + t + 1)
                link(nc.scalar.activation(y[:, t, :], y[:, t, :], ACT.Identity, bias=col("mlp_b1", t)))
                nc.scalar.activation(act_hi[:, t, :], y[:, t, :], ACT.Copy, scale=col("g_mix", t))\
                    .then_inc(norm_hi, 1)
                if t >= 4:
                    act.wait_ge(mix_sq, t - 3)
                nc.scalar.activation(tmp[:, t // 2 % 2, t % 2, :], y[:, t, :], ACT.Square).then_inc(sq_done, 1)

            root("mix")
            rstd_copy("mix", rstd, 6)
            for i in range(2):
                for j in range(3):
                    cast(CONV + 3 * i + j + 2)
                act.wait_ge(conv_done, i + 1)
                nc.scalar.activation(tmp[:, 1, :, :], yc[:, 2 * i:2 * i + 2, :], ACT.Square).then_inc(sq_done, 1)
            root("conv")
            for t in range(4):
                act.wait_ge(conv_done, 2 + t + 1)
                nc.scalar.activation(o_hi[:, t, :], yc[:, t, :], ACT.Copy).then_inc(mix_hi, 1)

            for half in range(2):
                g = DIL_HALF + 4 * half
                if half:
                    act.wait_ge(dil.biased, 16)
                    act.dma_start(strips[:, :], dilated[1]).then_inc(strips_landed, 16)
                for p, (dst, raw, scale) in enumerate(((dq_hi, tmp[:, 0, :, :], HEAD_SCALE),
                                                       (dk_hi, k_raw[:, :, :], 1.0))):
                    n = 2 * half + p
                    act.wait_ge(slab_read, g + p + 1)
                    nc.scalar.activation(tmp[:, 1, :, :], raw, ACT.Square).then_inc(qk_sq, 1)
                    cast(g + p + 2)
                    root("qk"[p] + str(half), 16)
                    act.wait_ge(qk_full, n + 1)
                    nc.scalar.activation(dst[:, :, :], raw, ACT.Copy, scale=scale).then_inc(proj_hi, 1)
                load_table(ACT.Exp)
                for p in range(2):
                    act.wait_ge(slab_read, g + p + 3)
                    nc.scalar.activation(dv_hi[:, p, :], tmp[:, 0, p, :], ACT.Copy).then_inc(proj_hi, 1)
                    cast(g + p + 4)
                u0 = 4 * half

                def dil_out(u):
                    r, t = 64 * (u % 2), u // 2
                    act.wait_ge(dil.mixed, u + 1)
                    nc.scalar.activation(o_hi[r:r + 64, 4 + t, :], ps[r:r + 64, 6 + u % 2, :], ACT.Copy,
                                         scale=vec[r:r + 64, VEC["g_oa"] + t:VEC["g_oa"] + t + 1])\
                        .then_inc(dil.out_hi, 1)
                    if t >= 1:
                        act.wait_ge(mix_sq, 8 + t)
                    nc.scalar.activation(stat[r:r + 64, :], ps[r:r + 64, 6 + u % 2, :], ACT.Square)\
                        .then_inc(sq_done, 1)

                exps(dil, d_prob, u0)
                for u in range(u0, u0 + 4):
                    if u + 1 < u0 + 4:
                        exps(dil, d_prob, u + 1)
                    turn_hi(dil, d_pt_hi, u)
                    if u > u0:
                        dil_out(u - 1)
                dil_out(u0 + 3)

            def rms_out(g, tiles, n, gain):
                act.wait_ge(slab_read, g + 1)
                for t in tiles:
                    nc.scalar.activation(act_hi[:, t, :], y[:, t, :], ACT.Copy, scale=col(gain, t))\
                        .then_inc(mix_hi, 1)
                nc.scalar.activation(tmp[:, n % 2, 0:len(tiles), :], y[:, tiles[0]:tiles[-1] + 1, :],
                                     ACT.Square).then_inc(sq_done, 1)

            root("attn")
            rstd_copy("attn", stat, 0)
            for j in range(4):
                rms_out(MIX_OUT + j, [2 * j, 2 * j + 1], j, "g_ffn")
                cast(MIX_OUT + j + 2)

            root("ffn")
            load_table(ACT.Silu)
            rstd_copy("ffn", rstd, 7)
            for rnd, (first, down, before, count) in enumerate(((FFN_A, FFN_A_DOWN, 0, FF_A),
                                                                (FFN_B, FFN_B_DOWN, FF_A, FF_B))):
                with act.Fori(0, count // 2) as i:
                    for b in range(2):
                        act.wait_ge(conv_done, 6 + before + b + 1 + i * 2)
                        nc.scalar.activation(silu[:, b, :], gconv[:, b, :], ACT.Silu).then_inc(silu_done, 1)
                        cast(first + b + 2, i * 2, SLAB)
                        act.wait_ge(ffh_done, before + b + 1 + i * 2)
                        nc.scalar.activation(h_hi[:, bass.ds(i * 2 + b, 1), :], ffh[:, b:b + 1, :], ACT.Copy)\
                            .then_inc(ffh_hi, 1)
                if rnd == 0:
                    for j in range(8):
                        cast(down + j + 2)
            load_table(ACT.Sqrt)
            for j in range(8):
                rms_out(FFN_B_DOWN + j, [j], j, "g_ple")
                cast(FFN_B_DOWN + j + 2)

            act.dma_start(p_raw[:, :, :], ple_t).then_inc(p_landed, 16)
            act.wait_ge(p_landed, 16)
            nc.scalar.activation(p_hi[:, :, :], p_raw[:, :, :], ACT.Copy).then_inc(p_split, 1)
            act.wait_ge(slab_done, PLE_PROJ + 1)
            for q in range(2):
                last = nc.scalar.activation(proj[:, 2 * q:2 * q + 2, :], ps[:, 2 * q:2 * q + 2, :], ACT.Copy)
            last.then_inc(proj_act, 1)
            cast(PLE_PROJ + 2)
            root("ple")
            load_table(ACT.Sigmoid)
            rstd_copy("ple", rstd, 7)
            for j in range(4):
                act.wait_ge(slab_read, PLE_GATE + j + 1)
                nc.scalar.activation(gate_in[:, j % 2, :, :], gate_in[:, j % 2, :, :], ACT.Sigmoid)\
                    .then_inc(sig_done, 1)
                cast(PLE_GATE + j + 2)
                act.wait_ge(out_ready, j + 1)
                act.dma_start(out[:, 2 * j:2 * j + 2, :], y[:, 2 * j:2 * j + 2, :]).then_inc(stored, 16)
            act.wait_ge(stored, 16 * 4)
            act.wait_ge(rows_stored, 16)


        @block.vector
        def _(dve):
            links = [0]

            def link(ins):
                links[0] += 1
                ins.then_inc(dve_link, 1)
                dve.wait_ge(dve_link, links[0])

            def split(dst, src, hi):
                return nc.vector.tensor_tensor(dst, src, f32(hi), ALU.subtract)

            def split_scaled(dst, src, scale, hi, op=ALU.mult):
                return nc.vector.scalar_tensor_tensor(dst, src, scale, f32(hi), op, ALU.subtract)

            def cast(g, more=0, width=None):
                if g >= SLABS:
                    return
                s, w = g % 2, width or slab_width(g)
                dve.wait_ge(cast_hi, g + 1 + more)
                split(w_lo[s][:, 0:w], stage[s][:, 0:w], w_hi[s][:, 0:w]).then_inc(cast_lo, 1)

            def mean_squares(name, bank, scale, width=4):
                dve.wait_ge(tok_sums, NORM[name])
                nc.vector.tensor_scalar(tok_v[:, 0:width], ps[:, bank, 0:width], float(scale), RMS_EPS, ALU.mult,
                                        ALU.add).then_inc(var_ready, 1)

            def invert_root(name, width=4):
                v, s, r, q = (x[:, 0:width] for x in (tok_v, tok_s, tok_r, tok_q))
                dve.wait_ge(std_ready, NORM[name])
                if name in ("mix", "attn", "ffn", "ple"):
                    dve.wait_ge(spread_done, NORM[name] - 1)
                link(nc.vector.reciprocal(r, s))
                link(nc.vector.scalar_tensor_tensor(q, r, -0.5, r, ALU.mult, ALU.mult))
                link(nc.vector.tensor_tensor(q, q, v, ALU.mult))
                nc.vector.scalar_tensor_tensor(r, q, 1.5, r, ALU.add, ALU.mult).then_inc(tok_ready, 1)

            def bias(a, prob, u, table, floor=None):
                h, at = a.h, a.score_banks[u % 2]
                if u >= 2:
                    dve.wait_ge(a.turned, a.nseg * (u - 1))
                k = 0
                for m, group in enumerate(h.groups):
                    dve.wait_ge(a.scored, len(h.groups) * u + m + 1)
                    for i in group:
                        bank, c = h.place[i]
                        w, n = h.width[i], 4 * (u % 16) + i
                        nc.vector.tensor_tensor_reduce(
                            prob[:, u % 2, h.off[i]:h.off[i] + w], ps[:, at + bank, c:c + w], table(w),
                            -1.0, HUGE if floor is None else floor, ALU.add, ALU.min,
                            negmax[:, n:n + 1]).then_inc(a.biased, 1)
                        k += 1

            def invert(a, u, sink=False):
                n = 4 * (u % 16)
                if sink:
                    dve.wait_ge(a.exped, 5 * u + 5)
                    link(nc.vector.tensor_tensor(rowsum[:, n:n + 4], rowsum[:, n:n + 4], sinkexp[:, n:n + 4],
                                                 ALU.add))
                    nc.vector.reciprocal(rden[:, n:n + 4], rowsum[:, n:n + 4]).then_inc(a.summed, 4)
                    return
                for k, i in enumerate(a.h.order):
                    dve.wait_ge(a.exped, 4 * u + k + 1)
                    nc.vector.reciprocal(rden[:, n + i:n + i + 1], rowsum[:, n + i:n + i + 1])\
                        .then_inc(a.summed, 1)

            def turn_lo(a, pt_hi, pt_lo, u):
                for n, w in enumerate(a.h.segments):
                    dve.wait_ge(a.turn_hi, a.nseg * u + n + 1)
                    split(pt_lo[:, BANK * n:BANK * n + w], ps[:, a.trans_bank + n, 0:w],
                          pt_hi[:, BANK * n:BANK * n + w]).then_inc(a.turn_lo, 1)

            def sums(tiles, squares, squared, first, last, with_mean):
                for dst, parts, wait in ((sum1, [y[:, t, :] for t in tiles], False), (sum2, squares, True)):
                    if dst is sum1 and not with_mean:
                        continue
                    if wait:
                        dve.wait_ge(sq_done, squared)
                    if first and len(parts) == 2:
                        ins = nc.vector.tensor_tensor(dst[:, :], parts[0], parts[1], ALU.add)
                        parts = []
                    elif first:
                        ins = nc.vector.tensor_copy(dst[:, :], parts[0])
                        parts = []
                    for k, part in enumerate(parts):
                        ins = nc.vector.tensor_tensor(dst[:, :], dst[:, :], part, ALU.add)
                        if k < len(parts) - 1:
                            link(ins)
                    if last:
                        ins.then_inc(sum_ready, 1)
                    else:
                        link(ins)

            def add_out(g, t, more=0):
                b = banks(g)
                dve.wait_ge(slab_done, g + 1 + more)
                nc.vector.tensor_tensor(y[:, t:t + 2, :], y[:, t:t + 2, :], ps[:, b:b + 2, :], ALU.add)\
                    .then_inc(slab_read, 1)

            def last_out(first, n):
                for j in range(3):
                    add_out(first + j, 2 * j)
                    cast(first + j + 2)
                    dve.wait_ge(slab_read, first + j + 1)
                    sums([2 * j, 2 * j + 1], [tmp[:, j % 2, k, :] for k in range(2)], 5 * n + j + 1, j == 0, False,
                         True)
                b = banks(first + 3)
                dve.wait_ge(half_done, n + 1)
                nc.vector.tensor_tensor(y[:, 6, :], y[:, 6, :], ps[:, b, :], ALU.add).then_inc(tile_added, 1)
                dve.wait_ge(tile_added, n + 1)
                sums([6], [tmp[:, 1, 0, :]], 5 * n + 4, False, False, True)
                dve.wait_ge(slab_done, first + 4)
                nc.vector.tensor_tensor(y[:, 7, :], y[:, 7, :], ps[:, b + 1, :], ALU.add).then_inc(slab_read, 1)
                dve.wait_ge(slab_read, first + 4)
                sums([7], [tmp[:, 1, 1, :]], 5 * n + 5, False, True, True)

            def layer_norm(n, gain, beta, last=False):
                def centre(p):
                    return nc.vector.tensor_tensor(y[:, 2 * p:2 * p + 2, :], y[:, 2 * p:2 * p + 2, :],
                                                   pair(stat[:, :]), ALU.subtract)

                def lo(t):
                    dve.wait_ge(norm_hi, 8 * n + t + 1)
                    if last:
                        split_scaled(act_lo[:, t, :], y[:, t, :], col("g_mix", t), act_hi[:, t, :])\
                            .then_inc(act_ready, 1)
                    else:
                        split_scaled(act_lo[:, t, :], y[:, t, :], col(beta, t), act_hi[:, t, :], ALU.add)\
                            .then_inc(act_ready, 1)

                v, q = tok_v[:, 0:4], tok_q[:, 0:4]
                dve.wait_ge(tok_sums, NORM[f"ln{n}"])
                link(nc.vector.tensor_copy(q, ps[:, 5, 0:4]))
                link(nc.vector.tensor_tensor(q, q, q, ALU.mult))
                link(nc.vector.tensor_tensor(v, ps[:, 5, 4:8], q, ALU.subtract))
                nc.vector.tensor_scalar(v, v, 0.0, LN_EPS, ALU.max, ALU.add).then_inc(var_ready, 1)
                invert_root(f"ln{n}")
                dve.wait_ge(mean_ready, n + 1)
                for p in range(3):
                    link(centre(p))
                dve.wait_ge(spread_done, NORM[f"ln{n}"])
                for t in range(KT):
                    if t == 6:
                        dve.wait_ge(centred, n + 1)
                    nc.vector.scalar_tensor_tensor(y[:, t, :], y[:, t, :], col(gain, t), ps[:, 5, :],
                                                   ALU.mult, ALU.mult).then_inc(norm_z, 1)
                    if t:
                        lo(t - 1)
                    if t == 6:
                        dve.wait_ge(pool_cast, n + 1)
                        nc.vector.tensor_copy(mark[:, :], eps[:, 0:1]).then_inc(cast_lo, 1)
                lo(KT - 1)

            def mlp(first, layer, scaled):
                def up(j, more, done):
                    dve.wait_ge(relu_done, done + j + 1)
                    nc.vector.tensor_tensor(relu[:, j % 2, :, :], relu[:, j % 2, :, :], relu[:, j % 2, :, :],
                                            ALU.mult).then_inc(sqr_done, 1)
                    dve.wait_ge(hid_split, done + j + 1)
                    split(hid_lo[:, 2 * j:2 * j + 2, :], relu[:, j % 2, :, :], hid_hi[:, 2 * j:2 * j + 2, :])\
                        .then_inc(slab_read, 1)
                    cast(first + j + 2, more)

                dve.wait_ge(x_scaled, scaled)
                with dve.Fori(0, 3) as r:
                    for j in range(4):
                        up(j, r * 8, r * 4 + 16 * layer)
                    for j in range(4):
                        add_out(first + 4 + j, 2 * j, r * 8)
                        cast(first + 4 + j + 2, r * 8)
                for j in range(4):
                    up(j, 24, 12 + 16 * layer)
                last_out(first + 28, 2 * layer + 1)



            for p in range(4):
                dve.wait_ge(x_hi, p + 1)
                split(act_lo[:, 2 * p:2 * p + 2, :], y[:, 2 * p:2 * p + 2, :], act_hi[:, 2 * p:2 * p + 2, :])\
                    .then_inc(act_ready, 2)
                if p < 2:
                    cast(p)
            dve.wait_ge(const_landed, 16 * 7)
            dve.wait_ge(line_done, 1)
            nc.vector.tensor_tensor(rstd[0:16, 0:LINE], ps[0:16, 7, 0:LINE], sum1[0:16, 0:LINE], ALU.add)\
                .then_inc(line_ready, 1)
            nc.vector.tensor_scalar(negsink[:, :], vec[:, VEC["sink"]:VEC["sink"] + 16], -1.0, None, ALU.mult)

            def rope_rotate(n):
                dve.wait_ge(rope_in, n + 1)
                if n:
                    dve.wait_ge(rope_lo, n)
                nc.vector.tensor_tensor(rope_cos[:, :], rope_raw[:, :], cossin[:, 0, :], ALU.mult)
                dve.wait_ge(rope_swapped, n + 1)
                bank = (6, 3, 7, 3, 7)[n]
                link(nc.vector.tensor_tensor(rope_sin[:, :], ps[:, bank, :], cossin[:, 1, :], ALU.mult))
                nc.vector.tensor_tensor(rope_cos[:, :], rope_cos[:, :], rope_sin[:, :], ALU.add)\
                    .then_inc(rope_out, 1)

            dve.wait_ge(line_done, 1)
            dve.wait_ge(c_read, 1)
            link(nc.vector.tensor_tensor(sum1[:, :], tmp[:, 0, 0, :], tmp[:, 0, 1, :], ALU.add))
            nc.vector.tensor_copy(negmax[:, 0:1], sum1[:, 0:1]).then_inc(c_split, 1)
            nc.vector.tensor_copy(negmax[:, 1:2], sum1[:, 0:1]).then_inc(slab_read, 1)
            cast(2)
            dve.wait_ge(slab_read, 1)
            dve.wait_ge(c_read, 2)
            nc.vector.tensor_tensor(sum1[:, :], sum1[:, :], tmp[:, 1, 0, :], ALU.add).then_inc(sum_ready, 1)
            nc.vector.tensor_copy(sum2[:, :], tmp[:, 1, 1, :]).then_inc(slab_read, 1)
            cast(3)
            dve.wait_ge(slab_read, 2)
            dve.wait_ge(c_read, 3)
            nc.vector.tensor_tensor(sum2[:, :], sum2[:, :], tmp[:, 0, 0, :], ALU.add).then_inc(sum_ready, 1)
            nc.vector.tensor_copy(negmax[:, 0:1], tmp[:, 0, 0, 0:1]).then_inc(slab_read, 1)
            dve.wait_ge(tok_sums, NORM["mla"])
            for at, scale in ((0, D / Q_RANK), (4, D / KV_RANK)):
                ins = nc.vector.tensor_scalar(tok_v[:, at:at + 4], ps[:, 4, at:at + 4], float(scale), RMS_EPS,
                                              ALU.mult, ALU.add)
            ins.then_inc(var_ready, 1)
            invert_root("mla", 8)
            dve.wait_ge(spread_done, NORM["mla"])
            for t in range(5):
                bank, gain = (4, col("g_q", t)) if t < 3 else (5, col("g_kv", t - 3))
                nc.vector.scalar_tensor_tensor(c_raw[:, t, :], c_raw[:, t, :], gain, ps[:, bank, :],
                                               ALU.mult, ALU.mult).then_inc(c_full, 1)
                if t:
                    dve.wait_ge(c_split, 1 + t)
                    split(c_lo[:, t - 1, :], c_raw[:, t - 1, :], c_hi[:, t - 1, :]).then_inc(c_ready, 1)
            dve.wait_ge(c_split, 6)
            split(c_lo[:, 4, :], c_raw[:, 4, :], c_hi[:, 4, :]).then_inc(c_ready, 1)
            cast(4)
            rope_rotate(0)
            dve.wait_ge(rope_hi, 1)
            split(kr_lo[:, :], rope_cos[:, :], kr_hi[:, :]).then_inc(rope_lo, 1)

            for half in range(2):
                g = MLA_HALF + 4 * half
                for p in range(2):
                    n = 6 * half + p
                    dve.wait_ge(proj_hi, n + 1)
                    split_scaled(act_lo[:, 4 + 2 * p:6 + 2 * p, :], ps[:, 4 * p:4 * p + 2, :], MLA_SCALE,
                                 act_hi[:, 4 + 2 * p:6 + 2 * p, :]).then_inc(slab_read, 1)
                    cast(g + p + 2)
                    rope_rotate(1 + 2 * half + p)
                    dve.wait_ge(rope_hi, 2 + 2 * half + p)
                    split(qr_lo[:, p, :], rope_cos[:, :], qr_hi[:, p, :]).then_inc(rope_lo, 1)
                for p, hi, lo in ((2, kn_hi, kn_lo), (3, mv_hi, mv_lo)):
                    for q in range(2):
                        n = 6 * half + 2 * p - 2 + q
                        dve.wait_ge(proj_hi, n + 1)
                        b = 4 * (p - 2) + 2 * q
                        ins = split(lo[:, 2 * q:2 * q + 2, :], ps[:, b:b + 2, :], hi[:, 2 * q:2 * q + 2, :])
                    ins.then_inc(slab_read, 1)
                    cast(g + p + 2)

                def mla_bias(u):
                    bias(mla, m_prob, u, lambda w: strip[:, T - w:T])
                    invert(mla, u)

                def mla_out(u):
                    dve.wait_ge(mla.out_hi, u + 1)
                    split(act_lo[:, u, :], ps[:, 6 + u % 2, :], act_hi[:, u, :]).then_inc(act_ready, 1)

                u0 = 4 * half
                mla_bias(u0)
                for u in range(u0, u0 + 4):
                    if u < u0 + 3:
                        mla_bias(u + 1)
                    turn_lo(mla, m_pt_hi, m_pt_lo, u)
                    if u > u0:
                        mla_out(u - 1)
                mla_out(u0 + 3)

            dve.wait_ge(x_scaled, 4)
            last_out(MLA_OUT, 0)
            layer_norm(0, "mix_g0", "mix_b0")
            mlp(MLP0, 0, 12)
            layer_norm(1, "mlp_g0", "mlp_b0")

            for half in range(2):
                g = SWA_HALF + 4 * half
                n = 12 + 5 * half
                dve.wait_ge(proj_hi, n + 1)
                split(swa_k_lo[:, :], ps[:, banks(g), :], swa_k_hi[:, :]).then_inc(slab_read, 1)
                cast(g + 2)
                dve.wait_ge(proj_hi, n + 3)
                for v_hi, v_lo, c in ((va_hi, va_lo, 0), (vb_hi, vb_lo, 64)):
                    ins = split(v_lo[:, :, c:c + 64],
                                ps[:, banks(g + 1), :].rearrange("p (i c) -> p i c", i=4)[:, :, c:c + 64],
                                v_hi[:, :, c:c + 64])
                ins.then_inc(slab_read, 1)
                cast(g + 3)
                for p in range(2):
                    b = banks(g + 2 + p)
                    dve.wait_ge(proj_hi, n + 4 + p)
                    split_scaled(sq_lo[:, 2 * p:2 * p + 2, :], ps[:, b:b + 2, :], HEAD_SCALE,
                                 sq_hi[:, 2 * p:2 * p + 2, :]).then_inc(slab_read, 1)
                    cast(g + 4 + p)
                dve.wait_ge(strips_landed, 16 * (half + 1))
                u0 = 8 * half

                def swa_bias(u):
                    c = 2 * P * (u % 8)
                    bias(swa, s_prob, u, lambda w: strips[:, c + 2 * P - w:c + 2 * P], negsink[:, u:u + 1])
                    invert(swa, u, True)

                swa_bias(u0)
                swa_bias(u0 + 1)
                for u in range(u0, u0 + 8):
                    turn_lo(swa, s_pt_hi, s_pt_lo, u)
                    if u + 2 < u0 + 8:
                        swa_bias(u + 2)
                    if u % 2:
                        t = u // 2
                        dve.wait_ge(swa.out_hi, t + 1)
                        split(o_lo[:, t, :], ps[:, 6 + t % 2, :], o_hi[:, t, :]).then_inc(act_ready, 1)

            dve.wait_ge(x_scaled, 20)
            last_out(SWA_OUT, 2)
            layer_norm(2, "mix_g1", "mix_b1")
            mlp(MLP1, 1, 28)
            layer_norm(3, "mlp_g1", "mlp_b1", True)

            mean_squares("mix", 6, 1.0)
            invert_root("mix")
            dve.wait_ge(tok_ready, NORM["mix"])
            nc.vector.tensor_copy(rstd_tok[:, :], tok_r[:, 0:4])
            dve.wait_ge(rstd_ready, RSTD["mix"])
            dve.wait_ge(u_zeroed, 1)
            for i in range(2):
                g = CONV + 3 * i
                for j, dst in ((0, zc[:, :, :]), (1, tmp[:, 0, :, :]), (2, yc[:, 2 * i:2 * i + 2, :])):
                    b = banks(g + j)
                    dve.wait_ge(slab_done, g + j + 1)
                    nc.vector.tensor_tensor(dst, ps[:, b:b + 2, :], pair(rstd[:, :]), ALU.mult)\
                        .then_inc(slab_read, 1)
                    cast(g + j + 2)
                    dve.wait_ge(slab_read, g + j + 1)
                    if j == 1:
                        link(nc.vector.tensor_tensor(u_pad[:, :, 2:T + 2], tmp[:, 0, :, :], zc[:, :, :], ALU.mult))
                        for k in range(2):
                            c, t = conv[:, k, :], 2 * i + k
                            link(nc.vector.tensor_scalar(c, u_pad[:, k, 2:T + 2], col("conv_w", 8 + t),
                                                         col("conv_b", t), ALU.mult, ALU.add))
                            link(nc.vector.scalar_tensor_tensor(c, u_pad[:, k, 1:T + 1], col("conv_w", 4 + t), c,
                                                                ALU.mult, ALU.add))
                            link(nc.vector.scalar_tensor_tensor(c, u_pad[:, k, 0:T], col("conv_w", t), c,
                                                                ALU.mult, ALU.add))
                nc.vector.tensor_tensor(yc[:, 2 * i:2 * i + 2, :], yc[:, 2 * i:2 * i + 2, :], conv[:, :, :],
                                        ALU.mult).then_inc(conv_done, 1)
                dve.wait_ge(sq_done, SQUARED["conv"] + i + 1)
                if i:
                    link(nc.vector.tensor_tensor(sum1[:, :], sum1[:, :], tmp[:, 1, 0, :], ALU.add))
                    nc.vector.tensor_tensor(sum1[:, :], sum1[:, :], tmp[:, 1, 1, :], ALU.add).then_inc(sum_ready, 1)
                else:
                    link(nc.vector.tensor_tensor(sum1[:, :], tmp[:, 1, 0, :], tmp[:, 1, 1, :], ALU.add))
            mean_squares("conv", 7, 2.0)
            invert_root("conv")
            dve.wait_ge(spread_done, NORM["conv"])
            for t in range(4):
                nc.vector.scalar_tensor_tensor(yc[:, t, :], yc[:, t, :], col("g_oc", t), ps[:, 7, :],
                                               ALU.mult, ALU.mult).then_inc(conv_done, 1)
                dve.wait_ge(mix_hi, t + 1)
                split(o_lo[:, t, :], yc[:, t, :], o_hi[:, t, :]).then_inc(act_ready, 1)

            for half in range(2):
                g = DIL_HALF + 4 * half
                n = 22 + 4 * half
                parts = ((dq_hi, dq_lo, tmp[:, 0, :, :], HEAD_SCALE, "qn_g"),
                         (dk_hi, dk_lo, k_raw[:, :, :], 1.0, "kn_g"))

                def qk_out(p):
                    b = banks(g + p)
                    dve.wait_ge(slab_done, g + p + 1)
                    nc.vector.tensor_tensor(parts[p][2], ps[:, b:b + 2, :], pair(rstd[:, :]), ALU.mult)\
                        .then_inc(slab_read, 1)
                    cast(g + p + 2)

                def qk_norm(p):
                    _, _, raw, _, gain = parts[p]
                    name, b = "qk"[p] + str(half), 4 + 2 * p
                    mean_squares(name, b, 1.0, 16)
                    invert_root(name, 16)
                    dve.wait_ge(spread_done, NORM[name])
                    nc.vector.scalar_tensor_tensor(raw, raw, col(gain), ps[:, b:b + 2, :], ALU.mult, ALU.mult)\
                        .then_inc(qk_full, 1)

                def qk_lo(p):
                    hi, lo, raw, scale, _ = parts[p]
                    dve.wait_ge(proj_hi, n + p + 1)
                    split_scaled(lo[:, :, :], raw, scale, hi[:, :, :]).then_inc(dil_ready, 1)

                def v_out(p):
                    dve.wait_ge(slab_done, g + p + 3)
                    nc.vector.tensor_tensor(tmp[:, 0, p, :].rearrange("p (i c) -> p i c", i=4),
                                            ps[:, banks(g + 2 + p), :].rearrange("p (i c) -> p i c", i=4),
                                            rstd_tok[:, :].unsqueeze(2).broadcast_to([P, 4, P]), ALU.mult)\
                        .then_inc(slab_read, 1)

                def v_lo(p):
                    dve.wait_ge(proj_hi, n + p + 3)
                    split(dv_lo[:, p, :], tmp[:, 0, p, :], dv_hi[:, p, :]).then_inc(dil_ready, 1)

                if half:
                    dve.wait_ge(dil_ready, 4)
                else:
                    dve.wait_ge(slab_read, g)
                qk_out(0)
                qk_norm(0)
                qk_lo(0)
                qk_out(1)
                qk_norm(1)
                dve.wait_ge(dil_ready, 4 * half + 1)
                v_out(0)
                qk_lo(1)
                v_lo(0)
                cast(g + 4)
                v_out(1)
                v_lo(1)
                cast(g + 5)
                dve.wait_ge(strips_landed, 16 * (half + 3))
                u0 = 4 * half

                def dil_bias(u):
                    c = T * (u % 4)
                    bias(dil, d_prob, u, lambda w: strips[:, c + T - w:c + T])
                    invert(dil, u)

                def dil_out(u):
                    r, t = 64 * (u % 2), u // 2
                    dve.wait_ge(sq_done, SQUARED["dil"] + u + 1)
                    ins = split_scaled(o_lo[r:r + 64, 4 + t, :], ps[r:r + 64, 6 + u % 2, :],
                                       vec[r:r + 64, VEC["g_oa"] + t:VEC["g_oa"] + t + 1],
                                       o_hi[r:r + 64, 4 + t, :]).then_inc(dil.out_read, 1)
                    if u % 2:
                        if t:
                            ins = nc.vector.tensor_tensor(sum2[:, :], sum2[:, :], stat[:, :], ALU.add)
                        else:
                            dve.wait_ge(tok_ready, NORM["mix"])
                            ins = nc.vector.tensor_copy(sum2[:, :], stat[:, :])
                        ins.then_inc(mix_sq, 1)
                        dve.wait_ge(mix_sq, 8 + t + 1)
                        dve.wait_ge(dil.out_read, u + 1)
                        ins = nc.vector.tensor_copy(negmax[:, 0:1], sum2[:, 0:1])
                        ins.then_inc(act_ready, 1)

                dil_bias(u0)
                for u in range(u0, u0 + 4):
                    if u + 1 < u0 + 4:
                        dil_bias(u + 1)
                    turn_lo(dil, d_pt_hi, d_pt_lo, u)
                    if u > u0:
                        dil_out(u - 1)
                dil_out(u0 + 3)

            def rms_out(tiles, n, gain, squared):
                for k, t in enumerate(tiles):
                    dve.wait_ge(mix_hi, n_hi[0] + 1)
                    n_hi[0] += 1
                    split_scaled(act_lo[:, t, :], y[:, t, :], col(gain, t), act_hi[:, t, :])\
                        .then_inc(act_ready, 1)
                last = tiles[-1] == KT - 1
                sums(tiles, [tmp[:, n % 2, k, :] for k in range(len(tiles))], squared + n + 1, n == 0, last, False)

            n_hi = [4]
            mean_squares("attn", 0, 2.0)
            invert_root("attn")
            dve.wait_ge(rstd_ready, RSTD["attn"])
            for j in range(4):
                g = MIX_OUT + j
                b = banks(g)
                dve.wait_ge(slab_done, g + 1)
                link(nc.vector.tensor_tensor(conv[:, :, :], ps[:, 4 + b:6 + b, :], pair(stat[:, :]), ALU.mult))
                link(nc.vector.tensor_tensor(y[:, 2 * j:2 * j + 2, :], y[:, 2 * j:2 * j + 2, :], conv[:, :, :],
                                             ALU.add))
                nc.vector.tensor_tensor(y[:, 2 * j:2 * j + 2, :], y[:, 2 * j:2 * j + 2, :], ps[:, b:b + 2, :],
                                        ALU.add).then_inc(slab_read, 1)
                cast(g + 2)
                rms_out([2 * j, 2 * j + 1], j, "g_ffn", SQUARED["ffn"])

            mean_squares("ffn", 7, 1.0)
            invert_root("ffn")
            dve.wait_ge(rstd_ready, RSTD["ffn"])
            dve.wait_ge(u_zeroed, 2)
            for rnd, (first, down, before, count) in enumerate(((FFN_A, FFN_A_DOWN, 0, FF_A),
                                                                (FFN_B, FFN_B_DOWN, FF_A, FF_B))):
                with dve.Fori(0, count // 2) as i:
                    for b in range(2):
                        more, at = i * 2, before + b
                        bank = banks(first + b)
                        dve.wait_ge(slab_done, first + b + 1 + more)
                        nc.vector.tensor_tensor(gate[:, b, 2:T + 2], ps[:, bank, :], rstd[:, :], ALU.mult)\
                            .then_inc(ff_step, 1)
                        nc.vector.tensor_tensor(ffh[:, b, :], ps[:, bank + 1, :], rstd[:, :], ALU.mult)\
                            .then_inc(slab_read, 1)

                        def taps(name, k):
                            c = VEC[name] + k * 22 + at
                            return vec[:, bass.ds(i * 2 + c, 1)]

                        dve.wait_ge(ff_step, 3 * at + 1 + i * 6)
                        nc.vector.tensor_scalar(gconv[:, b, :], gate[:, b, 2:T + 2], taps("fconv_w", 2),
                                                taps("fconv_b", 0), ALU.mult, ALU.add).then_inc(ff_step, 1)
                        dve.wait_ge(ff_step, 3 * at + 2 + i * 6)
                        nc.vector.scalar_tensor_tensor(gconv[:, b, :], gate[:, b, 1:T + 1], taps("fconv_w", 1),
                                                       gconv[:, b, :], ALU.mult, ALU.add).then_inc(ff_step, 1)
                        dve.wait_ge(ff_step, 3 * at + 3 + i * 6)
                        nc.vector.scalar_tensor_tensor(gconv[:, b, :], gate[:, b, 0:T], taps("fconv_w", 0),
                                                       gconv[:, b, :], ALU.mult, ALU.add).then_inc(conv_done, 1)
                        cast(first + b + 2, more, SLAB)
                        dve.wait_ge(silu_done, at + 1 + more)
                        nc.vector.tensor_tensor(ffh[:, b, :], ffh[:, b, :], silu[:, b, :], ALU.mult)\
                            .then_inc(ffh_done, 1)
                        dve.wait_ge(ffh_hi, at + 1 + more)
                        split(h_lo[:, bass.ds(i * 2 + b, 1), :], ffh[:, b:b + 1, :],
                              h_hi[:, bass.ds(i * 2 + b, 1), :]).then_inc(h_ready, 1)
                for j in range(8):
                    g = down + j
                    dve.wait_ge(slab_done, g + 1)
                    nc.vector.tensor_tensor(y[:, j, :], y[:, j, :], ps[:, banks(g), :], ALU.add)\
                        .then_inc(slab_read, 1)
                    cast(g + 2)
                    if rnd:
                        rms_out([j], j, "g_ple", SQUARED["ple"])

            dve.wait_ge(p_split, 1)
            split(p_lo[:, :, :], p_raw[:, :, :], p_hi[:, :, :]).then_inc(p_split, 1)
            dve.wait_ge(slab_done, PLE_PROJ + 1)
            link(nc.vector.tensor_copy(proj[:, 4:6, :], ps[:, 4:6, :]))
            dve.wait_ge(proj_act, 1)
            nc.vector.tensor_copy(proj[:, 6:8, :], ps[:, 6:8, :]).then_inc(slab_read, 1)
            cast(PLE_PROJ + 2)
            mean_squares("ple", 7, 1.0)
            invert_root("ple")
            dve.wait_ge(rstd_ready, RSTD["ple"])
            for j in range(4):
                b = banks(PLE_GATE + j)
                dve.wait_ge(slab_done, PLE_GATE + j + 1)
                nc.vector.tensor_tensor(gate_in[:, j % 2, :, :], ps[:, b:b + 2, :], pair(rstd[:, :]), ALU.mult)\
                    .then_inc(slab_read, 1)
                cast(PLE_GATE + j + 2)
                dve.wait_ge(slab_read, PLE_GATE + j + 1)
                dve.wait_ge(sig_done, j + 1)
                link(nc.vector.tensor_tensor(gate_in[:, j % 2, :, :], gate_in[:, j % 2, :, :],
                                             proj[:, 2 * j:2 * j + 2, :], ALU.mult))
                nc.vector.tensor_tensor(y[:, 2 * j:2 * j + 2, :], y[:, 2 * j:2 * j + 2, :],
                                        gate_in[:, j % 2, :, :], ALU.add).then_inc(out_ready, 1)

        @block.tensor
        def _(pe):
            def product(out, l_hi, l_lo, r_hi, r_lo, start, stop, shared=False):
                mm = nc.tensor.matmul
                mm(out, l_lo, r_hi, start=start, stop=False, skip_group_check=shared)
                mm(out, l_hi, r_hi, start=False, stop=False, skip_group_check=shared)
                return mm(out, l_hi, r_lo, start=False, stop=stop, skip_group_check=shared)

            def gemm(g, outs, kt, hi, lo, ready=None, more=0, free=None, at=0):
                s = g % 2
                if free is None:
                    free = g - 1
                if free > 0:
                    pe.wait_ge(slab_read, free + more)
                pe.wait_ge(cast_lo, g + 1 + more)
                for k in range(kt):
                    if ready:
                        ready(k)
                    for m, o in enumerate(outs):
                        c = (k * len(outs) + m) * P
                        last = product(o, w_hi[s][:, c:c + P], w_lo[s][:, c:c + P], hi[:, at + k, :],
                                       lo[:, at + k, :], k == 0, k == kt - 1)
                last.then_inc(slab_done, 1)

            def plain(g, kt=KT, hi=act_hi, lo=act_lo, ready=None, more=0, n=2, free=None):
                b = banks(g)
                gemm(g, [ps[:, b + m, :] for m in range(n)], kt, hi, lo, ready, more, free)

            def act_tiles(gen):
                return lambda k: pe.wait_ge(act_ready, gen + k + 1)

            def values(g, bank, free, ready=None):
                s = g % 2
                pe.wait_ge(slab_read, free)
                pe.wait_ge(cast_lo, g + 1)
                for i in range(4):
                    if ready:
                        ready(i)
                    for k in range(KT):
                        q = slice(i * P, (i + 1) * P)
                        last = product(ps[:, bank, q], act_hi[:, k, q], act_lo[:, k, q],
                                       w_hi[s][:, k * P:(k + 1) * P], w_lo[s][:, k * P:(k + 1) * P],
                                       k == 0, k == KT - 1)
                last.then_inc(slab_done, 1)

            def token_sums(src, bank, at=0):
                for i in range(4):
                    last = nc.tensor.matmul(ps[:, bank, at + i:at + i + 1], src[:, i * P:(i + 1) * P], ones[:, 0:1],
                                            start=True, stop=True)
                return last

            def spread(name, bank, at=0):
                pe.wait_ge(tok_ready, NORM[name])
                for i in range(4):
                    last = nc.tensor.matmul(ps[:, bank, i * P:(i + 1) * P],
                                            tok_r[:, at + i:at + i + 1].broadcast_to([P, P]), ident, start=True,
                                            stop=True)
                return last

            def between(steps):
                def ready(k):
                    if k in steps:
                        steps[k]()
                return ready

            def score(a, u, operands, first):
                h, at = a.h, a.score_banks[u % 2]
                for m, group in enumerate(h.groups):
                    v = u - a.ahead
                    if v >= first:
                        read = 4 * v + sum(len(x) for x in h.groups[:m + 1])
                        pe.wait_ge(a.biased, read)
                    for i in group:
                        bank, c = h.place[i]
                        dst = ps[:, at + bank, c:c + h.width[i]]
                        parts = operands(u, i, slice(h.key0[i], h.key0[i] + h.width[i]))
                        for x, part in enumerate(parts):
                            last = product(dst, *part, x == 0, x == len(parts) - 1)
                    last.then_inc(a.scored, 1)

            def turn(a, u, prob):
                h = a.h
                waited = 0
                for n in range(a.nseg):
                    if u:
                        pe.wait_ge(a.turn_lo, a.nseg * (u - 1) + n + 1)
                    for i, j, c in h.blocks(n):
                        need = h.order.index(i) + 1
                        if need > waited:
                            pe.wait_ge(a.normed, 4 * u + need)
                            waited = need
                        k = h.off[i] + j * P - h.key0[i]
                        last = nc.tensor.transpose(ps[:, a.trans_bank + n, c:c + P], prob[:, u % 2, k:k + P], ident)
                    last.then_inc(a.turned, 1)

            def mix(a, u, bank, pt_hi, pt_lo, v_of, start=True, stop=True):
                for j, (reach, seg, c) in enumerate(a.h.keys):
                    pe.wait_ge(a.turn_lo, a.nseg * u + seg + 1)
                    c += BANK * seg
                    w = reach * P
                    last = product(ps[:, bank, j * P:j * P + w], *v_of(u, j), pt_hi[:, c:c + w], pt_lo[:, c:c + w],
                                   start and j == 0, stop and j == 3, True)
                if stop:
                    last.then_inc(a.mixed, 1)

            for j in range(3):
                g = MLA_IN + j
                plain(g, ready=act_tiles(X_IN) if j == 0 else None)
                if j == 0:
                    pe.wait_ge(const_landed, 16 * 7)
                    nc.tensor.matmul(ps[0:16, 7, 0:LINE], stat[0:32, 0:16], sum2[0:32, 0:LINE], start=True,
                                     stop=True).then_inc(line_done, 1)
            pe.wait_ge(sum_ready, SUM_READY["mla_q"])
            token_sums(sum1, 4)
            pe.wait_ge(sum_ready, SUM_READY["mla_kv"])
            token_sums(sum2, 4, 4).then_inc(tok_sums, 1)
            pe.wait_ge(rope_in, 1)
            nc.tensor.matmul(ps[:, 6, :], swap, rope_raw[:, :], start=True, stop=True).then_inc(rope_swapped, 1)
            spread("mla", 4)
            spread("mla", 5, 4).then_inc(spread_done, 1)

            def mla_operands(u, i, keys):
                x, q, r = u % 4, slice(i * P, (i + 1) * P), 64 * (u % 2)
                return [(act_hi[:, 4 + x, q], act_lo[:, 4 + x, q], kn_hi[:, x, keys], kn_lo[:, x, keys]),
                        (qr_hi[r:r + 64, x // 2, q], qr_lo[r:r + 64, x // 2, q],
                         kr_hi[r:r + 64, keys], kr_lo[r:r + 64, keys])]

            def mla_values(u, j):
                c = slice(P * (u % 4), P * (u % 4) + P)
                return mv_hi[:, j, c], mv_lo[:, j, c]

            def c_tiles(at):
                return lambda k: pe.wait_ge(c_ready, at + k + 1)

            for half in range(2):
                g = MLA_HALF + 4 * half
                if half:
                    pe.wait_ge(mla.biased, 16)
                else:
                    pe.wait_ge(slab_read, 3)
                gemm(g, [ps[:, b, :] for b in range(3)], 3, c_hi, c_lo, c_tiles(0), free=g)
                if half:
                    pe.wait_ge(mla.turn_lo, 3 * 4)
                    pe.wait_ge(act_ready, MLA_O + 4)
                else:
                    pe.wait_ge(rope_out, 1)
                gemm(g + 1, [ps[:, b, :] for b in range(4, 7)], 3, c_hi, c_lo, c_tiles(0), free=g)
                pe.wait_ge(rope_in, 2 + 2 * half)
                nc.tensor.matmul(ps[:, 3, :], swap, rope_raw[:, :], start=True, stop=True).then_inc(rope_swapped, 1)
                pe.wait_ge(rope_out, 2 + 2 * half)
                gemm(g + 2, [ps[:, b, :] for b in range(4)], 2, c_hi, c_lo, c_tiles(3), free=g + 1, at=3)
                pe.wait_ge(rope_in, 3 + 2 * half)
                nc.tensor.matmul(ps[:, 7, :], swap, rope_raw[:, :], start=True, stop=True).then_inc(rope_swapped, 1)
                pe.wait_ge(rope_out, 3 + 2 * half)
                s = (g + 3) % 2
                pe.wait_ge(slab_read, g + 2)
                pe.wait_ge(cast_lo, g + 4)
                for i in range(4):
                    for k in range(2):
                        q = slice(i * P, (i + 1) * P)
                        last = product(ps[:, 4 + i, :], c_hi[:, 3 + k, q], c_lo[:, 3 + k, q],
                                       w_hi[s][:, k * T:(k + 1) * T], w_lo[s][:, k * T:(k + 1) * T],
                                       k == 0, k == 1)
                last.then_inc(slab_done, 1)
                pe.wait_ge(slab_read, g + 3)
                pe.wait_ge(rope_lo, 3 + 2 * half)
                u0 = 4 * half
                score(mla, u0, mla_operands, u0)
                pe.wait_ge(slab_read, g + 4)
                for u in range(u0, u0 + 4):
                    if u < u0 + 3:
                        score(mla, u + 1, mla_operands, u0)
                    turn(mla, u, m_prob)
                    if u > u0:
                        mix(mla, u - 1, 6 + (u - 1) % 2, m_pt_hi, m_pt_lo, mla_values)
                mix(mla, u, 6 + u % 2, m_pt_hi, m_pt_lo, mla_values)

            def last_plain(g, hi, lo):
                s, b = g % 2, banks(g)
                pe.wait_ge(slab_read, g - 1)
                pe.wait_ge(cast_lo, g + 1)
                for m in range(2):
                    for k in range(KT):
                        c = (k * 2 + m) * P
                        last = product(ps[:, b + m, :], w_hi[s][:, c:c + P], w_lo[s][:, c:c + P], hi[:, k, :],
                                       lo[:, k, :], k == 0, k == KT - 1)
                    last.then_inc((half_done, slab_done)[m], 1)

            def layer_stats(n):
                pe.wait_ge(sum_ready, SUM_READY["ln"] + 2 * n + 1)
                token_sums(sum1, 5)
                nc.tensor.matmul(ps[:, 4, :], ones, sum1[:, :], start=True, stop=True).then_inc(mean_done, 1)
                pe.wait_ge(sum_ready, SUM_READY["ln"] + 2 * n + 2)
                token_sums(sum2, 5, 4).then_inc(tok_sums, 1)
                spread(f"ln{n}", 5).then_inc(spread_done, 1)

            def mlp(first, gen):
                def hidden(g, more):
                    return lambda k: pe.wait_ge(slab_read, first + k // 2 + 1 + more)

                def rnd(more, downs=4):
                    for j in range(4):
                        plain(first + j, more=more, ready=act_tiles(gen))
                    for j in range(downs):
                        plain(first + 4 + j, hi=hid_hi, lo=hid_lo, more=more, ready=hidden(j, more) if j == 0 else None)

                with pe.Fori(0, 3) as r:
                    rnd(r * 8)
                rnd(24, 3)
                last_plain(first + 31, hid_hi, hid_lo)

            pe.wait_ge(mla.turn_lo, 3 * 8)
            for j in range(3):
                plain(MLA_OUT + j, ready=act_tiles(MLA_O))
            last_plain(MLA_OUT + 3, act_hi, act_lo)
            layer_stats(0)
            mlp(MLP0, LN_0)
            layer_stats(1)

            def swa_operands(u, i, keys):
                t, q, r = (u // 2) % 4, slice(i * P, (i + 1) * P), 64 * (u % 2)
                return [(sq_hi[r:r + 64, t, q], sq_lo[r:r + 64, t, q], swa_k_hi[r:r + 64, keys],
                         swa_k_lo[r:r + 64, keys])]

            def swa_values(u, j):
                hi, lo = ((va_hi, va_lo), (vb_hi, vb_lo))[u % 2]
                return hi[:, j, :], lo[:, j, :]

            for half in range(2):
                g = SWA_HALF + 4 * half
                if half:
                    pe.wait_ge(swa.biased, 32)
                plain(g, n=1, ready=act_tiles(LN_1))
                values(g + 1, banks(g + 1), g)
                for p in range(2):
                    plain(g + 2 + p)
                pe.wait_ge(slab_read, g + 4)
                u0 = 8 * half
                score(swa, u0, swa_operands, u0)
                score(swa, u0 + 1, swa_operands, u0)
                for u in range(u0, u0 + 8):
                    turn(swa, u, s_prob)
                    if u + 2 < u0 + 8:
                        score(swa, u + 2, swa_operands, u0)
                    t = u // 2
                    if u % 2 == 0 and t >= 2:
                        pe.wait_ge(act_ready, SWA_O + t - 1)
                    mix(swa, u, 6 + t % 2, s_pt_hi, s_pt_lo, swa_values, u % 2 == 0, u % 2 == 1)

            for j in range(3):
                plain(SWA_OUT + j, hi=o_hi, lo=o_lo, ready=act_tiles(SWA_O))
            last_plain(SWA_OUT + 3, o_hi, o_lo)
            layer_stats(2)
            mlp(MLP1, LN_2)
            layer_stats(3)

            def mix_sums():
                pe.wait_ge(mix_sq, 8)
                token_sums(sum2, 6).then_inc(tok_sums, 1)

            plain(CONV, ready=act_tiles(LN_3))
            plain(CONV + 1, ready=between({4: mix_sums, 6: lambda: spread("mix", 6).then_inc(spread_done, 1)}))
            for j in range(2, 6):
                plain(CONV + j)

            def dil_operands(u, i, keys):
                p, q, r = (u // 2) % 2, slice(i * P, (i + 1) * P), 64 * (u % 2)
                return [(dq_hi[r:r + 64, p, q], dq_lo[r:r + 64, p, q], dk_hi[r:r + 64, p, keys],
                         dk_lo[r:r + 64, p, keys])]

            def dil_values(u, j):
                p, c = (u // 2) % 2, slice(j * P, (j + 1) * P)
                return dv_hi[:, p, c], dv_lo[:, p, c]

            def head_sums(n, bank):
                pe.wait_ge(qk_sq, n + 1)
                for k in range(2):
                    for i in range(4):
                        c = 8 * k + 2 * i
                        last = nc.tensor.matmul(ps[:, bank, c:c + 2], tmp[:, 1, k, i * P:(i + 1) * P],
                                                ones64[:, 0:P:64], start=True, stop=True)
                last.then_inc(tok_sums, 1)

            def head_spread(name, bank):
                pe.wait_ge(tok_ready, NORM[name])
                for k in range(2):
                    for i in range(4):
                        for h in range(2):
                            c, r = 8 * k + 2 * i + h, 64 * h
                            last = nc.tensor.matmul(ps[r:r + 64, bank + k, i * P:(i + 1) * P],
                                                    tok_r[:, c:c + 1].broadcast_to([P, 64]), ident,
                                                    start=True, stop=True)
                last.then_inc(spread_done, 1)

            for half in range(2):
                g = DIL_HALF + 4 * half
                if half:
                    pe.wait_ge(dil.turn_lo, 3 * 4)
                def conv_sums():
                    pe.wait_ge(sum_ready, SUM_READY["conv"])
                    token_sums(sum1, 7).then_inc(tok_sums, 1)

                def k_sums():
                    if half == 0:
                        pe.wait_ge(conv_done, 6)
                    else:
                        pe.wait_ge(dil.out_read, 4)
                    head_sums(2 * half + 1, 6)

                steps = {5: conv_sums, 7: lambda: spread("conv", 7).then_inc(spread_done, 1)} if half == 0 else {}
                plain(g, ready=between(steps))
                plain(g + 1, ready=between({3: lambda: head_sums(2 * half, 4), 5: lambda: head_spread(f"q{half}", 4)}))
                values(g + 2, banks(g + 2), g + 1, between({2: k_sums}))
                values(g + 3, banks(g + 3), g + 2, between({0: lambda: head_spread(f"k{half}", 6)}))
                pe.wait_ge(slab_read, g + 4)
                pe.wait_ge(dil_ready, 4 * half + 2)
                u0 = 4 * half
                score(dil, u0, dil_operands, u0)

                def dil_mix(u):
                    if u - 2 >= u0:
                        pe.wait_ge(dil.out_read, u - 1)
                    mix(dil, u, 6 + u % 2, d_pt_hi, d_pt_lo, dil_values)

                for u in range(u0, u0 + 4):
                    if u < u0 + 3:
                        score(dil, u + 1, dil_operands, u0)
                    turn(dil, u, d_prob)
                    if u == u0 + 1:
                        pe.wait_ge(dil_ready, 4 * half + 4)
                    if u > u0:
                        dil_mix(u - 1)
                dil_mix(u0 + 3)

            pe.wait_ge(dil.turn_lo, 3 * 8)
            for j in range(4):
                g = MIX_OUT + j
                s, b = g % 2, banks(g)
                if j < 2:
                    pe.wait_ge(dil.turn_lo, 3 * 8)
                    if j == 0:
                        pe.wait_ge(dil.out_read, 8)
                else:
                    pe.wait_ge(slab_read, g - 1)
                if j == 1:
                    pe.wait_ge(rstd_ready, RSTD["attn"])
                pe.wait_ge(cast_lo, g + 1)
                for k in range(KT):
                    if j == 0:
                        pe.wait_ge(act_ready, MIX_Y + k + 1)
                    if j == 0 and k == 4:
                        pe.wait_ge(mix_sq, 12)
                        token_sums(sum2, 0).then_inc(tok_sums, 1)
                    if j == 0 and k == 6:
                        spread("attn", 0).then_inc(spread_done, 1)
                    for m in range(2):
                        c = (k * 2 + m) * P
                        last = product(ps[:, b + m + (4 if k >= 4 else 0), :], w_hi[s][:, c:c + P],
                                       w_lo[s][:, c:c + P], o_hi[:, k, :], o_lo[:, k, :], k % 4 == 0, k % 4 == 3)
                last.then_inc(slab_done, 1)

            for rnd, (first, down, before, count) in enumerate(((FFN_A, FFN_A_DOWN, 0, FF_A),
                                                                (FFN_B, FFN_B_DOWN, FF_A, FF_B))):
                if rnd == 0:
                    plain(first, ready=act_tiles(FFN_X))
                    pe.wait_ge(sum_ready, SUM_READY["ffn"])
                    token_sums(sum2, 7).then_inc(tok_sums, 1)
                    plain(first + 1, ready=between({2: lambda: spread("ffn", 7).then_inc(spread_done, 1)}))
                with pe.Fori(1 if rnd == 0 else 0, count // 2) as i:
                    for b in range(2):
                        plain(first + b, more=i * 2)
                for j in range(8):
                    def hidden(k):
                        pe.wait_ge(h_ready, before + k + 1)
                    plain(down + j, kt=count, hi=h_hi, lo=h_lo, ready=hidden if j == 0 else None, n=1)

            s = PLE_PROJ % 2
            pe.wait_ge(p_split, 2)
            pe.wait_ge(slab_read, PLE_PROJ)
            pe.wait_ge(cast_lo, PLE_PROJ + 1)
            for m in range(KT):
                for k in range(2):
                    c = (k * KT + m) * P
                    last = product(ps[:, m, :], w_hi[s][:, c:c + P], w_lo[s][:, c:c + P], p_hi[:, k, :],
                                   p_lo[:, k, :], k == 0, k == 1)
            last.then_inc(slab_done, 1)
            for j in range(4):
                steps = between({2: lambda: spread("ple", 7).then_inc(spread_done, 1)} if j == 1 else {})
                plain(PLE_GATE + j, ready=act_tiles(PLE_X) if j == 0 else steps, free=PLE_GATE if j < 2 else None)
                if j == 0:
                    pe.wait_ge(sum_ready, SUM_READY["ple"])
                    token_sums(sum2, 7).then_inc(tok_sums, 1)


def rope_table():
    half = 32
    inv = np.float32(10000.0) ** (-np.arange(half, dtype=np.float32) / np.float32(half))
    ang = (np.arange(T, dtype=np.float32)[:, None] * inv[None, :].astype(np.float32)).T.astype(np.float32)
    cos, sin = np.cos(ang), np.sin(ang)
    return np.stack([np.concatenate([cos] * 4), np.concatenate([-sin, sin] * 2)], 1).astype(np.float32)


def matrices():
    eye = np.eye(P)
    ones = np.full((P, P), 1.0 / D)
    heads = np.kron(np.eye(2), np.full((64, 64), 1.0 / 64))
    swap = eye[np.arange(P) ^ 32]
    return np.stack([eye, ones, heads, swap], 1).astype(np.float32)


def strip_distance():
    return np.arange(P)[:, None] + (T - P) - np.arange(T)[None, :]


def causal_table():
    return np.where(strip_distance() >= 0, 0.0, MASKED).astype(np.float32)


def dilated_table():
    d = strip_distance()
    count = (d <= 128).astype(int) + (d % 4 == 0) + (d % 16 == 0)
    slopes = np.exp2(-np.arange(1, 9, dtype=np.float32))
    table = np.where((d >= 0) & (count > 0), np.log(np.maximum(count, 1)) - slopes[:, None, None] * d, MASKED)
    return np.ascontiguousarray(table.reshape(2, 4, P, T).transpose(0, 2, 1, 3).reshape(2, P, 4 * T), np.float32)


def t5_tables():
    d = 2 * P - 1 - np.arange(LINE)
    n = np.maximum(d, 0)
    nf = np.maximum(n, 1).astype(np.float32)
    large = 16 + (np.log(nf / np.float32(16)) / np.float32(np.log(128 / 16)) * np.float32(16)).astype(np.int32)
    bucket = np.where(n < 16, n, np.minimum(large, 31))
    valid = (d >= 0) & (d < P)
    onehot = ((np.arange(32)[:, None] == bucket[None, :]) & valid[None, :]).astype(np.float32)
    return onehot, np.broadcast_to(np.where(valid, 0.0, MASKED), (16, LINE)).astype(np.float32)


def blocks(w):
    k, n = w.shape
    return w.reshape(k // P, P, n).transpose(1, 0, 2).reshape(P, -1)


def columns(w, n):
    return [blocks(w[:, c:c + n]) for c in range(0, w.shape[1], n)]


def head_order():
    return [(2 * (u // 8) + u % 2) * 4 + (u // 2) % 4 for u in range(16)]


def pack_slabs(a):
    out = []
    w = a["mla_w_in"][0]
    w = np.concatenate([w, w[:, Q_RANK + KV_RANK:]], 1)
    out += columns(w, 256)
    uq, uk, uv = a["mla_w_uq"][0], a["mla_w_uk"][0], a["mla_w_uv"][0]
    for half in range(2):
        for p in range(2):
            h = 4 * half + 2 * p
            out.append(blocks(np.concatenate([uq[:, h, :128], uq[:, h + 1, :128], uq[:, h, 128:],
                                              uq[:, h + 1, 128:]], 1)))
        for m in (uk, uv):
            out.append(blocks(m[:, 4 * half:4 * half + 4].reshape(KV_RANK, 512)))
    out += columns(a["mla_w_o"][0], 256)

    def mlp(layer):
        for r in range(4):
            s = slice(D * r, D * (r + 1))
            out.extend(columns(a["mlp_w_up"][layer][:, s], 256))
            out.extend(columns(a["mlp_w_down"][layer][s], 256))

    mlp(0)
    order = head_order()
    kv = a["kv_w_shared"]
    q = a["swa_w_q"][0].reshape(D, 16, 64)[:, order].reshape(D, D)
    for half in range(2):
        for at in (0, 256):
            out.append(blocks(kv[:, at + 128 * half:at + 128 * half + 128]))
        out += columns(q[:, 512 * half:512 * (half + 1)], 256)
    out += columns(a["swa_w_o"][0].reshape(16, 64, D)[order].reshape(D, D), 256)
    mlp(1)
    zb, zc, zx, zq, zk, zv = np.split(a["w_in_2"][0], 6, 1)
    for i in range(2):
        s = slice(256 * i, 256 * (i + 1))
        out += [blocks(zc[:, s]), blocks(zx[:, s]), blocks(zb[:, s])]
    for half in range(2):
        s = slice(256 * half, 256 * (half + 1))
        out += [blocks(zq[:, s]), blocks(zk[:, s]), *columns(zv[:, s], 128)]
    out += columns(a["w_out_2"][0], 256)
    gate, up, down = a["w_gate_2"][0], a["w_up_2"][0], a["w_down_2"][0]
    for before, count in ((0, FF_A), (FF_A, FF_B)):
        for t in range(before, before + count):
            s = slice(P * t, P * (t + 1))
            out.append(blocks(np.concatenate([gate[:, s], up[:, s]], 1)))
        out += columns(down[P * before:P * (before + count)], P)
    out.append(blocks(a["w_ple_proj_2"][0]))
    out += columns(a["w_ple_gate_2"][0], 256)
    slabs = np.zeros((SLABS, P, SLAB), np.float32)
    assert len(out) == SLABS
    for g, w in enumerate(out):
        assert w.shape[1] == slab_width(g) or w.shape[1] == SLAB, (g, w.shape)
        slabs[g, :, :w.shape[1]] = w
    return slabs


def pack_vectors(a):
    def tiles(v):
        return v.reshape(-1, P).T

    parts = {"g_q": tiles(a["mla_g_q"][0]), "g_kv": tiles(a["mla_g_kv"][0]), "g_mix": tiles(a["g_mix_2"][0]),
             "conv_w": tiles(a["conv_w_2"][0]), "conv_b": tiles(a["conv_b_2"][0]),
             "qn_g": tiles(np.tile(a["q_norm_g_2"][0], 2)), "kn_g": tiles(np.tile(a["k_norm_g_2"][0], 2)),
             "g_oc": tiles(a["g_out_conv_2"][0]), "g_oa": tiles(a["g_out_attn_2"][0]),
             "g_ffn": tiles(a["g_ffn_2"][0]), "fconv_w": tiles(a["ffn_conv_w_2"][0]),
             "fconv_b": tiles(a["ffn_conv_b_2"][0]), "g_ple": tiles(a["g_ple_2"][0]),
             "sink": np.broadcast_to(a["swa_sinks"][0][head_order()], (P, 16))}
    for layer in range(2):
        for kind in ("mix", "mlp"):
            parts[f"{kind}_g{layer}"] = tiles(a[f"ln_{kind}_g"][layer])
            parts[f"{kind}_b{layer}"] = tiles(a[f"ln_{kind}_b"][layer])
    vecs = np.zeros((P, NVEC), np.float32)
    for name, part in parts.items():
        vecs[:, VEC[name]:VEC[name] + part.shape[1]] = part
    return vecs


def kernel(**inputs):
    import concourse.bacc as bacc
    from concourse.bass_utils import run_bass_kernel_spmd as run

    a = {name: np.asarray(value) for name, value in inputs.items()}
    onehot, line_mask = t5_tables()
    arrays = {
        "slabs": pack_slabs(a),
        "x_t": a["x"][0].T.reshape(KT, P, T).transpose(1, 0, 2),
        "ple_t": a["p_2"][0, 0].T.reshape(2, P, T).transpose(1, 0, 2),
        "vecs": pack_vectors(a),
        "rel_bias": a["rel_bias"][:, head_order()],
        "onehot": onehot,
        "line_mask": line_mask,
        "rope": rope_table(),
        "mats": matrices(),
        "causal": causal_table(),
        "dilated": dilated_table(),
    }
    arrays = {name: np.ascontiguousarray(value) for name, value in arrays.items()}
    nc = bacc.Bacc("TRN2", target_bir_lowering=False, num_devices=1)
    args = {name: nc.dram_tensor(name, value.shape, F32, kind="ExternalInput").ap()
            for name, value in arrays.items()}
    out = nc.dram_tensor("out", (P, KT, T), F32, kind="ExternalOutput").ap()
    program(nc, **args, out=out)
    result = run(nc, [arrays], core_ids=[0]).results[0]["out"]
    return np.ascontiguousarray(result.transpose(1, 0, 2).reshape(D, T).T).reshape(1, T, D)
```

```python
from contextlib import ExitStack

import numpy as np

import concourse.bass as bass
from concourse import mybir

ALU = mybir.AluOpType
ACT = mybir.ActivationFunctionType
F32 = mybir.dt.float32
F32R = mybir.dt.float32r

P = 128
T = 512
D = 1024
KT = D // P
BANK = 512
SLAB = 2048
ALPHA = float((2 * 2) ** 0.25)
LN_EPS, RMS_EPS = 1e-5, 1e-6
Q_RANK, KV_RANK = 384, 256
MLA_SCALE = float((128 + 64) ** -0.5)
HEAD_SCALE = 64.0 ** -0.5
MASKED = -1e30
HUGE = 3e38

MLA_IN = 0
MLA_HALF = 3
MLA_OUT = 11
MLP0 = 15
SWA_KV = 47
SWA_Q = 49
SWA_OUT = 53
MLP1 = 57
CONV = 89
DIL_HALF = 95
MIX_OUT = 101
FFN_A, FFN_A_DOWN = 105, 117
FFN_B, FFN_B_DOWN = 125, 136
PLE_PROJ = 135
PLE_GATE = 144
SLABS = 148
FF_A, FF_B = 12, 10

NORM = {name: n + 1 for n, name in enumerate(
    ("mla", "ln0", "ln1", "ln2", "ln3", "mix", "conv", "q0", "k0", "q1", "k1", "attn", "ffn", "ple"))}
SUM_READY = {"mla_q": 1, "mla_kv": 2, "ln": 2, "conv": 11, "ffn": 12, "ple": 13}
SQUARED = {"mix": 20, "conv": 28, "dil": 30, "ffn": 38, "ple": 42}
RSTD = {"mix": 1, "attn": 2, "ffn": 3, "ple": 4}

X_IN, MLA_O, LN_0, LN_1, SWA_O, LN_2, LN_3, MIX_Y, FFN_X, PLE_X = range(0, 80, 8)


def slab_width(g):
    if MLA_HALF <= g < MLA_OUT:
        return (3 * 384, 3 * 384, 2 * 512, 2 * 512)[(g - MLA_HALF) % 4]

    if FFN_A_DOWN <= g < FFN_B:
        return FF_A * P
    if FFN_B_DOWN <= g < PLE_GATE:
        return FF_B * P
    return SLAB


VEC = {}
NVEC = 0
for _name, _n in (("g_q", 3), ("g_kv", 2), ("mix_g0", 8), ("mix_b0", 8), ("mlp_g0", 8), ("mlp_b0", 8),
                  ("mix_g1", 8), ("mix_b1", 8), ("mlp_g1", 8), ("mlp_b1", 8), ("g_mix", 8),
                  ("conv_w", 12), ("conv_b", 4), ("qn_g", 1), ("kn_g", 1), ("g_oc", 4), ("g_oa", 4),
                  ("g_ffn", 8), ("fconv_w", 66), ("fconv_b", 22), ("g_ple", 8), ("sink", 16),
                  ):
    VEC[_name] = NVEC
    NVEC += _n
LINE = 384


class Heads:

    def __init__(self, band):
        first = [max(0, i - 1) if band else 0 for i in range(4)]
        self.key0 = [f * P for f in first]
        self.tiles = [list(range(first[i], i + 1)) for i in range(4)]
        self.width = [len(t) * P for t in self.tiles]
        self.off = [sum(self.width[:i]) for i in range(4)]
        self.total = sum(self.width)
        if band:
            self.place = [(0, 0), (0, 128), (1, 0), (1, 256)]
            keys = [(0, 0), (0, 256), (1, 0), (1, 256)]
            self.segments = [512, 384]
        else:
            self.place = [(0, 0), (1, 0), (0, 128), (2, 0)]
            keys = [(0, 0), (1, 0), (2, 0), (1, 384)]
            self.segments = [512, 512, 256]
        reach = 2 if band else 4
        self.keys = [(min(4 - j, reach), *keys[j]) for j in range(4)]
        self.groups = [[0, 1], [2, 3]] if band else [[0, 2], [1], [3]]
        self.order = [i for group in self.groups for i in group]

    def blocks(self, n):
        return [(j + k, j, c + k * P) for j, (reach, bank, c) in enumerate(self.keys) if bank == n
                for k in range(reach)]


CAUSAL, BAND = Heads(False), Heads(True)


def program(nc, slabs, x_t, ple_t, vecs, rel_bias, onehot, line_mask, rope, mats, causal, dilated, out):
    ctx = ExitStack()
    with ctx:
        def sem(name):
            return ctx.enter_context(nc.semaphore(name))

        def keep(name, shape, dt=F32):
            return ctx.enter_context(nc.sbuf_tensor(name, shape, dt))

        stage = [keep(f"stage{s}", [P, SLAB]) for s in range(2)]
        w_hi = [keep(f"w_hi{s}", [P, SLAB], F32R) for s in range(2)]
        w_lo = [keep(f"w_lo{s}", [P, SLAB], F32R) for s in range(2)]
        act_hi = keep("act_hi", [P, KT, T], F32R)
        act_lo = keep("act_lo", [P, KT, T], F32R)
        y = keep("y", [P, KT, T])
        with ExitStack() as shared:
            s_pt2_hi = shared.enter_context(nc.sbuf_tensor("s_pt2_hi", [P, BAND.total], F32R))
            s_pt2_lo = shared.enter_context(nc.sbuf_tensor("s_pt2_lo", [P, BAND.total], F32R))
        tmp = keep("tmp", [P, 2, 2, T])
        vec = keep("vec", [P, NVEC])
        mat = keep("mat", [P, 4, P])
        ident, ones, ones64, swap = (mat[:, i, :] for i in range(4))
        eps = keep("eps", [P, 2])
        sum1 = keep("sum1", [P, T])
        sum2 = keep("sum2", [P, T])
        rstd = keep("rstd", [P, T])
        stat = keep("stat", [P, T])
        tok_v, tok_s, tok_r, tok_q = (keep(f"tok_{x}", [P, 16]) for x in "vsrq")
        rstd_tok = keep("rstd_tok", [P, 4])
        table_mark = keep("table_mark", [P, 1])
        mark = keep("mark", [P, 1])
        negmax = keep("negmax", [P, 4 * 16])
        rowsum = keep("rowsum", [P, 4 * 16])
        sinkexp = keep("sinkexp", [P, 4 * 16])
        rden = keep("rden", [P, 4 * 16])
        negsink = keep("negsink", [P, 16])
        ps = ctx.enter_context(nc.psum_tensor("ps", [P, 8, BANK], F32))

        floors = [0]

        def part(floor, *specs):
            made = []
            with ExitStack() as shared:
                if floor:
                    floors[0] += 1
                    shared.enter_context(nc.sbuf_tensor(f"floor{floors[0]}", [P, floor], F32))
                for name, shape, dt in specs:
                    made.append(shared.enter_context(nc.sbuf_tensor(name, shape, dt)))
                    floor += int(np.prod(shape[1:]))
            return (*made, floor)

        (qr_hi, qr_lo, kn_hi, kn_lo, kr_hi, kr_lo, mv_hi, mv_lo, c_hi, c_lo, cossin, strip, top) = part(
            0, ("qr_hi", [P, 2, T], F32R), ("qr_lo", [P, 2, T], F32R), ("kn_hi", [P, 4, T], F32R),
            ("kn_lo", [P, 4, T], F32R), ("kr_hi", [P, T], F32R), ("kr_lo", [P, T], F32R),
            ("mv_hi", [P, 4, T], F32R), ("mv_lo", [P, 4, T], F32R), ("c_hi", [P, 5, T], F32R),
            ("c_lo", [P, 5, T], F32R), ("cossin", [P, 2, T], F32), ("strip", [P, T], F32))
        c_raw, rope_raw, rope_cos, rope_sin, _ = part(
            top, ("c_raw", [P, 5, T], F32), ("rope_raw", [P, T], F32), ("rope_cos", [P, T], F32),
            ("rope_sin", [P, T], F32))
        m_prob, m_pt_hi, m_pt_lo, _ = part(
            top, ("m_prob", [P, 2, CAUSAL.total], F32), ("m_pt_hi", [P, CAUSAL.total], F32R),
            ("m_pt_lo", [P, CAUSAL.total], F32R))
        hid_hi, hid_lo, relu, top = part(
            0, ("hid_hi", [P, KT, T], F32R), ("hid_lo", [P, KT, T], F32R), ("relu", [P, 2, 2, T], F32))
        strips, top_strips = part(top, ("strips", [P, SLAB], F32))
        o_hi, o_lo, gap = part(0, ("o_hi", [P, KT, T], F32R), ("o_lo", [P, KT, T], F32R))
        swa_k_hi, swa_k_lo, _ = part(gap, ("swa_k_hi", [P, 2, T], F32R), ("swa_k_lo", [P, 2, T], F32R))
        dv_hi, dv_lo, top = part(gap, ("dv_hi", [P, 2, T], F32R), ("dv_lo", [P, 2, T], F32R))
        assert top <= top_strips - SLAB
        (sq_hi, sq_lo, sv_hi, sv_lo, s_prob, s_pt_hi, s_pt_lo, _) = part(
            top_strips, ("sq_hi", [P, 4, T], F32R), ("sq_lo", [P, 4, T], F32R), ("sv_hi", [P, 8, 3 * 64], F32R),
            ("sv_lo", [P, 8, 3 * 64], F32R), ("s_prob", [P, 2, BAND.total], F32), ("s_pt_hi", [P, BAND.total], F32R),
            ("s_pt_lo", [P, BAND.total], F32R))
        dq_hi, dq_lo, dk_hi, dk_lo, top = part(
            top_strips, ("dq_hi", [P, 2, T], F32R), ("dq_lo", [P, 2, T], F32R), ("dk_hi", [P, 2, T], F32R),
            ("dk_lo", [P, 2, T], F32R))
        zc, u_pad, conv, yc, _ = part(
            top, ("zc", [P, 2, T], F32), ("u_pad", [P, 2, T + 2], F32), ("conv", [P, 2, T], F32),
            ("yc", [P, 4, T], F32))
        d_prob, d_pt_hi, d_pt_lo, k_raw, _ = part(
            top, ("d_prob", [P, 2, CAUSAL.total], F32), ("d_pt_hi", [P, CAUSAL.total], F32R),
            ("d_pt_lo", [P, CAUSAL.total], F32R), ("k_raw", [P, 2, T], F32))
        h_hi, h_lo, top = part(0, ("h_hi", [P, FF_A, T], F32R), ("h_lo", [P, FF_A, T], F32R))
        proj_b, _ = part(top, ("proj_b", [P, 4, T], F32))
        gate, gconv, silu, ffh, top = part(
            top, ("gate", [P, 2, T + 2], F32), ("gconv", [P, 2, T], F32), ("silu", [P, 2, T], F32),
            ("ffh", [P, 2, T], F32))
        p_raw, p_hi, p_lo, proj_a, _ = part(top, ("p_raw", [P, 2, T], F32), ("p_hi", [P, 2, T], F32R),
                                            ("p_lo", [P, 2, T], F32R), ("proj_a", [P, 4, T], F32))
        gate_in, _ = part(0, ("gate_in", [P, 2, 2, T], F32))
        s_pt_hi, s_pt_lo = (s_pt_hi, s_pt2_hi), (s_pt_lo, s_pt2_lo)
        bias_line = nc.dram_tensor("bias_line", (16, LINE), F32, kind="Internal").ap()
        bias_rows = nc.dram_tensor("bias_rows", (16, P, LINE), F32, kind="Internal").ap()

        landed = [sem(f"landed{s}") for s in range(2)]
        first_landed = [sem(f"first_landed{i}") for i in range(4)]
        first_hi, first_lo = sem("first_hi"), sem("first_lo")
        cast_hi, cast_lo = sem("cast_hi"), sem("cast_lo")
        slab_done = sem("slab_done")
        slab_read = sem("slab_read")
        act_ready = sem("act_ready")
        x_landed = [sem(f"x_landed{i}") for i in range(4)]
        x_hi, x_scaled = sem("x_hi"), sem("x_scaled")
        const_landed, p_landed = sem("const_landed"), sem("p_landed")
        eps_set = sem("eps_set")
        act_link, dve_link = sem("act_link"), sem("dve_link")
        sq_done = sem("sq_done")
        sum_ready, mean_done, mean_ready = sem("sum_ready"), sem("mean_done"), sem("mean_ready")
        half_done, tile_added, centred = sem("half_done"), sem("tile_added"), sem("centred")
        pool_cast = sem("pool_cast")
        tok_sums, var_ready, std_ready = sem("tok_sums"), sem("var_ready"), sem("std_ready")
        tok_ready, spread_done, rstd_ready = sem("tok_ready"), sem("spread_done"), sem("rstd_ready")
        norm_z, norm_hi = sem("norm_z"), sem("norm_hi")
        c_read, c_full, c_split, c_ready = sem("c_read"), sem("c_full"), sem("c_split"), sem("c_ready")
        rope_in, rope_swapped, rope_out, rope_hi, rope_lo = (
            sem("rope_in"), sem("rope_swapped"), sem("rope_out"), sem("rope_hi"), sem("rope_lo"))
        proj_hi = sem("proj_hi")
        relu_done, sqr_done, hid_split = sem("relu_done"), sem("sqr_done"), sem("hid_split")
        line_done, line_ready, line_stored, rows_stored = (sem("line_done"), sem("line_ready"),
                                                           sem("line_stored"), sem("rows_stored"))
        strips_landed = sem("strips_landed")
        v_zeroed, u_zeroed = sem("v_zeroed"), sem("u_zeroed")
        qk_sq, qk_full = sem("qk_sq"), sem("qk_full")
        dil_ready = sem("dil_ready")
        mix_sq, mix_hi = sem("mix_sq"), sem("mix_hi")
        conv_done, silu_done, ffh_done, ffh_hi = sem("conv_done"), sem("silu_done"), sem("ffh_done"), sem("ffh_hi")
        ff_step, h_ready = sem("ff_step"), sem("h_ready")
        proj_half = sem("proj_half")
        p_split, proj_act, sig_done, out_ready, stored = (sem("p_split"), sem("proj_act"), sem("sig_done"),
                                                          sem("out_ready"), sem("stored"))

        class Attention:

            def __init__(self, name, heads, score_banks, trans_bank, ahead):
                self.h, self.score_banks, self.trans_bank, self.ahead = heads, score_banks, trans_bank, ahead
                self.scored = sem(name + "_scored")
                self.biased = sem(name + "_biased")
                self.exped = sem(name + "_exped")
                self.summed = sem(name + "_summed")
                self.normed = sem(name + "_normed")
                self.turned = sem(name + "_turned")
                self.turn_hi = sem(name + "_turn_hi")
                self.turn_lo = sem(name + "_turn_lo")
                self.mixed = sem(name + "_mixed")
                self.out_hi = sem(name + "_out_hi")
                self.out_read = sem(name + "_out_read")
                self.nseg = len(heads.segments)

        pool_normed = sem("pool_normed")
        mla = Attention("mla", CAUSAL, [0, 0], 3, 1)
        swa = Attention("swa", BAND, [2, 0], 4, 2)
        dil = Attention("dil", CAUSAL, [0, 0], 3, 1)

        def col(name, i=0):
            at = VEC[name] + i
            return vec[:, at:at + 1]

        def f32(ap):
            return ap.bitcast(F32)

        def pair(ap2d):
            return ap2d.unsqueeze(1).broadcast_to([P, 2, T])

        def head_values(g, e):
            b = banks(g)
            return ps[:, b:b + 2, :].rearrange("p t (x e c) -> p (t x) e c", e=2, c=64)[:, :, e, :]

        assert all(slab_width(g) == SLAB for g in range(SWA_KV, FFN_A_DOWN))

        def banks(g):
            flip = MLA_OUT <= g < MLP0 or g >= MIX_OUT
            return 2 * ((g + flip) % 2)

        block = ctx.enter_context(nc.Block())

        @block.sync
        def _(sp):
            for i in range(4):
                c = slice(BANK * i, BANK * (i + 1))
                sp.dma_start(stage[0][:, c], slabs[0][:, c]).then_inc(first_landed[i], 16)
            sp.dma_start(stage[1][:, :], slabs[1]).then_inc(landed[1], 16)
            for dst, src in ((stat[0:32, 0:16], rel_bias), (sum2[0:32, 0:LINE], onehot),
                             (sum1[0:16, 0:LINE], line_mask), (vec[:, :], vecs), (mat[:, :, :], mats),
                             (cossin[:, :, :], rope), (strip[:, :], causal)):
                sp.dma_start(dst, src).then_inc(const_landed, 16)
            with sp.Fori(1, SLABS // 2) as n:
                for s in range(2):
                    sp.wait_ge(cast_lo, n * 2 + (s - 1))
                    sp.dma_start(stage[s][:, :], slabs[bass.ds(n * 2 + s, 1)].rearrange("a p w -> p (a w)"))\
                      .then_inc(landed[s], 16)

        @block.gpsimd
        def _(pool):
            nc.gpsimd.memset(eps[:, 0:1], LN_EPS).then_inc(eps_set, 1)
            nc.gpsimd.memset(eps[:, 1:2], RMS_EPS).then_inc(eps_set, 1)
            for p in range(4):
                pool.wait_ge(act_ready, X_IN + 2 * p + 2)
                nc.gpsimd.tensor_scalar(y[:, 2 * p:2 * p + 2, :], y[:, 2 * p:2 * p + 2, :], ALPHA, None,
                                        ALU.mult).then_inc(x_scaled, 1)

            def divide(u):
                h = swa.h
                for i in (2, 3):
                    pool.wait_ge(swa.summed, u + 1)
                    n = 4 * u + i
                    part = s_prob[:, u % 2, h.off[i]:h.off[i] + h.width[i]]
                    nc.gpsimd.tensor_scalar(part, part, rden[:, n:n + 1], None, ALU.mult).then_inc(pool_normed, 1)

            def residual(gen, beta):
                for t in range(KT):
                    pool.wait_ge(act_ready, gen + t + 1)
                    nc.gpsimd.tensor_scalar(y[:, t, :], y[:, t, :], col(beta, t), ALPHA, ALU.add, ALU.mult)\
                        .then_inc(x_scaled, 1)

            def norm_share(n, g):
                pool.wait_ge(mean_ready, n + 1)
                pool.wait_ge(slab_read, g - 1)
                for t in (4, 6):
                    nc.gpsimd.tensor_tensor(y[:, t:t + 2, :], y[:, t:t + 2, :], pair(stat[:, :]), ALU.subtract)\
                        .then_inc(centred, 1)
                if n == 3:
                    for t in range(4):
                        mix_square(t)
                s = g % 2
                pool.wait_ge(cast_hi, g + 1)
                nc.gpsimd.tensor_tensor(w_lo[s][:, :], stage[s][:, :], f32(w_hi[s][:, :]), ALU.subtract)\
                    .then_inc(pool_cast, 1)

            def mix_square(t):
                pool.wait_ge(sq_done, SQUARED["mix"] + t + 1)
                if t == 0:
                    pool.wait_ge(tok_ready, NORM["ln3"])
                    nc.gpsimd.tensor_copy(sum2[:, :], tmp[:, 0, 0, :]).then_inc(mix_sq, 1)
                else:
                    pool.wait_ge(mix_sq, t)
                    nc.gpsimd.tensor_tensor(sum2[:, :], sum2[:, :], tmp[:, t // 2 % 2, t % 2, :], ALU.add)\
                        .then_inc(mix_sq, 1)

            norm_share(0, MLP0 + 1)
            residual(LN_0, "mix_b0")
            norm_share(1, SWA_KV + 1)
            residual(LN_1, "mlp_b0")

            pool.wait_ge(act_ready, LN_1 + 1)
            for v in (sv_hi, sv_lo):
                nc.gpsimd.memset(v[:, :, 64:128].bitcast(F32), 0.0).then_inc(v_zeroed, 1)
            for u in range(16):
                divide(u)
            norm_share(2, MLP1 + 1)
            residual(LN_2, "mix_b1")
            norm_share(3, CONV + 1)
            for t in range(4, KT):
                mix_square(t)
            pool.wait_ge(act_ready, LN_3 + 1)
            nc.gpsimd.memset(u_pad[:, :, 0:2], 0.0).then_inc(u_zeroed, 1)
            pool.wait_ge(act_ready, FFN_X + 1)
            nc.gpsimd.memset(gate[:, :, 0:2], 0.0).then_inc(u_zeroed, 1)

        @block.scalar
        def _(act):
            links = [0]

            def link(ins):
                links[0] += 1
                ins.then_inc(act_link, 1)
                act.wait_ge(act_link, links[0])

            def cast(g, more=0, width=None):
                if g >= SLABS:
                    return
                s, w = g % 2, width or slab_width(g)
                act.wait_ge(landed[s], 16 * (g // 2 + s) + more * 8)
                if g >= 2:
                    act.wait_ge(slab_done, g - 1 + more)
                nc.scalar.activation(w_hi[s][:, 0:w], stage[s][:, 0:w], ACT.Copy).then_inc(cast_hi, 1)

            def root(name, width=4):
                act.wait_ge(var_ready, NORM[name])
                nc.scalar.activation(tok_s[:, 0:width], tok_v[:, 0:width], ACT.Sqrt).then_inc(std_ready, 1)

            def rstd_copy(name, dst, bank):
                act.wait_ge(spread_done, NORM[name])
                nc.scalar.activation(dst[:, :], ps[:, bank, :], ACT.Copy).then_inc(rstd_ready, 1)

            def load_table(func):
                link(nc.scalar.activation(table_mark[:, :], eps[:, 0:1], func))

            def exps(a, prob, u, sink=None):
                h = a.h
                for k, i in enumerate(h.order):
                    n = 4 * (u % 16) + i
                    act.wait_ge(a.biased, 4 * u + k + 1)
                    part = prob[:, u % 2, h.off[i]:h.off[i] + h.width[i]]
                    nc.scalar.activation(part, part, ACT.Exp, scale=-1.0, bias=negmax[:, n:n + 1],
                                         accum_out=rowsum[:, n:n + 1]).then_inc(a.exped, 1)
                if sink is not None:
                    n = 4 * (u % 16)
                    nc.scalar.activation(sinkexp[:, n:n + 4], negmax[:, n:n + 4], ACT.Exp, bias=sink)\
                        .then_inc(a.exped, 1)

            def turn_hi(a, pt_hi, u):
                for n, w in enumerate(a.h.segments):
                    act.wait_ge(a.turned, a.nseg * u + n + 1)
                    if n == 0 and a is not swa and u:
                        act.wait_ge(a.mixed, u)
                    nc.scalar.activation(pt_hi[:, BANK * n:BANK * n + w], ps[:, a.trans_bank + n, 0:w],
                                         ACT.Copy).then_inc(a.turn_hi, 1)



            for p in range(4):
                act.dma_start(y[:, 2 * p:2 * p + 2, :], x_t[:, 2 * p:2 * p + 2, :]).then_inc(x_landed[p], 16)
            act.wait_ge(eps_set, 2)
            load_table(ACT.Copy)
            for p in range(4):
                act.wait_ge(x_landed[p], 16)
                nc.scalar.activation(act_hi[:, 2 * p:2 * p + 2, :], y[:, 2 * p:2 * p + 2, :], ACT.Copy)\
                    .then_inc(x_hi, 1)
                act.wait_ge(first_landed[p], 16)
                c = slice(BANK * p, BANK * (p + 1))
                nc.scalar.activation(w_hi[0][:, c], stage[0][:, c], ACT.Copy)\
                    .then_inc(first_hi if p < 3 else cast_hi, 1)
            cast(1)
            act.wait_ge(line_ready, 1)
            act.dma_start(bias_line, rstd[0:16, 0:LINE]).then_inc(line_stored, 16)
            act.wait_ge(line_stored, 16)
            act.dma_start(bias_rows, bias_line.unsqueeze(1).broadcast_to([16, P, LINE])).then_inc(rows_stored, 16)

            act.wait_ge(const_landed, 16 * 7)
            act.wait_ge(eps_set, 2)
            for j in range(3):
                g = MLA_IN + j
                b = banks(g)
                act.wait_ge(slab_done, g + 1)
                if j < 2:
                    nc.scalar.activation(c_raw[:, 2 * j:2 * j + 2, :], ps[:, b:b + 2, :], ACT.Copy)
                    nc.scalar.activation(tmp[:, j, :, :], ps[:, b:b + 2, :], ACT.Square).then_inc(c_read, 1)
                else:
                    act.wait_ge(c_split, 1)
                    nc.scalar.activation(rope_raw[:, :], ps[:, b + 1, :], ACT.Copy).then_inc(rope_in, 1)
                    nc.scalar.activation(c_raw[:, 4, :], ps[:, b, :], ACT.Copy)
                    nc.scalar.activation(tmp[:, 0, 0, :], ps[:, b, :], ACT.Square).then_inc(c_read, 1)
                cast(g + 2)
            root("mla", 8)
            for t in range(5):
                act.wait_ge(c_full, t + 1)
                nc.scalar.activation(c_hi[:, t, :], c_raw[:, t, :], ACT.Copy).then_inc(c_split, 1)
            act.wait_ge(rope_out, 1)
            nc.scalar.activation(kr_hi[:, :], rope_cos[:, :], ACT.Copy).then_inc(rope_hi, 1)

            for half in range(2):
                g = MLA_HALF + 4 * half
                for p in range(2):
                    b = 4 * p
                    act.wait_ge(slab_done, g + p + 1)
                    n = 1 + 2 * half + p
                    act.wait_ge(rope_out, n)
                    nc.scalar.activation(rope_raw[:, :], ps[:, b + 2, :], ACT.Copy, scale=MLA_SCALE)\
                        .then_inc(rope_in, 1)
                    nc.scalar.activation(act_hi[:, 4 + 2 * p:6 + 2 * p, :], ps[:, b:b + 2, :], ACT.Copy,
                                         scale=MLA_SCALE).then_inc(proj_hi, 1)
                    cast(g + p + 2)
                    act.wait_ge(rope_out, n + 1)
                    nc.scalar.activation(qr_hi[:, p, :], rope_cos[:, :], ACT.Copy).then_inc(rope_hi, 1)
                for p, dst in ((2, kn_hi), (3, mv_hi)):
                    b = 4 * (p - 2)
                    act.wait_ge(slab_done, g + p + 1)
                    for q in range(2):
                        nc.scalar.activation(dst[:, 2 * q:2 * q + 2, :], ps[:, b + 2 * q:b + 2 * q + 2, :],
                                             ACT.Copy).then_inc(proj_hi, 1)
                    if p == 2:
                        cast(g + 4)
                        load_table(ACT.Exp)
                def mla_out(u):
                    act.wait_ge(mla.mixed, u + 1)
                    nc.scalar.activation(act_hi[:, u, :], ps[:, 6 + u % 2, :], ACT.Copy).then_inc(mla.out_hi, 1)

                u0 = 4 * half
                exps(mla, m_prob, u0)
                for u in range(u0, u0 + 4):
                    if u < u0 + 3:
                        exps(mla, m_prob, u + 1)
                    turn_hi(mla, m_pt_hi, u)
                    if u > u0:
                        mla_out(u - 1)
                cast(g + 5)
                mla_out(u0 + 3)

            def load_bias(half):
                act.dma_start(strips[:, :].rearrange("p (h j) -> p h j", h=8),
                              bass.AP(bias_rows.tensor, 8 * half * P * LINE + P - 1,
                                      [[LINE - 1, P], [P * LINE, 8], [1, 2 * P]])).then_inc(strips_landed, 16)

            def last_squares(first, n):
                for j in range(3):
                    act.wait_ge(slab_read, first + j + 1)
                    nc.scalar.activation(tmp[:, j % 2, :, :], y[:, 2 * j:2 * j + 2, :], ACT.Square)\
                        .then_inc(sq_done, 1)
                    cast(first + j + 2)
                load_table(ACT.Sqrt)
                act.wait_ge(tile_added, n + 1)
                nc.scalar.activation(tmp[:, 1, 0, :], y[:, 6, :], ACT.Square).then_inc(sq_done, 1)
                act.wait_ge(slab_read, first + 4)
                nc.scalar.activation(tmp[:, 1, 1, :], y[:, 7, :], ACT.Square).then_inc(sq_done, 1)
                root(f"ln{n}")
                act.wait_ge(mean_done, n + 1)
                nc.scalar.activation(stat[:, :], ps[:, 4, :], ACT.Copy).then_inc(mean_ready, 1)
                cast(first + 5)

            def layer_norm(n, beta):
                for t in range(KT):
                    act.wait_ge(norm_z, 8 * n + t + 1)
                    nc.scalar.activation(act_hi[:, t, :], y[:, t, :], ACT.Identity, bias=col(beta, t))\
                        .then_inc(norm_hi, 1)

            def mlp(first, layer):
                def up(j, more, done):
                    g = first + j
                    b = banks(g)
                    act.wait_ge(slab_done, g + 1 + more)
                    act.wait_ge(slab_read, g - 1 + more)
                    nc.scalar.activation(relu[:, j % 2, :, :], ps[:, b:b + 2, :], ACT.Relu).then_inc(relu_done, 1)
                    act.wait_ge(sqr_done, done + j + 1)
                    nc.scalar.activation(hid_hi[:, 2 * j:2 * j + 2, :], relu[:, j % 2, :, :], ACT.Copy)\
                        .then_inc(hid_split, 1)
                    cast(g + 2, more)

                with act.Fori(0, 3) as r:
                    for j in range(4):
                        up(j, r * 8, r * 4 + 16 * layer)
                    for j in range(4, 8):
                        cast(first + j + 2, r * 8)
                for j in range(4):
                    up(j, 24, 12 + 16 * layer)
                last_squares(first + 28, 2 * layer + 1)

            last_squares(MLA_OUT, 0)
            layer_norm(0, "mix_b0")
            act.wait_ge(rows_stored, 16)
            load_bias(0)
            mlp(MLP0, 0)
            layer_norm(1, "mlp_b0")

            g = SWA_KV
            act.wait_ge(slab_done, g + 1)
            nc.scalar.activation(swa_k_hi[:, :, :], ps[:, banks(g):banks(g) + 2, :], ACT.Copy).then_inc(proj_hi, 1)
            cast(g + 2)
            act.wait_ge(slab_done, g + 2)
            for e in range(2):
                ins = nc.scalar.activation(sv_hi[:, :, 128 * e:128 * e + 64], head_values(g + 1, e), ACT.Copy)
            ins.then_inc(proj_hi, 1)
            cast(g + 3)
            for half in range(2):
                g = SWA_Q + 2 * half
                if half:
                    act.wait_ge(swa.biased, 32)
                    load_bias(1)
                for p in range(2):
                    b = banks(g + p)
                    act.wait_ge(slab_done, g + p + 1)
                    nc.scalar.activation(sq_hi[:, 2 * p:2 * p + 2, :], ps[:, b:b + 2, :], ACT.Copy,
                                         scale=HEAD_SCALE).then_inc(proj_hi, 1)
                    if p == 0:
                        cast(g + 2)
                        load_table(ACT.Exp)
                u0 = 8 * half
                for u in (u0, u0 + 1):
                    exps(swa, s_prob, u, col("sink", u))

                def swa_out(t):
                    act.wait_ge(swa.mixed, t + 1)
                    nc.scalar.activation(o_hi[:, t, :], ps[:, 6 + t % 2, :], ACT.Copy).then_inc(swa.out_hi, 1)

                for u in range(u0, u0 + 8):
                    turn_hi(swa, s_pt_hi[u % 2], u)
                    if u + 2 < u0 + 8:
                        exps(swa, s_prob, u + 2, col("sink", u + 2))
                    if u % 2 == 0 and u > u0:
                        swa_out(u // 2 - 1)
                cast(g + 3)
                swa_out(u0 // 2 + 3)

            act.wait_ge(swa.biased, 64)
            act.dma_start(strips[:, :], dilated[0]).then_inc(strips_landed, 16)
            last_squares(SWA_OUT, 2)
            layer_norm(2, "mix_b1")
            mlp(MLP1, 1)

            for t in range(KT):
                act.wait_ge(norm_z, 24 + t + 1)
                link(nc.scalar.activation(y[:, t, :], y[:, t, :], ACT.Identity, bias=col("mlp_b1", t)))
                nc.scalar.activation(act_hi[:, t, :], y[:, t, :], ACT.Copy, scale=col("g_mix", t))\
                    .then_inc(norm_hi, 1)
                if t >= 4:
                    act.wait_ge(mix_sq, t - 3)
                nc.scalar.activation(tmp[:, t // 2 % 2, t % 2, :], y[:, t, :], ACT.Square).then_inc(sq_done, 1)

            root("mix")
            rstd_copy("mix", rstd, 6)
            for i in range(2):
                for j in range(3):
                    cast(CONV + 3 * i + j + 2)
                act.wait_ge(conv_done, i + 1)
                nc.scalar.activation(tmp[:, 1, :, :], yc[:, 2 * i:2 * i + 2, :], ACT.Square).then_inc(sq_done, 1)
            root("conv")

            def conv_hi(t):
                act.wait_ge(conv_done, 2 + t + 1)
                nc.scalar.activation(o_hi[:, t, :], yc[:, t, :], ACT.Copy).then_inc(mix_hi, 1)

            for half in range(2):
                g = DIL_HALF + 3 * half
                if half:
                    act.wait_ge(dil.biased, 16)
                    act.dma_start(strips[:, :], dilated[1]).then_inc(strips_landed, 16)
                for p, (dst, raw, scale) in enumerate(((dq_hi, tmp[:, 0, :, :], HEAD_SCALE),
                                                       (dk_hi, k_raw[:, :, :], 1.0))):
                    n = 2 * half + p
                    act.wait_ge(slab_read, g + p + 1)
                    nc.scalar.activation(tmp[:, 1, :, :], raw, ACT.Square).then_inc(qk_sq, 1)
                    cast(g + p + 2)
                    root("qk"[p] + str(half), 16)
                    if n == 0:
                        conv_hi(0)
                        conv_hi(1)
                        conv_hi(2)
                    act.wait_ge(qk_full, n + 1)
                    nc.scalar.activation(dst[:, :, :], raw, ACT.Copy, scale=scale).then_inc(proj_hi, 1)
                    if n == 0:
                        conv_hi(3)
                load_table(ACT.Exp)
                act.wait_ge(slab_read, g + 3)
                nc.scalar.activation(dv_hi[:, :, :], tmp[:, 0, :, :], ACT.Copy).then_inc(proj_hi, 1)
                u0 = 4 * half

                def dil_out(u):
                    r, t = 64 * (u % 2), u // 2
                    act.wait_ge(dil.mixed, u + 1)
                    nc.scalar.activation(o_hi[r:r + 64, 4 + t, :], ps[r:r + 64, 6 + u % 2, :], ACT.Copy,
                                         scale=vec[r:r + 64, VEC["g_oa"] + t:VEC["g_oa"] + t + 1])\
                        .then_inc(dil.out_hi, 1)
                    if t >= 1:
                        act.wait_ge(mix_sq, 8 + t)
                    nc.scalar.activation(stat[r:r + 64, :], ps[r:r + 64, 6 + u % 2, :], ACT.Square)\
                        .then_inc(sq_done, 1)

                exps(dil, d_prob, u0)
                for u in range(u0, u0 + 4):
                    if u + 1 < u0 + 4:
                        exps(dil, d_prob, u + 1)
                    turn_hi(dil, d_pt_hi, u)
                    if u > u0:
                        dil_out(u - 1)
                cast(g + 4)
                dil_out(u0 + 3)

            def rms_out(g, tiles, n, gain):
                act.wait_ge(slab_read, g + 1)
                for t in tiles:
                    nc.scalar.activation(act_hi[:, t, :], y[:, t, :], ACT.Copy, scale=col(gain, t))\
                        .then_inc(mix_hi, 1)
                nc.scalar.activation(tmp[:, n % 2, 0:len(tiles), :], y[:, tiles[0]:tiles[-1] + 1, :],
                                     ACT.Square).then_inc(sq_done, 1)

            root("attn")
            rstd_copy("attn", stat, 2)
            for j in range(4):
                rms_out(MIX_OUT + j, [2 * j, 2 * j + 1], j, "g_ffn")
                cast(MIX_OUT + j + 2)

            act.wait_ge(slab_read, FFN_A)
            act.dma_start(p_raw[:, :, :], ple_t).then_inc(p_landed, 16)
            root("ffn")
            load_table(ACT.Silu)
            rstd_copy("ffn", rstd, 7)
            for rnd, (first, down, before, count) in enumerate(((FFN_A, FFN_A_DOWN, 0, FF_A),
                                                                (FFN_B, FFN_B_DOWN, FF_A, FF_B))):
                with act.Fori(0, count // 2) as i:
                    for b in range(2):
                        cast(first + b + 2, i * 2, SLAB)
                        act.wait_ge(conv_done, 6 + before + b + 1 + i * 2)
                        nc.scalar.activation(silu[:, b, :], gconv[:, b, :], ACT.Silu).then_inc(silu_done, 1)
                        act.wait_ge(ffh_done, before + b + 1 + i * 2)
                        nc.scalar.activation(h_hi[:, bass.ds(i * 2 + b, 1), :], ffh[:, b:b + 1, :], ACT.Copy)\
                            .then_inc(ffh_hi, 1)
                if rnd == 0:
                    for j in range(8):
                        cast(down + j + 2)
                    act.wait_ge(p_landed, 16)
                    nc.scalar.activation(p_hi[:, :, :], p_raw[:, :, :], ACT.Copy).then_inc(p_split, 1)

            act.wait_ge(proj_half, 1)
            for q in range(2):
                last = nc.scalar.activation(proj_a[:, 2 * q:2 * q + 2, :], ps[:, 2 * q:2 * q + 2, :], ACT.Copy)
            last.then_inc(proj_act, 1)
            cast(PLE_PROJ + 2)
            load_table(ACT.Sqrt)
            for j in range(8):
                rms_out(FFN_B_DOWN + j, [j], j, "g_ple")
                cast(FFN_B_DOWN + j + 2)

            root("ple")
            load_table(ACT.Sigmoid)
            rstd_copy("ple", rstd, 7)
            for j in range(4):
                act.wait_ge(slab_read, PLE_GATE + j + 1)
                nc.scalar.activation(gate_in[:, j % 2, :, :], gate_in[:, j % 2, :, :], ACT.Sigmoid)\
                    .then_inc(sig_done, 1)
                cast(PLE_GATE + j + 2)
                act.wait_ge(out_ready, j + 1)
                act.dma_start(out[:, 2 * j:2 * j + 2, :], y[:, 2 * j:2 * j + 2, :]).then_inc(stored, 16)
            act.wait_ge(stored, 16 * 4)
            act.wait_ge(rows_stored, 16)


        @block.vector
        def _(dve):
            links = [0]

            def link(ins):
                links[0] += 1
                ins.then_inc(dve_link, 1)
                dve.wait_ge(dve_link, links[0])

            def split(dst, src, hi):
                return nc.vector.tensor_tensor(dst, src, f32(hi), ALU.subtract)

            def split_scaled(dst, src, scale, hi, op=ALU.mult):
                return nc.vector.scalar_tensor_tensor(dst, src, scale, f32(hi), op, ALU.subtract)

            def cast(g, more=0, width=None):
                if g >= SLABS:
                    return
                s, w = g % 2, width or slab_width(g)
                dve.wait_ge(cast_hi, g + 1 + more)
                split(w_lo[s][:, 0:w], stage[s][:, 0:w], w_hi[s][:, 0:w]).then_inc(cast_lo, 1)

            def mean_squares(name, bank, scale, width=4):
                dve.wait_ge(tok_sums, NORM[name])
                nc.vector.tensor_scalar(tok_v[:, 0:width], ps[:, bank, 0:width], float(scale), RMS_EPS, ALU.mult,
                                        ALU.add).then_inc(var_ready, 1)

            def invert_root(name, width=4):
                v, s, r, q = (x[:, 0:width] for x in (tok_v, tok_s, tok_r, tok_q))
                dve.wait_ge(std_ready, NORM[name])
                if name in ("mix", "attn", "ffn", "ple"):
                    dve.wait_ge(spread_done, NORM[name] - 1)
                link(nc.vector.reciprocal(r, s))
                link(nc.vector.scalar_tensor_tensor(q, r, -0.5, r, ALU.mult, ALU.mult))
                link(nc.vector.tensor_tensor(q, q, v, ALU.mult))
                nc.vector.scalar_tensor_tensor(r, q, 1.5, r, ALU.add, ALU.mult).then_inc(tok_ready, 1)

            def bias(a, prob, u, table, floor=None):
                h, at = a.h, a.score_banks[u % 2]
                if u >= 2:
                    dve.wait_ge(a.turned, a.nseg * (u - 1))
                k = 0
                for m, group in enumerate(h.groups):
                    dve.wait_ge(a.scored, len(h.groups) * u + m + 1)
                    for i in group:
                        bank, c = h.place[i]
                        w, n = h.width[i], 4 * (u % 16) + i
                        nc.vector.tensor_tensor_reduce(
                            prob[:, u % 2, h.off[i]:h.off[i] + w], ps[:, at + bank, c:c + w], table(w),
                            -1.0, HUGE if floor is None else floor, ALU.add, ALU.min,
                            negmax[:, n:n + 1]).then_inc(a.biased, 1)
                        k += 1

            def divide(a, prob, u, sink=False):
                h, n = a.h, 4 * (u % 16)
                if sink:
                    dve.wait_ge(a.exped, 5 * u + 5)
                    link(nc.vector.tensor_tensor(rowsum[:, n:n + 4], rowsum[:, n:n + 4], sinkexp[:, n:n + 4],
                                                 ALU.add))
                else:
                    dve.wait_ge(a.exped, 4 * u + 4)
                nc.vector.reciprocal(rden[:, n:n + 4], rowsum[:, n:n + 4]).then_inc(a.summed, 1)
                dve.wait_ge(a.summed, u + 1)
                for i in h.order[:2 if sink else 4]:
                    part = prob[:, u % 2, h.off[i]:h.off[i] + h.width[i]]
                    nc.vector.tensor_scalar(part, part, rden[:, n + i:n + i + 1], None, ALU.mult)\
                        .then_inc(a.normed, 1)

            def turn_lo(a, pt_hi, pt_lo, u):
                for n, w in enumerate(a.h.segments):
                    dve.wait_ge(a.turn_hi, a.nseg * u + n + 1)
                    split(pt_lo[:, BANK * n:BANK * n + w], ps[:, a.trans_bank + n, 0:w],
                          pt_hi[:, BANK * n:BANK * n + w]).then_inc(a.turn_lo, 1)

            def sums(tiles, squares, squared, first, last, with_mean):
                for dst, parts, wait in ((sum1, [y[:, t, :] for t in tiles], False), (sum2, squares, True)):
                    if dst is sum1 and not with_mean:
                        continue
                    if wait:
                        dve.wait_ge(sq_done, squared)
                    if first and len(parts) == 2:
                        ins = nc.vector.tensor_tensor(dst[:, :], parts[0], parts[1], ALU.add)
                        parts = []
                    elif first:
                        ins = nc.vector.tensor_copy(dst[:, :], parts[0])
                        parts = []
                    for k, part in enumerate(parts):
                        ins = nc.vector.tensor_tensor(dst[:, :], dst[:, :], part, ALU.add)
                        if k < len(parts) - 1:
                            link(ins)
                    if last:
                        ins.then_inc(sum_ready, 1)
                    else:
                        link(ins)

            def add_out(g, t, more=0):
                b = banks(g)
                dve.wait_ge(slab_done, g + 1 + more)
                nc.vector.tensor_tensor(y[:, t:t + 2, :], y[:, t:t + 2, :], ps[:, b:b + 2, :], ALU.add)\
                    .then_inc(slab_read, 1)

            def last_out(first, n):
                for j in range(3):
                    add_out(first + j, 2 * j)
                    dve.wait_ge(slab_read, first + j + 1)
                    sums([2 * j, 2 * j + 1], [tmp[:, j % 2, k, :] for k in range(2)], 5 * n + j + 1, j == 0, False,
                         True)
                    cast(first + j + 2)
                b = banks(first + 3)
                dve.wait_ge(half_done, n + 1)
                nc.vector.tensor_tensor(y[:, 6, :], y[:, 6, :], ps[:, b, :], ALU.add).then_inc(tile_added, 1)
                dve.wait_ge(tile_added, n + 1)
                sums([6], [tmp[:, 1, 0, :]], 5 * n + 4, False, False, True)
                dve.wait_ge(slab_done, first + 4)
                nc.vector.tensor_tensor(y[:, 7, :], y[:, 7, :], ps[:, b + 1, :], ALU.add).then_inc(slab_read, 1)
                dve.wait_ge(slab_read, first + 4)
                sums([7], [tmp[:, 1, 1, :]], 5 * n + 5, False, True, True)

            def layer_norm(n, gain, beta, last=False):
                def centre(p):
                    return nc.vector.tensor_tensor(y[:, 2 * p:2 * p + 2, :], y[:, 2 * p:2 * p + 2, :],
                                                   pair(stat[:, :]), ALU.subtract)

                def lo(t):
                    dve.wait_ge(norm_hi, 8 * n + t + 1)
                    if last:
                        split_scaled(act_lo[:, t, :], y[:, t, :], col("g_mix", t), act_hi[:, t, :])\
                            .then_inc(act_ready, 1)
                    else:
                        split_scaled(act_lo[:, t, :], y[:, t, :], col(beta, t), act_hi[:, t, :], ALU.add)\
                            .then_inc(act_ready, 1)

                v, q = tok_v[:, 0:4], tok_q[:, 0:4]
                dve.wait_ge(tok_sums, NORM[f"ln{n}"])
                link(nc.vector.tensor_copy(q, ps[:, 5, 0:4]))
                link(nc.vector.tensor_tensor(q, q, q, ALU.mult))
                link(nc.vector.tensor_tensor(v, ps[:, 5, 4:8], q, ALU.subtract))
                nc.vector.tensor_scalar(v, v, 0.0, LN_EPS, ALU.max, ALU.add).then_inc(var_ready, 1)
                invert_root(f"ln{n}")
                dve.wait_ge(mean_ready, n + 1)
                link(centre(0))
                link(centre(1))
                dve.wait_ge(spread_done, NORM[f"ln{n}"])
                for t in range(KT):
                    if t in (4, 6):
                        dve.wait_ge(centred, 2 * n + t // 2 - 1)
                    nc.vector.scalar_tensor_tensor(y[:, t, :], y[:, t, :], col(gain, t), ps[:, 5, :],
                                                   ALU.mult, ALU.mult).then_inc(norm_z, 1)

                    if t:
                        lo(t - 1)
                    if t == (7 if last else 6):
                        dve.wait_ge(pool_cast, n + 1)
                        nc.vector.tensor_copy(mark[:, :], eps[:, 0:1]).then_inc(cast_lo, 1)
                lo(KT - 1)

            def mlp(first, layer, scaled):
                def up(j, more, done):
                    dve.wait_ge(relu_done, done + j + 1)
                    nc.vector.tensor_tensor(relu[:, j % 2, :, :], relu[:, j % 2, :, :], relu[:, j % 2, :, :],
                                            ALU.mult).then_inc(sqr_done, 1)
                    dve.wait_ge(hid_split, done + j + 1)
                    split(hid_lo[:, 2 * j:2 * j + 2, :], relu[:, j % 2, :, :], hid_hi[:, 2 * j:2 * j + 2, :])\
                        .then_inc(slab_read, 1)
                    cast(first + j + 2, more)

                dve.wait_ge(x_scaled, scaled)
                with dve.Fori(0, 3) as r:
                    for j in range(4):
                        up(j, r * 8, r * 4 + 16 * layer)
                    for j in range(4):
                        add_out(first + 4 + j, 2 * j, r * 8)
                        cast(first + 4 + j + 2, r * 8)
                for j in range(4):
                    up(j, 24, 12 + 16 * layer)
                last_out(first + 28, 2 * layer + 1)



            for p in range(4):
                dve.wait_ge(x_hi, p + 1)
                split(act_lo[:, 2 * p:2 * p + 2, :], y[:, 2 * p:2 * p + 2, :], act_hi[:, 2 * p:2 * p + 2, :])\
                    .then_inc(act_ready, 2)
                if p < 3:
                    dve.wait_ge(first_hi, p + 1)
                else:
                    dve.wait_ge(cast_hi, 1)
                c = slice(BANK * p, BANK * (p + 1))
                split(w_lo[0][:, c], stage[0][:, c], w_hi[0][:, c]).then_inc(first_lo if p < 3 else cast_lo, 1)
            cast(1)
            dve.wait_ge(const_landed, 16 * 7)
            dve.wait_ge(line_done, 1)
            nc.vector.tensor_tensor(rstd[0:16, 0:LINE], ps[0:16, 7, 0:LINE], sum1[0:16, 0:LINE], ALU.add)\
                .then_inc(line_ready, 1)
            nc.vector.tensor_scalar(negsink[:, :], vec[:, VEC["sink"]:VEC["sink"] + 16], -1.0, None, ALU.mult)

            def rope_rotate(n):
                dve.wait_ge(rope_in, n + 1)
                if n:
                    dve.wait_ge(rope_lo, n)
                nc.vector.tensor_tensor(rope_cos[:, :], rope_raw[:, :], cossin[:, 0, :], ALU.mult)
                dve.wait_ge(rope_swapped, n + 1)
                bank = (6, 3, 7, 3, 7)[n]
                link(nc.vector.tensor_tensor(rope_sin[:, :], ps[:, bank, :], cossin[:, 1, :], ALU.mult))
                nc.vector.tensor_tensor(rope_cos[:, :], rope_cos[:, :], rope_sin[:, :], ALU.add)\
                    .then_inc(rope_out, 1)

            dve.wait_ge(line_done, 1)
            dve.wait_ge(c_read, 1)
            link(nc.vector.tensor_tensor(sum1[:, :], tmp[:, 0, 0, :], tmp[:, 0, 1, :], ALU.add))
            nc.vector.tensor_copy(mark[:, :], sum1[:, 0:1]).then_inc(c_split, 1)
            nc.vector.tensor_copy(negmax[:, 1:2], sum1[:, 0:1]).then_inc(slab_read, 1)
            cast(2)
            dve.wait_ge(slab_read, 1)
            dve.wait_ge(c_read, 2)
            nc.vector.tensor_tensor(sum1[:, :], sum1[:, :], tmp[:, 1, 0, :], ALU.add).then_inc(sum_ready, 1)
            nc.vector.tensor_copy(sum2[:, :], tmp[:, 1, 1, :]).then_inc(slab_read, 1)
            cast(3)
            dve.wait_ge(slab_read, 2)
            dve.wait_ge(c_read, 3)
            nc.vector.tensor_tensor(sum2[:, :], sum2[:, :], tmp[:, 0, 0, :], ALU.add).then_inc(sum_ready, 1)
            nc.vector.tensor_copy(negmax[:, 0:1], tmp[:, 0, 0, 0:1]).then_inc(slab_read, 1)
            dve.wait_ge(tok_sums, NORM["mla"])
            for at, scale in ((0, D / Q_RANK), (4, D / KV_RANK)):
                ins = nc.vector.tensor_scalar(tok_v[:, at:at + 4], ps[:, 4, at:at + 4], float(scale), RMS_EPS,
                                              ALU.mult, ALU.add)
            ins.then_inc(var_ready, 1)
            invert_root("mla", 8)
            dve.wait_ge(spread_done, NORM["mla"])
            for t in range(5):
                bank, gain = (4, col("g_q", t)) if t < 3 else (5, col("g_kv", t - 3))
                nc.vector.scalar_tensor_tensor(c_raw[:, t, :], c_raw[:, t, :], gain, ps[:, bank, :],
                                               ALU.mult, ALU.mult).then_inc(c_full, 1)
                if t:
                    dve.wait_ge(c_split, 1 + t)
                    split(c_lo[:, t - 1, :], c_raw[:, t - 1, :], c_hi[:, t - 1, :]).then_inc(c_ready, 1)
            dve.wait_ge(c_split, 6)
            split(c_lo[:, 4, :], c_raw[:, 4, :], c_hi[:, 4, :]).then_inc(c_ready, 1)
            cast(4)
            rope_rotate(0)
            dve.wait_ge(rope_hi, 1)
            split(kr_lo[:, :], rope_cos[:, :], kr_hi[:, :]).then_inc(rope_lo, 1)

            for half in range(2):
                g = MLA_HALF + 4 * half
                for p in range(2):
                    n = 6 * half + p
                    dve.wait_ge(proj_hi, n + 1)
                    split_scaled(act_lo[:, 4 + 2 * p:6 + 2 * p, :], ps[:, 4 * p:4 * p + 2, :], MLA_SCALE,
                                 act_hi[:, 4 + 2 * p:6 + 2 * p, :]).then_inc(slab_read, 1)
                    cast(g + p + 2)
                    rope_rotate(1 + 2 * half + p)
                    dve.wait_ge(rope_hi, 2 + 2 * half + p)
                    split(qr_lo[:, p, :], rope_cos[:, :], qr_hi[:, p, :]).then_inc(rope_lo, 1)
                for p, hi, lo in ((2, kn_hi, kn_lo), (3, mv_hi, mv_lo)):
                    for q in range(2):
                        n = 6 * half + 2 * p - 2 + q
                        dve.wait_ge(proj_hi, n + 1)
                        b = 4 * (p - 2) + 2 * q
                        ins = split(lo[:, 2 * q:2 * q + 2, :], ps[:, b:b + 2, :], hi[:, 2 * q:2 * q + 2, :])
                    ins.then_inc(slab_read, 1)
                    if p == 2:
                        cast(g + 4)

                def mla_bias(u):
                    bias(mla, m_prob, u, lambda w: strip[:, T - w:T])
                    divide(mla, m_prob, u)

                def mla_out(u):
                    dve.wait_ge(mla.out_hi, u + 1)
                    split(act_lo[:, u, :], ps[:, 6 + u % 2, :], act_hi[:, u, :]).then_inc(act_ready, 1)

                u0 = 4 * half
                mla_bias(u0)
                for u in range(u0, u0 + 4):
                    if u < u0 + 3:
                        mla_bias(u + 1)
                    turn_lo(mla, m_pt_hi, m_pt_lo, u)
                    if u > u0:
                        mla_out(u - 1)
                cast(g + 5)
                mla_out(u0 + 3)

            dve.wait_ge(x_scaled, 4)
            last_out(MLA_OUT, 0)
            layer_norm(0, "mix_g0", "mix_b0")
            mlp(MLP0, 0, 12)
            layer_norm(1, "mlp_g0", "mlp_b0")

            g = SWA_KV
            dve.wait_ge(proj_hi, 12 + 1)
            split(swa_k_lo[:, :, :], ps[:, banks(g):banks(g) + 2, :], swa_k_hi[:, :, :]).then_inc(slab_read, 1)
            cast(g + 2)
            dve.wait_ge(proj_hi, 12 + 2)
            for e in range(2):
                c = slice(128 * e, 128 * e + 64)
                ins = split(sv_lo[:, :, c], head_values(g + 1, e), sv_hi[:, :, c])
            ins.then_inc(slab_read, 1)
            cast(g + 3)
            for half in range(2):
                g = SWA_Q + 2 * half
                for p in range(2):
                    b = banks(g + p)
                    dve.wait_ge(proj_hi, 14 + 2 * half + p + 1)
                    split_scaled(sq_lo[:, 2 * p:2 * p + 2, :], ps[:, b:b + 2, :], HEAD_SCALE,
                                 sq_hi[:, 2 * p:2 * p + 2, :]).then_inc(slab_read, 1)
                    if p == 0:
                        cast(g + 2)
                dve.wait_ge(strips_landed, 16 * (half + 1))
                u0 = 8 * half

                def swa_bias(u):
                    c = 2 * P * (u % 8)
                    bias(swa, s_prob, u, lambda w: strips[:, c + 2 * P - w:c + 2 * P], negsink[:, u:u + 1])


                swa_bias(u0)
                swa_bias(u0 + 1)
                divide(swa, s_prob, u0, True)
                def swa_out(t):
                    dve.wait_ge(swa.out_hi, t + 1)
                    split(o_lo[:, t, :], ps[:, 6 + t % 2, :], o_hi[:, t, :]).then_inc(act_ready, 1)

                for u in range(u0, u0 + 8):
                    if u + 1 < u0 + 8:
                        divide(swa, s_prob, u + 1, True)
                    turn_lo(swa, s_pt_hi[u % 2], s_pt_lo[u % 2], u)
                    if u + 2 < u0 + 8:
                        swa_bias(u + 2)
                    if u % 2 == 0 and u > u0:
                        swa_out(u // 2 - 1)
                cast(g + 3)
                swa_out(u0 // 2 + 3)

            dve.wait_ge(x_scaled, 20)
            last_out(SWA_OUT, 2)
            layer_norm(2, "mix_g1", "mix_b1")
            mlp(MLP1, 1, 28)
            layer_norm(3, "mlp_g1", "mlp_b1", True)

            mean_squares("mix", 6, 1.0)
            invert_root("mix")
            dve.wait_ge(tok_ready, NORM["mix"])
            nc.vector.tensor_copy(rstd_tok[:, :], tok_r[:, 0:4])
            dve.wait_ge(rstd_ready, RSTD["mix"])
            dve.wait_ge(u_zeroed, 1)
            for i in range(2):
                g = CONV + 3 * i
                for j, dst in ((0, zc[:, :, :]), (1, tmp[:, 0, :, :]), (2, yc[:, 2 * i:2 * i + 2, :])):
                    b = banks(g + j)
                    dve.wait_ge(slab_done, g + j + 1)
                    nc.vector.tensor_tensor(dst, ps[:, b:b + 2, :], pair(rstd[:, :]), ALU.mult)\
                        .then_inc(slab_read, 1)
                    cast(g + j + 2)
                    dve.wait_ge(slab_read, g + j + 1)
                    if j == 1:
                        link(nc.vector.tensor_tensor(u_pad[:, :, 2:T + 2], tmp[:, 0, :, :], zc[:, :, :], ALU.mult))
                        for k in range(2):
                            c, t = conv[:, k, :], 2 * i + k
                            link(nc.vector.tensor_scalar(c, u_pad[:, k, 2:T + 2], col("conv_w", 8 + t),
                                                         col("conv_b", t), ALU.mult, ALU.add))
                            link(nc.vector.scalar_tensor_tensor(c, u_pad[:, k, 1:T + 1], col("conv_w", 4 + t), c,
                                                                ALU.mult, ALU.add))
                            link(nc.vector.scalar_tensor_tensor(c, u_pad[:, k, 0:T], col("conv_w", t), c,
                                                                ALU.mult, ALU.add))
                nc.vector.tensor_tensor(yc[:, 2 * i:2 * i + 2, :], yc[:, 2 * i:2 * i + 2, :], conv[:, :, :],
                                        ALU.mult).then_inc(conv_done, 1)
                dve.wait_ge(sq_done, SQUARED["conv"] + i + 1)
                if i:
                    link(nc.vector.tensor_tensor(sum1[:, :], sum1[:, :], tmp[:, 1, 0, :], ALU.add))
                    nc.vector.tensor_tensor(sum1[:, :], sum1[:, :], tmp[:, 1, 1, :], ALU.add).then_inc(sum_ready, 1)
                else:
                    link(nc.vector.tensor_tensor(sum1[:, :], tmp[:, 1, 0, :], tmp[:, 1, 1, :], ALU.add))
            mean_squares("conv", 7, 2.0)
            invert_root("conv")

            for half in range(2):
                g = DIL_HALF + 3 * half
                n = 18 + 3 * half
                parts = ((dq_hi, dq_lo, tmp[:, 0, :, :], HEAD_SCALE, "qn_g"),
                         (dk_hi, dk_lo, k_raw[:, :, :], 1.0, "kn_g"))

                def conv_out(t):
                    nc.vector.scalar_tensor_tensor(yc[:, t, :], yc[:, t, :], col("g_oc", t), ps[:, 7, :],
                                                   ALU.mult, ALU.mult).then_inc(conv_done, 1)
                    dve.wait_ge(mix_hi, t + 1)
                    split(o_lo[:, t, :], yc[:, t, :], o_hi[:, t, :]).then_inc(act_ready, 1)

                def qk_out(p):
                    b = banks(g + p)
                    dve.wait_ge(slab_done, g + p + 1)
                    nc.vector.tensor_tensor(parts[p][2], ps[:, b:b + 2, :], pair(rstd[:, :]), ALU.mult)\
                        .then_inc(slab_read, 1)
                    cast(g + p + 2)

                def qk_full_out(p):
                    _, _, raw, _, gain = parts[p]
                    b = 4 + 2 * p
                    dve.wait_ge(spread_done, NORM["qk"[p] + str(half)])
                    nc.vector.scalar_tensor_tensor(raw, raw, col(gain), ps[:, b:b + 2, :], ALU.mult, ALU.mult)\
                        .then_inc(qk_full, 1)

                def qk_lo(p):
                    hi, lo, raw, scale, _ = parts[p]
                    dve.wait_ge(proj_hi, n + p + 1)
                    split_scaled(lo[:, :, :], raw, scale, hi[:, :, :]).then_inc(dil_ready, 1)

                def v_out():
                    b = banks(g + 2)
                    dve.wait_ge(slab_done, g + 3)
                    nc.vector.tensor_tensor(tmp[:, 0, :, :].rearrange("p t (i c) -> p (t i) c", i=2),
                                            ps[:, b:b + 2, :].rearrange("p t (i c) -> p (t i) c", i=2),
                                            rstd_tok[:, :].unsqueeze(2).broadcast_to([P, 4, 2 * P]), ALU.mult)\
                        .then_inc(slab_read, 1)

                def v_lo():
                    dve.wait_ge(proj_hi, n + 3)
                    split(dv_lo[:, :, :], tmp[:, 0, :, :], dv_hi[:, :, :]).then_inc(dil_ready, 1)

                if half:
                    dve.wait_ge(dil_ready, 3)
                else:
                    dve.wait_ge(slab_read, g)
                qk_out(0)
                if half == 0:
                    dve.wait_ge(spread_done, NORM["conv"])
                mean_squares(f"q{half}", 4, 1.0, 16)
                invert_root(f"q{half}", 16)
                if half == 0:
                    conv_out(0)
                    conv_out(1)
                    conv_out(2)
                qk_full_out(0)
                qk_lo(0)
                if half == 0:
                    conv_out(3)
                    dve.wait_ge(act_ready, MIX_Y + 4)
                qk_out(1)
                mean_squares(f"k{half}", 6, 1.0, 16)
                invert_root(f"k{half}", 16)
                qk_full_out(1)
                qk_lo(1)
                dve.wait_ge(dil_ready, 3 * half + 1)
                v_out()
                v_lo()
                dve.wait_ge(strips_landed, 16 * (half + 3))
                u0 = 4 * half

                def dil_bias(u):
                    c = T * (u % 4)
                    bias(dil, d_prob, u, lambda w: strips[:, c + T - w:c + T])
                    divide(dil, d_prob, u)

                def dil_out(u):
                    r, t = 64 * (u % 2), u // 2
                    dve.wait_ge(sq_done, SQUARED["dil"] + u + 1)
                    ins = split_scaled(o_lo[r:r + 64, 4 + t, :], ps[r:r + 64, 6 + u % 2, :],
                                       vec[r:r + 64, VEC["g_oa"] + t:VEC["g_oa"] + t + 1],
                                       o_hi[r:r + 64, 4 + t, :]).then_inc(dil.out_read, 1)
                    if u % 2:
                        if t:
                            ins = nc.vector.tensor_tensor(sum2[:, :], sum2[:, :], stat[:, :], ALU.add)
                        else:
                            dve.wait_ge(tok_ready, NORM["mix"])
                            ins = nc.vector.tensor_copy(sum2[:, :], stat[:, :])
                        ins.then_inc(mix_sq, 1)
                        dve.wait_ge(mix_sq, 8 + t + 1)
                        dve.wait_ge(dil.out_read, u + 1)
                        nc.vector.tensor_copy(mark[:, :], sum2[:, 0:1]).then_inc(act_ready, 1)

                dil_bias(u0)
                for u in range(u0, u0 + 4):
                    if u + 1 < u0 + 4:
                        dil_bias(u + 1)
                    turn_lo(dil, d_pt_hi, d_pt_lo, u)
                    if u > u0:
                        dil_out(u - 1)
                cast(g + 4)
                dil_out(u0 + 3)

            def rms_out(tiles, n, gain, squared):
                for k, t in enumerate(tiles):
                    dve.wait_ge(mix_hi, n_hi[0] + 1)
                    n_hi[0] += 1
                    split_scaled(act_lo[:, t, :], y[:, t, :], col(gain, t), act_hi[:, t, :])\
                        .then_inc(act_ready, 1)
                last = tiles[-1] == KT - 1
                sums(tiles, [tmp[:, n % 2, k, :] for k in range(len(tiles))], squared + n + 1, n == 0, last, False)

            n_hi = [4]
            mean_squares("attn", 2, 2.0)
            invert_root("attn")
            dve.wait_ge(rstd_ready, RSTD["attn"])
            for j in range(4):
                g = MIX_OUT + j
                b = banks(g)
                dve.wait_ge(slab_done, g + 1)
                link(nc.vector.tensor_tensor(conv[:, :, :], ps[:, 4 + b:6 + b, :], pair(stat[:, :]), ALU.mult))
                link(nc.vector.tensor_tensor(y[:, 2 * j:2 * j + 2, :], y[:, 2 * j:2 * j + 2, :], conv[:, :, :],
                                             ALU.add))
                nc.vector.tensor_tensor(y[:, 2 * j:2 * j + 2, :], y[:, 2 * j:2 * j + 2, :], ps[:, b:b + 2, :],
                                        ALU.add).then_inc(slab_read, 1)
                rms_out([2 * j, 2 * j + 1], j, "g_ffn", SQUARED["ffn"])
                cast(g + 2)

            mean_squares("ffn", 7, 1.0)
            invert_root("ffn")
            dve.wait_ge(rstd_ready, RSTD["ffn"])
            dve.wait_ge(u_zeroed, 2)
            for rnd, (first, down, before, count) in enumerate(((FFN_A, FFN_A_DOWN, 0, FF_A),
                                                                (FFN_B, FFN_B_DOWN, FF_A, FF_B))):
                with dve.Fori(0, count // 2) as i:
                    for b in range(2):
                        more, at = i * 2, before + b
                        bank = banks(first + b)
                        dve.wait_ge(slab_done, first + b + 1 + more)
                        nc.vector.tensor_tensor(gate[:, b, 2:T + 2], ps[:, bank, :], rstd[:, :], ALU.mult)\
                            .then_inc(ff_step, 1)
                        nc.vector.tensor_tensor(ffh[:, b, :], ps[:, bank + 1, :], rstd[:, :], ALU.mult)\
                            .then_inc(slab_read, 1)

                        def taps(name, k):
                            c = VEC[name] + k * 22 + at
                            return vec[:, bass.ds(i * 2 + c, 1)]

                        dve.wait_ge(ff_step, 3 * at + 1 + i * 6)
                        nc.vector.tensor_scalar(gconv[:, b, :], gate[:, b, 2:T + 2], taps("fconv_w", 2),
                                                taps("fconv_b", 0), ALU.mult, ALU.add).then_inc(ff_step, 1)
                        dve.wait_ge(ff_step, 3 * at + 2 + i * 6)
                        nc.vector.scalar_tensor_tensor(gconv[:, b, :], gate[:, b, 1:T + 1], taps("fconv_w", 1),
                                                       gconv[:, b, :], ALU.mult, ALU.add).then_inc(ff_step, 1)
                        dve.wait_ge(ff_step, 3 * at + 3 + i * 6)
                        nc.vector.scalar_tensor_tensor(gconv[:, b, :], gate[:, b, 0:T], taps("fconv_w", 0),
                                                       gconv[:, b, :], ALU.mult, ALU.add).then_inc(conv_done, 1)
                        dve.wait_ge(silu_done, at + 1 + more)
                        nc.vector.tensor_tensor(ffh[:, b, :], ffh[:, b, :], silu[:, b, :], ALU.mult)\
                            .then_inc(ffh_done, 1)
                        dve.wait_ge(ffh_hi, at + 1 + more)
                        split(h_lo[:, bass.ds(i * 2 + b, 1), :], ffh[:, b:b + 1, :],
                              h_hi[:, bass.ds(i * 2 + b, 1), :]).then_inc(h_ready, 1)
                        cast(first + b + 2, more, SLAB)
                if rnd:
                    dve.wait_ge(slab_done, PLE_PROJ + 1)
                    link(nc.vector.tensor_copy(proj_b[:, 0:2, :], ps[:, 4:6, :]))
                    nc.vector.tensor_copy(proj_b[:, 2:4, :], ps[:, 6:8, :]).then_inc(slab_read, 1)
                    cast(PLE_PROJ + 2)
                for j in range(8):
                    g = down + j
                    dve.wait_ge(slab_done, g + 1)
                    nc.vector.tensor_tensor(y[:, j, :], y[:, j, :], ps[:, banks(g), :], ALU.add)\
                        .then_inc(slab_read, 1)
                    if rnd:
                        rms_out([j], j, "g_ple", SQUARED["ple"])
                    cast(g + 2)
                if rnd == 0:
                    dve.wait_ge(p_split, 1)
                    split(p_lo[:, :, :], p_raw[:, :, :], p_hi[:, :, :]).then_inc(p_split, 1)

            mean_squares("ple", 7, 1.0)
            invert_root("ple")
            dve.wait_ge(rstd_ready, RSTD["ple"])
            for j in range(4):
                b = banks(PLE_GATE + j)
                dve.wait_ge(slab_done, PLE_GATE + j + 1)
                nc.vector.tensor_tensor(gate_in[:, j % 2, :, :], ps[:, b:b + 2, :], pair(rstd[:, :]), ALU.mult)\
                    .then_inc(slab_read, 1)
                cast(PLE_GATE + j + 2)
                dve.wait_ge(slab_read, PLE_GATE + j + 1)
                dve.wait_ge(sig_done, j + 1)
                link(nc.vector.tensor_tensor(gate_in[:, j % 2, :, :], gate_in[:, j % 2, :, :],
                                             (proj_a, proj_b)[j // 2][:, 2 * (j % 2):2 * (j % 2) + 2, :],
                                             ALU.mult))
                nc.vector.tensor_tensor(y[:, 2 * j:2 * j + 2, :], y[:, 2 * j:2 * j + 2, :],
                                        gate_in[:, j % 2, :, :], ALU.add).then_inc(out_ready, 1)

        @block.tensor
        def _(pe):
            def product(out, l_hi, l_lo, r_hi, r_lo, start, stop, shared=False):
                mm = nc.tensor.matmul
                mm(out, l_lo, r_hi, start=start, stop=False, skip_group_check=shared)
                mm(out, l_hi, r_hi, start=False, stop=False, skip_group_check=shared)
                return mm(out, l_hi, r_lo, start=False, stop=stop, skip_group_check=shared)

            def gemm(g, outs, kt, hi, lo, ready=None, more=0, free=None, at=0):
                s = g % 2
                if free is None:
                    free = g - 1
                if free > 0:
                    pe.wait_ge(slab_read, free + more)
                if g:
                    pe.wait_ge(cast_lo, g + 1 + more)
                for k in range(kt):
                    if ready:
                        ready(k)
                    for m, o in enumerate(outs):
                        c = (k * len(outs) + m) * P
                        last = product(o, w_hi[s][:, c:c + P], w_lo[s][:, c:c + P], hi[:, at + k, :],
                                       lo[:, at + k, :], k == 0, k == kt - 1)
                last.then_inc(slab_done, 1)

            def plain(g, kt=KT, hi=act_hi, lo=act_lo, ready=None, more=0, n=2, free=None):
                b = banks(g)
                gemm(g, [ps[:, b + m, :] for m in range(n)], kt, hi, lo, ready, more, free)

            def act_tiles(gen):
                return lambda k: pe.wait_ge(act_ready, gen + k + 1)

            def values(g, ready=None):
                s, w = g % 2, 2 * P
                pe.wait_ge(slab_read, g - 1)
                pe.wait_ge(cast_lo, g + 1)
                for i in range(4):
                    if ready:
                        ready(i)
                    for k in range(KT):
                        q, c = slice(i * P, (i + 1) * P), i % 2 * w
                        last = product(ps[:, banks(g) + i // 2, c:c + w], act_hi[:, k, q], act_lo[:, k, q],
                                       w_hi[s][:, k * w:(k + 1) * w], w_lo[s][:, k * w:(k + 1) * w],
                                       k == 0, k == KT - 1)
                last.then_inc(slab_done, 1)

            def token_sums(src, bank, at=0):
                for i in range(4):
                    last = nc.tensor.matmul(ps[:, bank, at + i:at + i + 1], src[:, i * P:(i + 1) * P], ones[:, 0:1],
                                            start=True, stop=True)
                return last


            def spread(name, bank, at=0):
                pe.wait_ge(tok_ready, NORM[name])
                for i in range(4):
                    last = nc.tensor.matmul(ps[:, bank, i * P:(i + 1) * P],
                                            tok_r[:, at + i:at + i + 1].broadcast_to([P, P]), ident, start=True,
                                            stop=True)
                return last

            def between(steps, then=None):
                def ready(k):
                    if k in steps:
                        steps[k]()
                    if then:
                        then(k)
                return ready

            def score(a, u, operands, first):
                h, at = a.h, a.score_banks[u % 2]
                for m, group in enumerate(h.groups):
                    v = u - a.ahead
                    if v >= first:
                        read = 4 * v + sum(len(x) for x in h.groups[:m + 1])
                        pe.wait_ge(a.biased, read)
                    for i in group:
                        bank, c = h.place[i]
                        dst = ps[:, at + bank, c:c + h.width[i]]
                        parts = operands(u, i, slice(h.key0[i], h.key0[i] + h.width[i]))
                        for x, part in enumerate(parts):
                            last = product(dst, *part, x == 0, x == len(parts) - 1)
                    last.then_inc(a.scored, 1)

            def turn(a, u, prob):
                h = a.h
                waited = 0
                for n in range(a.nseg):
                    if u:
                        pe.wait_ge(a.turn_lo, a.nseg * (u - 1) + n + 1)
                    for i, j, c in h.blocks(n):
                        need = h.order.index(i) + 1
                        if need > waited:
                            if a is not swa:
                                pe.wait_ge(a.normed, 4 * u + need)
                            elif need <= 2:
                                pe.wait_ge(a.normed, 2 * u + need)
                            else:
                                pe.wait_ge(pool_normed, 2 * u + need - 2)
                            waited = need
                        k = h.off[i] + j * P - h.key0[i]
                        last = nc.tensor.transpose(ps[:, a.trans_bank + n, c:c + P], prob[:, u % 2, k:k + P], ident)
                    last.then_inc(a.turned, 1)

            def mix(a, u, bank, pt_hi, pt_lo, v_of, start=True, stop=True):
                for j, (reach, seg, c) in enumerate(a.h.keys):
                    pe.wait_ge(a.turn_lo, a.nseg * u + seg + 1)
                    c += BANK * seg
                    w = reach * P
                    last = product(ps[:, bank, j * P:j * P + w], *v_of(u, j), pt_hi[:, c:c + w], pt_lo[:, c:c + w],
                                   start and j == 0, stop and j == 3, True)
                if stop:
                    last.then_inc(a.mixed, 1)

            def first_tiles(k):
                if k < 6:
                    pe.wait_ge(first_lo, k // 2 + 1)
                else:
                    pe.wait_ge(cast_lo, 1)
                pe.wait_ge(act_ready, X_IN + k + 1)

            for j in range(3):
                g = MLA_IN + j
                plain(g, ready=first_tiles if j == 0 else None)
                if j == 0:
                    pe.wait_ge(const_landed, 16 * 7)
                    nc.tensor.matmul(ps[0:16, 7, 0:LINE], stat[0:32, 0:16], sum2[0:32, 0:LINE], start=True,
                                     stop=True).then_inc(line_done, 1)
            pe.wait_ge(sum_ready, SUM_READY["mla_q"])
            token_sums(sum1, 4)
            pe.wait_ge(sum_ready, SUM_READY["mla_kv"])
            token_sums(sum2, 4, 4).then_inc(tok_sums, 1)
            pe.wait_ge(rope_in, 1)
            nc.tensor.matmul(ps[:, 6, :], swap, rope_raw[:, :], start=True, stop=True).then_inc(rope_swapped, 1)
            spread("mla", 4)
            spread("mla", 5, 4).then_inc(spread_done, 1)

            def mla_operands(u, i, keys):
                x, q, r = u % 4, slice(i * P, (i + 1) * P), 64 * (u % 2)
                return [(act_hi[:, 4 + x, q], act_lo[:, 4 + x, q], kn_hi[:, x, keys], kn_lo[:, x, keys]),
                        (qr_hi[r:r + 64, x // 2, q], qr_lo[r:r + 64, x // 2, q],
                         kr_hi[r:r + 64, keys], kr_lo[r:r + 64, keys])]

            def mla_values(u, j):
                c = slice(P * (u % 4), P * (u % 4) + P)
                return mv_hi[:, j, c], mv_lo[:, j, c]

            def mla_mix(u):
                mix(mla, u, 6 + u % 2, m_pt_hi, m_pt_lo, mla_values)

            def mla_turn(u):
                turn(mla, u, m_prob)
                if u % 4:
                    mla_mix(u - 1)

            def c_tiles(at):
                return lambda k: pe.wait_ge(c_ready, at + k + 1)

            for half in range(2):
                g = MLA_HALF + 4 * half
                if half:
                    pe.wait_ge(mla.biased, 16)
                else:
                    pe.wait_ge(slab_read, 3)
                steps = {1: lambda: mla_turn(3), 2: lambda: mla_mix(3)} if half else {}
                gemm(g, [ps[:, b, :] for b in range(3)], 3, c_hi, c_lo, between(steps, c_tiles(0)), free=g)
                if half:
                    pe.wait_ge(mla.turn_lo, 3 * 4)
                    pe.wait_ge(act_ready, MLA_O + 4)
                else:
                    pe.wait_ge(rope_out, 1)

                def rope_swap(n, bank):
                    pe.wait_ge(rope_in, n + 1)
                    nc.tensor.matmul(ps[:, bank, :], swap, rope_raw[:, :], start=True, stop=True)\
                        .then_inc(rope_swapped, 1)

                n = 1 + 2 * half
                gemm(g + 1, [ps[:, b, :] for b in range(4, 7)], 3, c_hi, c_lo,
                     between({1: lambda: rope_swap(n, 3)}), free=g)
                pe.wait_ge(rope_out, n + 1)
                gemm(g + 2, [ps[:, b, :] for b in range(4)], 2, c_hi, c_lo,
                     between({0: lambda: pe.wait_ge(c_ready, 5), 1: lambda: rope_swap(n + 1, 7)}), free=g + 1, at=3)
                pe.wait_ge(rope_out, n + 2)
                s = (g + 3) % 2
                pe.wait_ge(slab_read, g + 2)
                pe.wait_ge(cast_lo, g + 4)
                for i in range(4):
                    for k in range(2):
                        q = slice(i * P, (i + 1) * P)
                        last = product(ps[:, 4 + i, :], c_hi[:, 3 + k, q], c_lo[:, 3 + k, q],
                                       w_hi[s][:, k * T:(k + 1) * T], w_lo[s][:, k * T:(k + 1) * T],
                                       k == 0, k == 1)
                last.then_inc(slab_done, 1)
                pe.wait_ge(slab_read, g + 3)
                pe.wait_ge(rope_lo, 3 + 2 * half)
                u0 = 4 * half
                score(mla, u0, mla_operands, u0)
                for u in range(u0, u0 + 3):
                    score(mla, u + 1, mla_operands, u0)
                    if u == u0:
                        pe.wait_ge(slab_read, g + 4)
                    mla_turn(u)

            def last_plain(g, hi, lo):
                s, b = g % 2, banks(g)
                pe.wait_ge(slab_read, g - 1)
                pe.wait_ge(cast_lo, g + 1)
                for m in range(2):
                    for k in range(KT):
                        c = (k * 2 + m) * P
                        last = product(ps[:, b + m, :], w_hi[s][:, c:c + P], w_lo[s][:, c:c + P], hi[:, k, :],
                                       lo[:, k, :], k == 0, k == KT - 1)
                    last.then_inc((half_done, slab_done)[m], 1)

            def layer_stats(n):
                pe.wait_ge(sum_ready, SUM_READY["ln"] + 2 * n + 1)
                token_sums(sum1, 5)
                pe.wait_ge(sum_ready, SUM_READY["ln"] + 2 * n + 2)
                token_sums(sum2, 5, 4).then_inc(tok_sums, 1)
                nc.tensor.matmul(ps[:, 4, :], ones, sum1[:, :], start=True, stop=True).then_inc(mean_done, 1)
                spread(f"ln{n}", 5).then_inc(spread_done, 1)

            def mlp(first, gen):
                def hidden(g, more):
                    return lambda k: pe.wait_ge(slab_read, first + k // 2 + 1 + more)

                def rnd(more, downs=4):
                    for j in range(4):
                        plain(first + j, more=more, ready=act_tiles(gen))
                    for j in range(downs):
                        plain(first + 4 + j, hi=hid_hi, lo=hid_lo, more=more, ready=hidden(j, more) if j == 0 else None)

                with pe.Fori(0, 3) as r:
                    rnd(r * 8)
                rnd(24, 3)
                last_plain(first + 31, hid_hi, hid_lo)

            pe.wait_ge(mla.biased, 4 * 8)
            plain(MLA_OUT, ready=between({2: lambda: mla_turn(7), 6: lambda: mla_mix(7)}, act_tiles(MLA_O)))
            for j in range(1, 3):
                plain(MLA_OUT + j)
            last_plain(MLA_OUT + 3, act_hi, act_lo)
            layer_stats(0)
            mlp(MLP0, LN_0)
            layer_stats(1)

            def swa_operands(u, i, keys):
                t, q, r = (u // 2) % 4, slice(i * P, (i + 1) * P), 64 * (u % 2)
                return [(sq_hi[r:r + 64, t, q], sq_lo[r:r + 64, t, q], swa_k_hi[r:r + 64, u // 8, keys],
                         swa_k_lo[r:r + 64, u // 8, keys])]

            def swa_values(u, j):
                x, c = 2 * j + u // 8, 64 * (u % 2)
                return sv_hi[:, x, c:c + P], sv_lo[:, x, c:c + P]

            def swa_mix(u):
                t = u // 2
                if u % 2 == 0 and t >= 2:
                    pe.wait_ge(act_ready, SWA_O + t - 1)
                mix(swa, u, 6 + t % 2, s_pt_hi[u % 2], s_pt_lo[u % 2], swa_values, u % 2 == 0, u % 2 == 1)

            def swa_turn(u):
                turn(swa, u, s_prob)
                if u % 8:
                    swa_mix(u - 1)

            plain(SWA_KV, ready=act_tiles(LN_1))
            values(SWA_KV + 1)
            pe.wait_ge(v_zeroed, 2)
            for half in range(2):
                g = SWA_Q + 2 * half
                if half:
                    pe.wait_ge(swa.biased, 32)
                plain(g, ready=between({1: lambda: swa_turn(7), 4: lambda: swa_mix(7)} if half else {}))
                plain(g + 1)
                pe.wait_ge(slab_read, g + 1)
                u0 = 8 * half
                score(swa, u0, swa_operands, u0)
                pe.wait_ge(slab_read, g + 2)
                score(swa, u0 + 1, swa_operands, u0)
                for u in range(u0, u0 + 7):
                    turn(swa, u, s_prob)
                    if u + 2 < u0 + 8:
                        score(swa, u + 2, swa_operands, u0)
                    if u > u0:
                        swa_mix(u - 1)

            pe.wait_ge(swa.biased, 64)
            plain(SWA_OUT, hi=o_hi, lo=o_lo, ready=between({2: lambda: swa_turn(15), 6: lambda: swa_mix(15)}, act_tiles(SWA_O)))
            for j in range(1, 3):
                plain(SWA_OUT + j, hi=o_hi, lo=o_lo)
            last_plain(SWA_OUT + 3, o_hi, o_lo)
            layer_stats(2)
            mlp(MLP1, LN_2)
            layer_stats(3)

            def mix_sums():
                pe.wait_ge(mix_sq, 8)
                token_sums(sum2, 6).then_inc(tok_sums, 1)

            plain(CONV, ready=act_tiles(LN_3))
            plain(CONV + 1, ready=between({2: mix_sums, 4: lambda: spread("mix", 6).then_inc(spread_done, 1)}))
            for j in range(2, 6):
                plain(CONV + j)

            def dil_operands(u, i, keys):
                p, q, r = (u // 2) % 2, slice(i * P, (i + 1) * P), 64 * (u % 2)
                return [(dq_hi[r:r + 64, p, q], dq_lo[r:r + 64, p, q], dk_hi[r:r + 64, p, keys],
                         dk_lo[r:r + 64, p, keys])]

            def dil_values(u, j):
                c = 2 * P * (j % 2) + P * (u // 2 % 2)
                return dv_hi[:, j // 2, c:c + P], dv_lo[:, j // 2, c:c + P]

            def dil_mix(u):
                if u % 4 >= 2:
                    pe.wait_ge(dil.out_read, u - 1)
                mix(dil, u, 6 + u % 2, d_pt_hi, d_pt_lo, dil_values)

            def dil_turn(u):
                turn(dil, u, d_prob)
                if u % 4:
                    dil_mix(u - 1)

            def head_sums(n, bank):
                pe.wait_ge(qk_sq, n + 1)
                for k in range(2):
                    for i in range(4):
                        c = 8 * k + 2 * i
                        last = nc.tensor.matmul(ps[:, bank, c:c + 2], tmp[:, 1, k, i * P:(i + 1) * P],
                                                ones64[:, 0:P:64], start=True, stop=True)
                last.then_inc(tok_sums, 1)

            def head_spread(name, bank):
                pe.wait_ge(tok_ready, NORM[name])
                for k in range(2):
                    for i in range(4):
                        for h in range(2):
                            c, r = 8 * k + 2 * i + h, 64 * h
                            last = nc.tensor.matmul(ps[r:r + 64, bank + k, i * P:(i + 1) * P],
                                                    tok_r[:, c:c + 1].broadcast_to([P, 64]), ident,
                                                    start=True, stop=True)
                last.then_inc(spread_done, 1)

            for half in range(2):
                g = DIL_HALF + 3 * half
                if half:
                    pe.wait_ge(dil.biased, 16)
                def conv_sums():
                    pe.wait_ge(sum_ready, SUM_READY["conv"])
                    token_sums(sum1, 7).then_inc(tok_sums, 1)

                def k_sums():
                    if half == 0:
                        pe.wait_ge(conv_done, 6)
                    else:
                        pe.wait_ge(dil.out_read, 4)
                    head_sums(2 * half + 1, 6)

                if half == 0:
                    steps = {5: conv_sums, 7: lambda: spread("conv", 7).then_inc(spread_done, 1)}
                else:
                    steps = {1: lambda: dil_turn(3), 4: lambda: dil_mix(3)}
                plain(g, ready=between(steps))
                if half:
                    pe.wait_ge(dil.turn_lo, 3 * 4)
                plain(g + 1, ready=between({3: lambda: head_sums(2 * half, 4), 6: lambda: head_spread(f"q{half}", 4)}))
                values(g + 2, between({1: k_sums, 2: lambda: head_spread(f"k{half}", 6)}))
                pe.wait_ge(slab_read, g + 3)
                pe.wait_ge(dil_ready, 3 * half + 2)
                u0 = 4 * half
                score(dil, u0, dil_operands, u0)
                for u in range(u0, u0 + 3):
                    score(dil, u + 1, dil_operands, u0)
                    if u == u0 + 1:
                        pe.wait_ge(dil_ready, 3 * half + 3)
                    dil_turn(u)

            pe.wait_ge(dil.biased, 4 * 8)
            for j in range(4):
                g = MIX_OUT + j
                s, b = g % 2, banks(g)
                if j >= 2:
                    pe.wait_ge(slab_read, g - 1)
                if j == 1:
                    pe.wait_ge(rstd_ready, RSTD["attn"])
                pe.wait_ge(cast_lo, g + 1)
                for k in range(KT):
                    if j == 0 and k == 1:
                        dil_turn(7)
                    if j == 0 and k == 4:
                        dil_mix(7)
                        pe.wait_ge(dil.turn_lo, 3 * 8)
                    if j == 0:
                        pe.wait_ge(act_ready, MIX_Y + k + 1)
                    if j == 0 and k == 4:
                        pe.wait_ge(mix_sq, 12)
                        token_sums(sum2, 2).then_inc(tok_sums, 1)
                    if j == 0 and k == 6:
                        spread("attn", 2).then_inc(spread_done, 1)
                    for m in range(2):
                        c = (k * 2 + m) * P
                        last = product(ps[:, b + m + (4 if k >= 4 else 0), :], w_hi[s][:, c:c + P],
                                       w_lo[s][:, c:c + P], o_hi[:, k, :], o_lo[:, k, :], k % 4 == 0, k % 4 == 3)
                last.then_inc(slab_done, 1)

            def ple_projection():
                s = PLE_PROJ % 2
                pe.wait_ge(p_split, 2)
                pe.wait_ge(cast_lo, PLE_PROJ + 1)
                for m in (4, 5, 0, 1, 2, 3, 6, 7):
                    if m == 0:
                        pe.wait_ge(slab_read, PLE_PROJ)
                    for k in range(2):
                        c = (k * KT + m) * P
                        last = product(ps[:, m, :], w_hi[s][:, c:c + P], w_lo[s][:, c:c + P], p_hi[:, k, :],
                                       p_lo[:, k, :], k == 0, k == 1)
                    if m == 3:
                        last.then_inc(proj_half, 1)
                last.then_inc(slab_done, 1)

            for rnd, (first, down, before, count) in enumerate(((FFN_A, FFN_A_DOWN, 0, FF_A),
                                                                (FFN_B, FFN_B_DOWN, FF_A, FF_B))):
                if rnd == 0:
                    plain(first, ready=act_tiles(FFN_X))
                    pe.wait_ge(sum_ready, SUM_READY["ffn"])
                    token_sums(sum2, 7).then_inc(tok_sums, 1)
                    plain(first + 1, ready=between({2: lambda: spread("ffn", 7).then_inc(spread_done, 1)}))
                with pe.Fori(1 if rnd == 0 else 0, count // 2) as i:
                    for b in range(2):
                        plain(first + b, more=i * 2)
                if rnd:
                    ple_projection()
                for j in range(8):
                    def hidden(k):
                        pe.wait_ge(h_ready, before + k + 1)
                    if rnd and j == 0:
                        pe.wait_ge(proj_act, 1)
                    plain(down + j, kt=count, hi=h_hi, lo=h_lo, ready=hidden if j == 0 else None, n=1)

            for j in range(4):
                steps = between({2: lambda: spread("ple", 7).then_inc(spread_done, 1)} if j == 1 else {})
                plain(PLE_GATE + j, ready=act_tiles(PLE_X) if j == 0 else steps, free=PLE_GATE if j < 2 else None)
                if j == 0:
                    pe.wait_ge(sum_ready, SUM_READY["ple"])
                    token_sums(sum2, 7).then_inc(tok_sums, 1)


def rope_table():
    half = 32
    inv = np.float32(10000.0) ** (-np.arange(half, dtype=np.float32) / np.float32(half))
    ang = (np.arange(T, dtype=np.float32)[:, None] * inv[None, :].astype(np.float32)).T.astype(np.float32)
    cos, sin = np.cos(ang), np.sin(ang)
    return np.stack([np.concatenate([cos] * 4), np.concatenate([-sin, sin] * 2)], 1).astype(np.float32)


def matrices():
    eye = np.eye(P)
    ones = np.full((P, P), 1.0 / D)
    heads = np.kron(np.eye(2), np.full((64, 64), 1.0 / 64))
    swap = eye[np.arange(P) ^ 32]
    return np.stack([eye, ones, heads, swap], 1).astype(np.float32)


def strip_distance():
    return np.arange(P)[:, None] + (T - P) - np.arange(T)[None, :]


def causal_table():
    return np.where(strip_distance() >= 0, 0.0, MASKED).astype(np.float32)


def dilated_table():
    d = strip_distance()
    count = (d <= 128).astype(int) + (d % 4 == 0) + (d % 16 == 0)
    slopes = np.exp2(-np.arange(1, 9, dtype=np.float32))
    table = np.where((d >= 0) & (count > 0), np.log(np.maximum(count, 1)) - slopes[:, None, None] * d, MASKED)
    return np.ascontiguousarray(table.reshape(2, 4, P, T).transpose(0, 2, 1, 3).reshape(2, P, 4 * T), np.float32)


def t5_tables():
    d = 2 * P - 1 - np.arange(LINE)
    n = np.maximum(d, 0)
    nf = np.maximum(n, 1).astype(np.float32)
    large = 16 + (np.log(nf / np.float32(16)) / np.float32(np.log(128 / 16)) * np.float32(16)).astype(np.int32)
    bucket = np.where(n < 16, n, np.minimum(large, 31))
    valid = (d >= 0) & (d < P)
    onehot = ((np.arange(32)[:, None] == bucket[None, :]) & valid[None, :]).astype(np.float32)
    return onehot, np.broadcast_to(np.where(valid, 0.0, MASKED), (16, LINE)).astype(np.float32)


def blocks(w):
    k, n = w.shape
    return w.reshape(k // P, P, n).transpose(1, 0, 2).reshape(P, -1)


def columns(w, n):
    return [blocks(w[:, c:c + n]) for c in range(0, w.shape[1], n)]


def head_order():
    return [(2 * (u // 8) + u % 2) * 4 + (u // 2) % 4 for u in range(16)]


def pack_slabs(a):
    out = []
    w = a["mla_w_in"][0]
    w = np.concatenate([w, w[:, Q_RANK + KV_RANK:]], 1)
    out += columns(w, 256)
    uq, uk, uv = a["mla_w_uq"][0], a["mla_w_uk"][0], a["mla_w_uv"][0]
    for half in range(2):
        for p in range(2):
            h = 4 * half + 2 * p
            out.append(blocks(np.concatenate([uq[:, h, :128], uq[:, h + 1, :128], uq[:, h, 128:],
                                              uq[:, h + 1, 128:]], 1)))
        for m in (uk, uv):
            out.append(blocks(m[:, 4 * half:4 * half + 4].reshape(KV_RANK, 512)))
    out += columns(a["mla_w_o"][0], 256)

    def mlp(layer):
        for r in range(4):
            s = slice(D * r, D * (r + 1))
            out.extend(columns(a["mlp_w_up"][layer][:, s], 256))
            out.extend(columns(a["mlp_w_down"][layer][s], 256))

    mlp(0)
    order = head_order()
    out += columns(a["kv_w_shared"], 256)
    out += columns(a["swa_w_q"][0].reshape(D, 16, 64)[:, order].reshape(D, D), 256)
    out += columns(a["swa_w_o"][0].reshape(16, 64, D)[order].reshape(D, D), 256)
    mlp(1)
    zb, zc, zx, zq, zk, zv = np.split(a["w_in_2"][0], 6, 1)
    for i in range(2):
        s = slice(256 * i, 256 * (i + 1))
        out += [blocks(zc[:, s]), blocks(zx[:, s]), blocks(zb[:, s])]
    for half in range(2):
        s = slice(256 * half, 256 * (half + 1))
        out += [blocks(zq[:, s]), blocks(zk[:, s]), blocks(zv[:, s])]
    out += columns(a["w_out_2"][0], 256)
    gate, up, down = a["w_gate_2"][0], a["w_up_2"][0], a["w_down_2"][0]
    for before, count in ((0, FF_A), (FF_A, FF_B)):
        for t in range(before, before + count):
            s = slice(P * t, P * (t + 1))
            out.append(blocks(np.concatenate([gate[:, s], up[:, s]], 1)))
        if before:
            out.append(blocks(a["w_ple_proj_2"][0]))
        out += columns(down[P * before:P * (before + count)], P)
    out += columns(a["w_ple_gate_2"][0], 256)
    slabs = np.zeros((SLABS, P, SLAB), np.float32)
    assert len(out) == SLABS
    for g, w in enumerate(out):
        assert w.shape[1] == slab_width(g) or w.shape[1] == SLAB, (g, w.shape)
        slabs[g, :, :w.shape[1]] = w
    return slabs


def pack_vectors(a):
    def tiles(v):
        return v.reshape(-1, P).T

    parts = {"g_q": tiles(a["mla_g_q"][0]), "g_kv": tiles(a["mla_g_kv"][0]), "g_mix": tiles(a["g_mix_2"][0]),
             "conv_w": tiles(a["conv_w_2"][0]), "conv_b": tiles(a["conv_b_2"][0]),
             "qn_g": tiles(np.tile(a["q_norm_g_2"][0], 2)), "kn_g": tiles(np.tile(a["k_norm_g_2"][0], 2)),
             "g_oc": tiles(a["g_out_conv_2"][0]), "g_oa": tiles(a["g_out_attn_2"][0]),
             "g_ffn": tiles(a["g_ffn_2"][0]), "fconv_w": tiles(a["ffn_conv_w_2"][0]),
             "fconv_b": tiles(a["ffn_conv_b_2"][0]), "g_ple": tiles(a["g_ple_2"][0]),
             "sink": np.broadcast_to(a["swa_sinks"][0][head_order()], (P, 16))}
    for layer in range(2):
        for kind in ("mix", "mlp"):
            parts[f"{kind}_g{layer}"] = tiles(a[f"ln_{kind}_g"][layer])
            parts[f"{kind}_b{layer}"] = tiles(a[f"ln_{kind}_b"][layer])
    vecs = np.zeros((P, NVEC), np.float32)
    for name, part in parts.items():
        vecs[:, VEC[name]:VEC[name] + part.shape[1]] = part
    return vecs


def kernel(**inputs):
    import concourse.bacc as bacc
    from concourse.bass_utils import run_bass_kernel_spmd as run

    a = {name: np.asarray(value) for name, value in inputs.items()}
    onehot, line_mask = t5_tables()
    arrays = {
        "slabs": pack_slabs(a),
        "x_t": a["x"][0].T.reshape(KT, P, T).transpose(1, 0, 2),
        "ple_t": a["p_2"][0, 0].T.reshape(2, P, T).transpose(1, 0, 2),
        "vecs": pack_vectors(a),
        "rel_bias": a["rel_bias"][:, head_order()],
        "onehot": onehot,
        "line_mask": line_mask,
        "rope": rope_table(),
        "mats": matrices(),
        "causal": causal_table(),
        "dilated": dilated_table(),
    }
    arrays = {name: np.ascontiguousarray(value) for name, value in arrays.items()}
    nc = bacc.Bacc("TRN2", target_bir_lowering=False, num_devices=1)
    args = {name: nc.dram_tensor(name, value.shape, F32, kind="ExternalInput").ap()
            for name, value in arrays.items()}
    out = nc.dram_tensor("out", (P, KT, T), F32, kind="ExternalOutput").ap()
    program(nc, **args, out=out)
    result = run(nc, [arrays], core_ids=[0]).results[0]["out"]
    return np.ascontiguousarray(result.transpose(1, 0, 2).reshape(D, T).T).reshape(1, T, D)
```
